# Optimizing a Trainium2 kernel written in Bass

```python
import math
import jax, jax.numpy as jnp
from jax import lax
import numpy as np

'''Hybrid decoder trunk: DEPTH layers, each
  h = x + 1/2 SwiGLU(rms(x))                                   (macaron half-step FFN, pre)
  n = rms(h); z = n @ W_in   (one combined projection, columns split among all mixers + gates)
  A = Conformer conv module (GLU -> causal depthwise conv w=31 -> LayerNorm -> swish) @ P_A
  B = chunked causal spatial gating unit (u * (tril(W_s) v + b), 128-position chunks, 4 groups) @ P_B
  C = native sparse attention (compressed / top-k gathered blocks / sliding window, ALiBi, QK-norm, per-head gates) @ P_C
  h = h + W_out( sig(g_A)*A + sig(g_B)*B + sig(g_C)*C )        (per-channel gates from n)
  h = h + CrossAttn(rms(h), rms(mem))                           (4 heads, QK-norm, 256 memory tokens)
  h = h + 1/2 SwiGLU(rms(h))                                    (macaron half-step FFN, post)
Inputs: x (BATCH, SEQ, D_MODEL), mem (BATCH, 256, D_MODEL), per-layer weights stacked on a leading DEPTH axis.
Output: (BATCH, SEQ, D_MODEL).
'''

D_MODEL = 1024
BATCH = 1
SEQ = 512
DEPTH = 2

MEM_LEN = 256
D_FF = 2816
D_CONV = 512
CONV_WIDTH = 31
D_SGU = 512
SGU_GROUPS = 4
SGU_CHUNK = 128
SGU_GROUP_DIM = D_SGU // SGU_GROUPS
NSA_HEADS = 8
NSA_KV_GROUPS = 2
NSA_HEADS_PER_GROUP = NSA_HEADS // NSA_KV_GROUPS
NSA_HEAD_DIM = 64
CMP_LEN = 32
CMP_STRIDE = 16
SEL_BLOCK = 64
TOP_N = 16
WINDOW = 512
Q_BLOCK = 128
X_HEADS = 4
X_HEAD_DIM = 128
N_BRANCHES = 3
NEG_INF = -1e30
FORCE_SCORE = 1e4
EPS = 1e-6

COLS_CONV = 2 * D_CONV
COLS_SGU = 2 * D_SGU
COLS_Q = NSA_HEADS * NSA_HEAD_DIM
COLS_KV = 3 * 2 * NSA_KV_GROUPS * NSA_HEAD_DIM
COLS_NSA_GATE = NSA_HEADS * 3
COLS_MERGE = N_BRANCHES * D_MODEL
IN_COLS = COLS_CONV + COLS_SGU + COLS_Q + COLS_KV + COLS_NSA_GATE + COLS_MERGE
SPLITS = [COLS_CONV,
          COLS_CONV + COLS_SGU,
          COLS_CONV + COLS_SGU + COLS_Q,
          COLS_CONV + COLS_SGU + COLS_Q + COLS_KV,
          COLS_CONV + COLS_SGU + COLS_Q + COLS_KV + COLS_NSA_GATE]

kernel_name = 'hybrid_conv_sgu_nsa_macaron_block'

def _rms_norm(x, g):
    xf = x.astype(jnp.float32)
    y = xf * lax.rsqrt(jnp.mean(xf * xf, axis=-1, keepdims=True) + EPS)
    return (y * g.astype(jnp.float32)).astype(x.dtype)

def _layer_norm(x, g, b):
    xf = x.astype(jnp.float32)
    mu = jnp.mean(xf, axis=-1, keepdims=True)
    var = jnp.mean(jnp.square(xf - mu), axis=-1, keepdims=True)
    y = (xf - mu) * lax.rsqrt(var + EPS)
    return (y * g.astype(jnp.float32) + b.astype(jnp.float32)).astype(x.dtype)

def _masked_softmax(s, mask):
    return jax.nn.softmax(jnp.where(mask, s, NEG_INF), axis=-1)

def _alibi_slopes(n):
    return jnp.asarray(2.0 ** (-8.0 * np.arange(1, n + 1) / n), dtype=jnp.float32)

def _swiglu(x, wi, wo):
    a, b = jnp.split(x @ wi, 2, axis=-1)
    return (jax.nn.silu(a) * b) @ wo

def _conv_module(z, w, bias, ln_g, ln_b):
    a, g = jnp.split(z, 2, axis=-1)
    h = a * jax.nn.sigmoid(g)
    h = lax.conv_general_dilated(h, w[:, None, :], window_strides=(1,),
                                 padding=[(CONV_WIDTH - 1, 0)],
                                 dimension_numbers=('NWC', 'WIO', 'NWC'),
                                 feature_group_count=D_CONV) + bias
    return jax.nn.silu(_layer_norm(h, ln_g, ln_b))

def _spatial_gating(z, norm_g, ws, b):
    B, T = z.shape[0], z.shape[1]
    u, v = jnp.split(jax.nn.gelu(z), 2, axis=-1)
    v = _rms_norm(v, norm_g).reshape(B, T // SGU_CHUNK, SGU_CHUNK, SGU_GROUPS, SGU_GROUP_DIM)
    mixed = jnp.einsum('gts,bcsgk->bctgk', jnp.tril(ws), v) + b.T[None, None, :, :, None]
    return u * mixed.reshape(B, T, D_SGU)

def _compress(x, idx, pe, w1, w2):
    B, G = x.shape[0], x.shape[2]
    blocks = x[:, idx] + pe[:, None, :]
    blocks = jnp.swapaxes(blocks, 2, 3).reshape(B, idx.shape[0], G, -1)
    return jax.nn.silu(blocks @ w1) @ w2

def _nsa(q, kv, gate_logits, q_g, k_g, cmp_pe, cmp_w1, cmp_w2):
    B, T = q.shape[0], q.shape[1]
    G, HG, dh = NSA_KV_GROUPS, NSA_HEADS_PER_GROUP, NSA_HEAD_DIM
    scale = 1.0 / math.sqrt(dh)
    slopes = _alibi_slopes(NSA_HEADS).reshape(G, HG)
    q = _rms_norm(q.reshape(B, T, G, HG, dh), q_g)
    kv = kv.reshape(B, T, 6, G, dh)
    k_cmp, v_cmp, k_sel, v_sel, k_win, v_win = (kv[:, :, i] for i in range(6))
    k_sel = _rms_norm(k_sel, k_g[1])
    k_win = _rms_norm(k_win, k_g[2])

    n_cmp = (T - CMP_LEN) // CMP_STRIDE + 1
    cmp_start = CMP_STRIDE * jnp.arange(n_cmp)
    cmp_idx = cmp_start[:, None] + jnp.arange(CMP_LEN)[None, :]
    cmp_end = cmp_start + CMP_LEN - 1
    kc = _rms_norm(_compress(k_cmp, cmp_idx, cmp_pe[0], cmp_w1[0], cmp_w2[0]), k_g[0])
    vc = _compress(v_cmp, cmp_idx, cmp_pe[1], cmp_w1[1], cmp_w2[1])

    n_sel = T // SEL_BLOCK
    n_top = min(TOP_N, n_sel)
    sel_start = SEL_BLOCK * jnp.arange(n_sel)
    overlap = ((cmp_start[:, None] < sel_start[None, :] + SEL_BLOCK)
               & (cmp_end[:, None] >= sel_start[None, :])).astype(jnp.float32)
    kb = k_sel.reshape(B, n_sel, SEL_BLOCK, G, dh).transpose(0, 3, 1, 2, 4)
    vb = v_sel.reshape(B, n_sel, SEL_BLOCK, G, dh).transpose(0, 3, 1, 2, 4)

    kp = jnp.pad(k_win, ((0, 0), (WINDOW, 0), (0, 0), (0, 0)))
    vp = jnp.pad(v_win, ((0, 0), (WINDOW, 0), (0, 0), (0, 0)))

    n_qb = T // Q_BLOCK
    qb = q.reshape(B, n_qb, Q_BLOCK, G, HG, dh).transpose(1, 0, 2, 3, 4, 5)
    gb = jax.nn.sigmoid(gate_logits).reshape(B, n_qb, Q_BLOCK, G, HG, 3).transpose(1, 0, 2, 3, 4, 5)
    gather = jax.vmap(jax.vmap(lambda blocks, ix: blocks[ix]))

    def block_fn(args):
        c, qc, gc = args
        t = c * Q_BLOCK + jnp.arange(Q_BLOCK)
        d_c = t[:, None] - cmp_end[None, :]
        m_c = d_c >= 0
        s_c = (jnp.einsum('bqghd,bngd->bghqn', qc, kc).astype(jnp.float32) * scale
               - slopes[:, :, None, None] * d_c.astype(jnp.float32))
        p_c = _masked_softmax(s_c, m_c) * m_c
        o_c = jnp.einsum('bghqn,bngd->bqghd', p_c.astype(vc.dtype), vc)
        imp = jnp.einsum('bghqn,nj->bgqj', p_c, overlap)
        cur = t // SEL_BLOCK
        j = jnp.arange(n_sel)
        forced = (j[None, :] == 0) | (j[None, :] == cur[:, None]) | (j[None, :] == cur[:, None] - 1)
        imp = jnp.where(sel_start[None, :] <= t[:, None], jnp.where(forced, FORCE_SCORE, imp), NEG_INF)
        top_val, top_idx = lax.top_k(imp, n_top)
        ks = gather(kb, top_idx)
        vs = gather(vb, top_idx)
        pos = top_idx[..., None] * SEL_BLOCK + jnp.arange(SEL_BLOCK)
        d_s = t[None, None, :, None, None] - pos
        m_s = (top_val > 0.5 * NEG_INF)[..., None] & (d_s >= 0)
        s_s = (jnp.einsum('bqghd,bgqnkd->bghqnk', qc, ks).astype(jnp.float32) * scale
               - slopes[:, :, None, None, None] * d_s[:, :, None].astype(jnp.float32))
        s_s = s_s.reshape(B, G, HG, Q_BLOCK, n_top * SEL_BLOCK)
        m_s = m_s.reshape(B, G, 1, Q_BLOCK, n_top * SEL_BLOCK)
        p_s = _masked_softmax(s_s, m_s)
        o_s = jnp.einsum('bghqm,bgqmd->bqghd', p_s.astype(vs.dtype),
                         vs.reshape(B, G, Q_BLOCK, n_top * SEL_BLOCK, dh))
        kw = lax.dynamic_slice_in_dim(kp, c * Q_BLOCK, Q_BLOCK + WINDOW, axis=1)
        vw = lax.dynamic_slice_in_dim(vp, c * Q_BLOCK, Q_BLOCK + WINDOW, axis=1)
        s_pos = c * Q_BLOCK - WINDOW + jnp.arange(Q_BLOCK + WINDOW)
        d_w = t[:, None] - s_pos[None, :]
        m_w = (d_w >= 0) & (d_w < WINDOW) & (s_pos[None, :] >= 0)
        s_w = (jnp.einsum('bqghd,bsgd->bghqs', qc, kw).astype(jnp.float32) * scale
               - slopes[:, :, None, None] * d_w.astype(jnp.float32))
        p_w = _masked_softmax(s_w, m_w)
        o_w = jnp.einsum('bghqs,bsgd->bqghd', p_w.astype(vw.dtype), vw)
        return gc[..., 0:1] * o_c + gc[..., 1:2] * o_s + gc[..., 2:3] * o_w

    out = lax.map(block_fn, (jnp.arange(n_qb), qb, gb))
    return out.transpose(1, 0, 2, 3, 4, 5).reshape(B, T, NSA_HEADS * dh)

def _memory_cross_attention(h, mem_n, wq, wkv, q_g, k_g, wo):
    B, T = h.shape[0], h.shape[1]
    M = mem_n.shape[1]
    q = _rms_norm((h @ wq).reshape(B, T, X_HEADS, X_HEAD_DIM), q_g)
    k, v = jnp.split(mem_n @ wkv, 2, axis=-1)
    k = _rms_norm(k.reshape(B, M, X_HEADS, X_HEAD_DIM), k_g)
    v = v.reshape(B, M, X_HEADS, X_HEAD_DIM)
    s = jnp.einsum('bthd,bmhd->bhtm', q, k).astype(jnp.float32) / math.sqrt(X_HEAD_DIM)
    p = jax.nn.softmax(s, axis=-1)
    o = jnp.einsum('bhtm,bmhd->bthd', p.astype(v.dtype), v)
    return o.reshape(B, T, X_HEADS * X_HEAD_DIM) @ wo

def setup_inputs(seed: int = 0) -> dict:
    key = jax.random.key(seed)
    ks = list(jax.random.split(key, 40))
    L = DEPTH
    dh = NSA_HEAD_DIM

    def nrm(shape, scale):
        return jax.random.normal(ks.pop(), shape, jnp.float32) * scale

    def gain(shape):
        return 1.0 + nrm(shape, 0.02)

    return {
        'x': nrm((BATCH, SEQ, D_MODEL), 1.0),
        'mem': nrm((BATCH, MEM_LEN, D_MODEL), 1.0),
        'norm_ffn1': gain((L, D_MODEL)),
        'ffn1_wi': nrm((L, D_MODEL, 2 * D_FF), D_MODEL ** -0.5),
        'ffn1_wo': nrm((L, D_FF, D_MODEL), D_FF ** -0.5),
        'norm_mix': gain((L, D_MODEL)),
        'w_in': nrm((L, D_MODEL, IN_COLS), D_MODEL ** -0.5),
        'conv_w': nrm((L, CONV_WIDTH, D_CONV), CONV_WIDTH ** -0.5),
        'conv_b': nrm((L, D_CONV), 0.02),
        'conv_ln_g': gain((L, D_CONV)),
        'conv_ln_b': nrm((L, D_CONV), 0.02),
        'conv_out': nrm((L, D_CONV, D_MODEL), D_CONV ** -0.5),
        'sgu_norm': gain((L, D_SGU)),
        'sgu_ws': nrm((L, SGU_GROUPS, SGU_CHUNK, SGU_CHUNK), SGU_CHUNK ** -0.5),
        'sgu_b': nrm((L, SGU_GROUPS, SGU_CHUNK), 0.02),
        'sgu_out': nrm((L, D_SGU, D_MODEL), D_SGU ** -0.5),
        'nsa_q_norm': gain((L, dh)),
        'nsa_k_norm': gain((L, 3, dh)),
        'cmp_pe': nrm((L, 2, CMP_LEN, dh), 0.1),
        'cmp_w1': nrm((L, 2, CMP_LEN * dh, dh), (CMP_LEN * dh) ** -0.5),
        'cmp_w2': nrm((L, 2, dh, dh), dh ** -0.5),
        'nsa_out': nrm((L, NSA_HEADS * dh, D_MODEL), (NSA_HEADS * dh) ** -0.5),
        'w_out': nrm((L, D_MODEL, D_MODEL), D_MODEL ** -0.5),
        'norm_xattn': gain((L, D_MODEL)),
        'mem_norm': gain((L, D_MODEL)),
        'xq': nrm((L, D_MODEL, X_HEADS * X_HEAD_DIM), D_MODEL ** -0.5),
        'xkv': nrm((L, D_MODEL, 2 * X_HEADS * X_HEAD_DIM), D_MODEL ** -0.5),
        'xq_norm': gain((L, X_HEAD_DIM)),
        'xk_norm': gain((L, X_HEAD_DIM)),
        'xo': nrm((L, X_HEADS * X_HEAD_DIM, D_MODEL), (X_HEADS * X_HEAD_DIM) ** -0.5),
        'norm_ffn2': gain((L, D_MODEL)),
        'ffn2_wi': nrm((L, D_MODEL, 2 * D_FF), D_MODEL ** -0.5),
        'ffn2_wo': nrm((L, D_FF, D_MODEL), D_FF ** -0.5),
    }

def reference(x, mem, norm_ffn1, ffn1_wi, ffn1_wo, norm_mix, w_in,
              conv_w, conv_b, conv_ln_g, conv_ln_b, conv_out,
              sgu_norm, sgu_ws, sgu_b, sgu_out,
              nsa_q_norm, nsa_k_norm, cmp_pe, cmp_w1, cmp_w2, nsa_out,
              w_out, norm_xattn, mem_norm, xq, xkv, xq_norm, xk_norm, xo,
              norm_ffn2, ffn2_wi, ffn2_wo):
    h = x
    for l in range(DEPTH):
        h = h + 0.5 * _swiglu(_rms_norm(h, norm_ffn1[l]), ffn1_wi[l], ffn1_wo[l])
        n = _rms_norm(h, norm_mix[l])
        z = n @ w_in[l]
        z_conv, z_sgu, z_q, z_kv, z_ngate, z_merge = jnp.split(z, SPLITS, axis=-1)
        y_a = _conv_module(z_conv, conv_w[l], conv_b[l], conv_ln_g[l], conv_ln_b[l]) @ conv_out[l]
        y_b = _spatial_gating(z_sgu, sgu_norm[l], sgu_ws[l], sgu_b[l]) @ sgu_out[l]
        y_c = _nsa(z_q, z_kv, z_ngate, nsa_q_norm[l], nsa_k_norm[l],
                   cmp_pe[l], cmp_w1[l], cmp_w2[l]) @ nsa_out[l]
        g_a, g_b, g_c = jnp.split(jax.nn.sigmoid(z_merge), N_BRANCHES, axis=-1)
        h = h + (g_a * y_a + g_b * y_b + g_c * y_c) @ w_out[l]
        h = h + _memory_cross_attention(_rms_norm(h, norm_xattn[l]), _rms_norm(mem, mem_norm[l]),
                                        xq[l], xkv[l], xq_norm[l], xk_norm[l], xo[l])
        h = h + 0.5 * _swiglu(_rms_norm(h, norm_ffn2[l]), ffn2_wi[l], ffn2_wo[l])
    return h


_drawn_inputs = setup_inputs


def setup_inputs(seed=0):
    import zlib

    import numpy as np

    out = dict(_drawn_inputs(seed))
    spreads = {}
    factors = {'norm_ffn1': 4.579,
     'norm_mix': 3.71,
     'conv_b': 3.375,
     'conv_ln_g': 5.616,
     'conv_ln_b': 6.84,
     'sgu_norm': 8.0,
     'sgu_b': 6.235,
     'nsa_q_norm': 8.0,
     'nsa_k_norm': 8.0,
     'norm_xattn': 8.0,
     'mem_norm': 8.0,
     'xq_norm': 8.0,
     'xk_norm': 8.0,
     'norm_ffn2': 5.43}
    for name, (base, spread) in spreads.items():
        noise = np.random.default_rng([zlib.crc32(name.encode()), seed]).standard_normal(out[name].shape)
        drawn = base * np.exp(spread * noise) if base else spread * noise
        out[name] = __import__('jax').numpy.asarray(drawn.astype(out[name].dtype))
    for name, factor in factors.items():
        out[name] = (out[name] * factor).astype(out[name].dtype)
    return out
```

```python
from contextlib import ExitStack

import concourse.bass as bass
from concourse import mybir

F32 = mybir.dt.float32
F32R = mybir.dt.float32r
ALU = mybir.AluOpType
ACT = mybir.ActivationFunctionType
AX_X = mybir.AxisListType.X

P = 128
EPS = 1e-6
NEG = -1e30


def trunk(nc, x, mem, norm_ffn1, ffn1_wi, ffn1_wo, norm_mix, w_in, conv_w, conv_b, conv_ln_g,
          conv_ln_b, conv_out, sgu_norm, sgu_ws, sgu_b, sgu_out, nsa_q_norm, nsa_k_norm, cmp_pe,
          cmp_w1, cmp_w2, nsa_out, w_out, norm_xattn, mem_norm, xq, xkv, xq_norm, xk_norm, xo,
          norm_ffn2, ffn2_wi, ffn2_wo, out):
    _, T, D = x.shape
    L = norm_ffn1.shape[0]
    M = mem.shape[1]
    F = ffn1_wo.shape[1]
    CONV_W, DC = conv_w.shape[1:]
    GROUPS, CHUNK = sgu_b.shape[1:]
    DS = sgu_norm.shape[1]
    DH = nsa_q_norm.shape[1]
    XDH = xq_norm.shape[1]
    CMP_LEN = cmp_pe.shape[2]
    HEADS = nsa_out.shape[1] // DH
    KVG = 2
    CMP_STRIDE = CMP_LEN // 2
    NCMP = (T - CMP_LEN) // CMP_STRIDE + 1
    assert T == 512 and D == 1024 and DC == 512 and DS == 512 and CHUNK == P and GROUPS == 4
    assert DH == 64 and HEADS == 8 and XDH == P and M == 256 and F % P == 0 and NCMP == 31
    KD = D // P
    KB = DC // P
    TT = T // P
    FT = F // P
    C_SGU, C_Q = 2 * DC, 2 * DC + 2 * DS
    C_KV = C_Q + HEADS * DH
    C_NG = C_KV + 6 * KVG * DH
    C_MG = C_NG + 3 * HEADS
    PAIRS = HEADS // KVG
    slope = [2.0 ** (-8.0 * (h + 1) / HEADS) for h in range(HEADS)]

    CH = [8, 8, FT - 16]
    FFN = 2 * FT + 3 * KD
    U_MIX = FFN
    U_KV, U_QP = U_MIX, U_MIX + 6
    U_NG = U_QP + 4
    U_CONV = U_NG + 2
    U_SGU = U_CONV + 8
    U_B = U_SGU + 8
    U_A = U_B + 16
    U_CM = U_A + 16
    U_CO = U_CM + 8
    U_XKV = U_CO + 8
    U_WO = U_XKV + 8
    U_XQ = U_WO + 8
    U_XO = U_XQ + 4
    U_F2 = U_XO + 8
    U = U_F2 + FFN
    assert U % 4 == 0

    ctx = ExitStack()
    with ctx:
        def sb(name, shape, dt=F32):
            return ctx.enter_context(nc.sbuf_tensor(name, shape, dt))

        raw = sb("raw", [P, 2, KD, P])
        wH = sb("wH", [P, 4, KD, P], F32R)
        wL = sb("wL", [P, 4, KD, P], F32R)
        xT = sb("xT", [P, KD, T])
        gxH = sb("gxH", [P, KD, T], F32R)
        gxL = sb("gxL", [P, KD, T], F32R)
        hH = sb("hH", [P, 8, T], F32R)
        hL = sb("hL", [P, 8, T], F32R)
        big = sb("big", [P, 8 * T])
        convb = sb("convb", [P, 4 * (T + CONV_W - 1) + 4 * T])
        qT = sb("qT", [P, 4, T])
        kT = sb("kT", [P, 2, T])
        vtok = sb("vtok", [P, 4, 2 * P])
        att = sb("att", [P, 2, 2, T])
        kvc = att[:, 1, :, :]
        tmp3 = sb("tmp3", [P, 3, T])
        ptc = sb("ptc", [32, 2, T])
        rstd = sb("rstd", [P, T])
        rv = sb("rv", [P, T])
        sacc = sb("sacc", [P, T])
        sq = sb("sq", [P, 2, T])
        tb = sb("tb", [P, 2, T])
        tab = sb("tab", [P, T])
        wsT = sb("wsT", [P, 4, P])
        wsn = sb("wsn", [P, 4, P])
        bbc = sb("bbc", [P, 4, P])
        ident = sb("ident", [P, P])
        ones = sb("ones", [P, P])
        bdon = sb("bdon", [P, P])
        tri = sb("tri", [P, P])
        tabc = sb("tabc", [P, 4, NCMP])
        valid = sb("valid", [P, 4])
        eps = sb("eps", [P, 1])
        w2 = sb("w2", [P, 2, DH])
        hc = sb("hc", [P, 2, 32])
        kcn = sb("kcn", [P, 32])
        vcs = sb("vcs", [32, P])
        gates = sb("gates", [P, TT, 3 * HEADS])
        cs = sb("cs", [P, 8, NCMP])
        cmx = sb("cmx", [P, 8])
        cw = sb("cw", [P, 8])
        nmx = sb("nmx", [P, 2])
        lsum = sb("lsum", [P, 2])
        lw = sb("lw", [P, 2])
        g8 = sb("g8", [P, 2])
        mst = sb("mst", [P, 2])
        NP_ROWS = 126
        NPAR = NP_ROWS + 4 * CONV_W
        pall = sb("pall", [P, L, NPAR])
        par = sb("par", [P, NPAR])

        TP = T + CONV_W - 1
        cin = convb[:, 0:4 * TP].rearrange("p (j t) -> p j t", j=4)
        cacc = convb[:, 4 * TP:4 * TP + 4 * T].rearrange("p (j t) -> p j t", j=4)
        gC = convb[:, 0:8 * T].rearrange("p (j t) -> p j t", j=8)
        w1v = cacc.rearrange("p j t -> p (j t)").rearrange("p (j e) -> p j e", j=CMP_LEN)
        w1k = big[:, 0:4 * T].rearrange("p (j e) -> p j e", j=CMP_LEN)
        blk = [big[:, (4 + 2 * i) * T:(4 + 2 * i) * T + CMP_LEN * NCMP]
               .rearrange("p (j n) -> p j n", j=CMP_LEN) for i in range(2)]
        uG = big[:, 0:4 * T].rearrange("p (j t) -> p j t", j=4)
        vG = big[:, 4 * T:8 * T].rearrange("p (j t) -> p j t", j=4)
        mrg = big[:, :].rearrange("p (j t) -> p j t", j=8)
        xnat = big[:, :].rearrange("p (a d) -> p a d", a=TT)
        sil, sr, hb = tmp3[:, 0, :], tmp3[:, 1, :], tmp3[:, 2, :]
        pt = tmp3[:, 0:2, :].rearrange("p b (k q) -> p b k q", k=TT)
        memn = att[:, :, :, :].rearrange("p a b t -> p (a b t)").rearrange("p (a d) -> p a d", a=2)
        memH = hH[:, 0:4, :].rearrange("p a t -> p (a t)").rearrange("p (k m) -> p k m", k=KD)
        memL = hL[:, 0:4, :].rearrange("p a t -> p (a t)").rearrange("p (k m) -> p k m", k=KD)
        kx = kT[:, :, :].rearrange("p a t -> p (a t)").rearrange("p (h m) -> p h m", h=4)
        vx = vtok[:, :, :].rearrange("p a b -> p (a b)").rearrange("p (a c) -> p a c", a=2)
        ctab = convb[:, 0:4 * P].rearrange("p (a c) -> p a c", a=4)

        G_F1, G_MIX, G_X, G_MEM, G_F2 = 0, 8, 16, 24, 32
        P_CB, P_LG, P_LB, P_SG = 40, 44, 48, 52
        P_XQ, P_XK, P_NQ, P_NK, P_PE, P_CW = 56, 57, 58, 59, 62, NP_ROWS

        def col(c, rows=slice(0, P)):
            return par[rows, c:c + 1]

        pg = ctx.enter_context(nc.psum_tensor("pg", [P, 4, T], F32))
        pS = ctx.enter_context(nc.psum_tensor("pS", [P, 2, T], F32))
        pT = ctx.enter_context(nc.psum_tensor("pT", [P, T], F32))
        pO = ctx.enter_context(nc.psum_tensor("pO", [P, T], F32))

        NSTAT = 20
        R = HEADS * TT
        XR = 4 * TT
        rises = {}

        def sig(name, per_layer, lead=0):
            rises[name] = (per_layer, lead)
            return ctx.enter_context(nc.semaphore(name))

        def risen(s, layer, n):
            per_layer, lead = rises[s.name]
            return layer * per_layer + (lead + n)

        landed = [sig(f"landed{i}", 32 * (U // 2)) for i in range(2)]
        split_h = sig("split_h", U)
        split_l = sig("split_l", U, 2)
        unit_mm = sig("unit_mm", U, 4)
        evac = sig("evac", U, 4)
        gx_h = sig("gx_h", 4 * KD)
        gx_l = sig("gx_l", 4 * KD)
        sq_done = sig("sq_done", 4 * KD)
        sq_used = sig("sq_used", 4 * KD, 2)
        stat_in = sig("stat_in", NSTAT)
        stat_mm = sig("stat_mm", NSTAT)
        stat_rt = sig("stat_rt", NSTAT - 1)
        silu = sig("silu", 2 * FT)
        hid_h = sig("hid_h", 2 * FT)
        hid_l = sig("hid_l", 2 * FT)
        small = sig("small", 16 * 10)
        memld = sig("memld", 16 * 1)
        blk_in = sig("blk_in", 1)
        cmp1 = sig("cmp1", 1)
        cmp_act = sig("cmp_act", 1)
        cmp2 = sig("cmp2", 1)
        ws_tr = sig("ws_tr", 1)
        v_tr = sig("v_tr", 2)
        t_free = sig("t_free", 4)
        ng_in = sig("ng_in", 1)
        ng_sig = sig("ng_sig", 1)
        ng_tr = sig("ng_tr", 1)
        conv_sig = sig("conv_sig", 4)
        gelu = sig("gelu", 8)
        vn = sig("vn", 1)
        sg_tr = sig("sg_tr", TT)
        sg_cp = sig("sg_cp", TT)
        sg_mm = sig("sg_mm", TT)
        sg_out = sig("sg_out", TT)
        ln_sc = sig("ln_sc", 4)
        br_h = sig("br_h", 12)
        br_l = sig("br_l", 12)
        mg_sig = sig("mg_sig", 24)
        c_s = sig("c_s", PAIRS)
        c_in = sig("c_in", PAIRS)
        c_exp = sig("c_exp", PAIRS)
        c_p = sig("c_p", PAIRS)
        c_tr = sig("c_tr", PAIRS)
        c_cp = sig("c_cp", PAIRS)
        s_mm = sig("s_mm", R)
        s_out = sig("s_out", R)
        s_exp = sig("s_exp", R)
        p_in = sig("p_in", R)
        t_mm = sig("t_mm", R + R // 2)
        t_out = sig("t_out", R + R // 2)
        pv = sig("pv", R // 2)
        o_out = sig("o_out", R // 2, 1)
        m_h = sig("m_h", 8)
        m_in = sig("m_in", 8)
        m_l = sig("m_l", 8)
        mem_st = sig("mem_st", 1)
        mem_sc = sig("mem_sc", 1)
        mem_tr = sig("mem_tr", 4)
        mem_h = sig("mem_h", 4)
        mem_l = sig("mem_l", 4)
        xv_tr = sig("xv_tr", 2)
        xv_cp = sig("xv_cp", 2)
        xs_mm = sig("xs_mm", XR)
        xs_max = sig("xs_max", XR)
        xs_exp = sig("xs_exp", XR)
        xp_in = sig("xp_in", XR)
        xt_mm = sig("xt_mm", XR)
        xt_out = sig("xt_out", XR)
        xpv = sig("xpv", 4)
        xo_h = sig("xo_h", 4)
        xo_l = sig("xo_l", 4)
        par_in = sig("par_in", 1)
        q_ok = sig("q_ok", 1)
        xq_ok = sig("xq_ok", 1)
        consts = ctx.enter_context(nc.semaphore("consts"))
        pro_ld = ctx.enter_context(nc.semaphore("pro_ld"))
        pro_par = ctx.enter_context(nc.semaphore("pro_par"))
        pro_tr = ctx.enter_context(nc.semaphore("pro_tr"))
        pro_cp = ctx.enter_context(nc.semaphore("pro_cp"))
        fin_tr = ctx.enter_context(nc.semaphore("fin_tr"))
        fin_cp = ctx.enter_context(nc.semaphore("fin_cp"))
        stored = ctx.enter_context(nc.semaphore("stored"))
        pconst = ctx.enter_context(nc.semaphore("pconst"))

        block = ctx.enter_context(nc.Block())

        BR = {"B": 4, "A": 0, "C": 4}
        rows = [(j, c, e) for j in range(PAIRS) for c in range(TT) for e in range(KVG)]

        @block.sync
        def _(sp):
            for a in range(TT):
                sp.dma_start(xnat[:, a, :], x[0, a * P:(a + 1) * P, :]).then_inc(pro_ld, 16)

            def rows_of(ap, l, n, at):
                sp.dma_start(ctab[at:at + n, l, :], ap.rearrange("(a b) -> a b", b=P))\
                  .then_inc(pro_par, 16)

            for l in range(L):
                for g, at in ((norm_ffn1, G_F1), (norm_mix, G_MIX), (norm_xattn, G_X),
                              (mem_norm, G_MEM), (norm_ffn2, G_F2), (conv_b, P_CB),
                              (conv_ln_g, P_LG), (conv_ln_b, P_LB), (sgu_norm, P_SG),
                              (xq_norm, P_XQ), (xk_norm, P_XK)):
                    rows_of(g[l], l, g.shape[1] // P, at)
                for half in range(2):
                    cols = slice(half * DH, (half + 1) * DH)
                    sp.dma_start(ctab[P_NQ:P_NQ + 1, l, cols], nsa_q_norm[l:l + 1, :])\
                      .then_inc(pro_par, 16)
                    sp.dma_start(ctab[P_NK:P_NK + 3, l, cols], nsa_k_norm[l]).then_inc(pro_par, 16)
                    for i in range(2):
                        at = P_PE + i * CMP_LEN
                        sp.dma_start(ctab[at:at + CMP_LEN, l, cols], cmp_pe[l, i])\
                          .then_inc(pro_par, 16)
                for j in range(4):
                    sp.dma_start(ctab[j * CONV_W:(j + 1) * CONV_W, L + l, :],
                                 conv_w[l, :, j * P:(j + 1) * P]).then_inc(pro_par, 16)

            def k_rows(w):
                return w.rearrange("(k p) c -> p k c", p=P)

            def unit(l, u, i, src, kt=KD):
                s = u % 2
                sp.wait_ge(split_l, risen(split_l, l, u - 1 + 4 * i))
                half = kt // 2
                for h in (1, 0):
                    sp.dma_start(raw[:, s, h * half:(h + 1) * half, :], src(h, half))\
                        .then_inc(landed[s], 16)

            def cols_of(w, c0):
                def src(h, half):
                    return k_rows(w)[:, h * half:(h + 1) * half, c0:c0 + P]
                return src

            def at_col(w, c0, width=P):
                def src(h, half):
                    return k_rows(w)[:, h * half:(h + 1) * half, bass.ds(c0, width)]
                return src

            def ffn(l, u, wi, wo):
                ft = 0
                for n in CH:
                    with sp.Fori(0, n // 2) as i:
                        for c in range(4):
                            a, b = divmod(c, 2)
                            c0 = i * (2 * P) + (b * F + (ft + a) * P)
                            unit(l, u + c, i, at_col(wi, c0))
                    u += 2 * n
                    rows_ = wo[ft * P:(ft + n) * P, :]
                    with sp.Fori(0, KD // 4) as i:
                        for c in range(4):
                            unit(l, u + c, i, at_col(rows_, i * (4 * P) + c * P), n)
                    u += KD
                    ft += n

            with sp.Fori(0, L) as l:
                wi1, wo1, wi2, wo2 = ffn1_wi[l], ffn1_wo[l], ffn2_wi[l], ffn2_wo[l]
                win = w_in[l]
                ffn(l, 0, wi1, wo1)
                def load_small(dst, src):
                    sp.dma_start(dst, src).then_inc(small, 16)

                load_small(wsn[:, :, :], sgu_ws[l].rearrange("g t s -> t g s"))
                load_small(bbc[:, :, :].rearrange("p g t -> p (g t)"),
                           sgu_b[l].rearrange("g t -> (g t)").partition_broadcast(P))
                for half in range(2):
                    r = slice(half * DH, (half + 1) * DH)
                    for i, w1 in ((0, w1k), (1, w1v)):
                        load_small(w1[r, :, :], cmp_w1[l][i].rearrange("(j d) e -> d j e", d=DH))
                        load_small(w2[r, i, :], cmp_w2[l][i])
                for i in range(6):
                    unit(l, U_KV + i, 0, cols_of(win, C_KV + i * P))

                def pair_cols(j):
                    def src(h, half):
                        return k_rows(win)[:, :, C_Q + (j + 4 * h) * DH:C_Q + (j + 4 * h + 1) * DH]
                    return src

                for j in range(PAIRS):
                    u = U_QP + j
                    sp.wait_ge(split_l, risen(split_l, l, u - 1))
                    for h in range(2):
                        sp.dma_start(raw[:, u % 2, :, h * DH:(h + 1) * DH],
                                     pair_cols(j)(h, 0)).then_inc(landed[u % 2], 16)
                for i in range(2):
                    u = U_NG + i
                    sp.wait_ge(split_l, risen(split_l, l, u - 1))
                    for h in range(2):
                        k0 = 4 * i + 2 * h
                        sp.dma_start(raw[:, u % 2, 2 * h:2 * h + 2, :],
                                     k_rows(win)[:, k0:k0 + 2, C_NG:C_NG + P])\
                                         .then_inc(landed[u % 2], 16)
                for j in range(4):
                    unit(l, U_CONV + 2 * j, 0, cols_of(win, j * P))
                    unit(l, U_CONV + 2 * j + 1, 0, cols_of(win, DC + j * P))
                for j in range(4):
                    unit(l, U_SGU + j, 0, cols_of(win, C_SGU + DS + j * P))
                for j in range(4):
                    unit(l, U_SGU + 4 + j, 0, cols_of(win, C_SGU + j * P))
                for u0, w, br in ((U_B, sgu_out[l], 1), (U_A, conv_out[l], 0)):
                    with sp.Fori(0, KD // 2) as i:
                        for c in range(2):
                            unit(l, u0 + 2 * c, i,
                                 at_col(win, i * (2 * P) + (C_MG + br * D + c * P)))
                            unit(l, u0 + 2 * c + 1, i, at_col(w, i * (2 * P) + c * P), KB)
                with sp.Fori(0, KD // 4) as i:
                    for c in range(4):
                        unit(l, U_CM + c, i, at_col(win, i * (4 * P) + (C_MG + 2 * D + c * P)))
                sp.wait_ge(t_mm, risen(t_mm, l, R + R // 2))
                sp.dma_start(memn, mem[0].rearrange("(a p) d -> p a d", p=P)).then_inc(memld, 16)
                for m in range(KD):
                    u = U_CO + m
                    sp.wait_ge(split_l, risen(split_l, l, u - 1))
                    for h in range(2):
                        half_rows = nsa_out[l][h * 4 * DH:(h + 1) * 4 * DH, m * P:(m + 1) * P]
                        sp.dma_start(raw[h * DH:(h + 1) * DH, u % 2, 0:4, :],
                                     half_rows.rearrange("(j d) c -> d j c", d=DH))\
                                         .then_inc(landed[u % 2], 16)
                for u0, w, n, kt in ((U_XKV, xkv[l], 8, KD), (U_WO, w_out[l], 8, KD),
                                     (U_XQ, xq[l], 4, KD), (U_XO, xo[l], 8, 4)):
                    with sp.Fori(0, n // 4) as i:
                        for c in range(4):
                            unit(l, u0 + c, i, at_col(w, i * (4 * P) + c * P), kt)
                ffn(l, U_F2, wi2, wo2)

            for a in range(TT):
                sp.wait_ge(fin_cp, 2 * (a + 1))
                sp.dma_start(out[0, a * P:(a + 1) * P, :], xnat[:, a, :]).then_inc(stored, 16)
            sp.wait_ge(stored, 16 * TT)

        @block.gpsimd
        def _(pool):
            pool.memset(ident[:, :], 0.0)
            pool.memset(ones[:, :], 1.0)
            pool.memset(bdon[:, :], 0.0)
            pool.memset(tri[:, :], 1.0)
            pool.memset(valid[:, :], 1.0)
            pool.memset(eps[:, :], EPS)
            pool.iota(tab[:, :], pattern=[[1, T]], base=-(T - P), channel_multiplier=-1,
                      allow_small_or_imprecise_dtypes=True)
            pool.iota(tabc[:, :, :], pattern=[[-P, 4], [CMP_STRIDE, NCMP]], base=CMP_LEN - 1,
                      channel_multiplier=-1, allow_small_or_imprecise_dtypes=True)
            pool.drain().then_inc(pconst, 1)
            pool.wait_ge(pconst, 1)
            pool.memset(bdon[0:DH, 0:DH], 1.0)
            pool.drain().then_inc(pconst, 1)
            pool.wait_ge(pconst, 2)
            pool.memset(bdon[DH:P, DH:P], 1.0)
            pool.drain().then_inc(pconst, 1)
            pool.wait_ge(pconst, 3)
            pool.affine_select(out=ident[:, :], in_=ident[:, :], compare_op=ALU.not_equal, fill=1.0,
                               base=0, pattern=[[-1, P]], channel_multiplier=1)
            pool.affine_select(out=tri[:, :], in_=tri[:, :], compare_op=ALU.is_ge, fill=0.0,
                               base=0, pattern=[[1, P]], channel_multiplier=-1)
            pool.affine_select(out=tab[:, :], in_=tab[:, :], compare_op=ALU.is_ge, fill=NEG,
                               base=T - P, pattern=[[-1, T]], channel_multiplier=1)
            pool.affine_select(out=tabc[:, :, :], in_=tabc[:, :, :], compare_op=ALU.is_ge, fill=NEG,
                               base=-(CMP_LEN - 1), pattern=[[P, 4], [-CMP_STRIDE, NCMP]],
                               channel_multiplier=1)
            pool.affine_select(out=valid[:, 0:1], in_=valid[:, 0:1], compare_op=ALU.is_ge, fill=0.0,
                               base=-(CMP_LEN - 1), pattern=[[1, 1]], channel_multiplier=1)
            pool.drain().then_inc(consts, 1)
            pool.sem_inc(split_l, risen(split_l, 0, 0))

            with pool.Fori(0, L * U // 4) as g:
                for s in range(4):
                    pool.wait_ge(split_h, g * 4 + (s + 1))
                    pool.tensor_tensor(wL[:, s, :, :], raw[:, s % 2, :, :],
                                       wH[:, s, :, :].bitcast(F32), ALU.subtract)\
                        .then_inc(split_l, 1)

        @block.tensor
        def _(pe):
            mm = pe.matmul

            def unit(l, u, i, kt, rh, rl, n=T, before=None):
                s = u % 4
                pe.wait_ge(split_l, risen(split_l, l, u + 1 + 4 * i))
                pe.wait_ge(evac, risen(evac, l, u - 3 + 4 * i))
                o = pg[:, s, 0:n]
                for k in range(kt):
                    if before:
                        before(k)
                    mm(o, wH[:, s, k, :], rh(k), start=(k == 0), stop=False)
                    mm(o, wH[:, s, k, :], rl(k), start=False, stop=False)
                    last = mm(o, wL[:, s, k, :], rh(k), start=False, stop=(k == kt - 1))
                last.then_inc(unit_mm, 1)

            def stat(l, s, weights, n=T):
                pe.wait_ge(stat_in, risen(stat_in, l, s + 1))
                mm(pO[:, 0:n], weights[:, :], sacc[:, 0:n], start=True, stop=True)\
                    .then_inc(stat_mm, 1)

            gH, gL = (lambda k: gxH[:, k, :]), (lambda k: gxL[:, k, :])

            def norm_ready(l, n):
                def before(k):
                    pe.wait_ge(gx_l, risen(gx_l, l, KD * n + k + 1))
                return before

            def ffn(l, u, f, n_norm, s_norm):
                ft = 0
                for ch, n in enumerate(CH):
                    first = 0
                    if ch == 0:
                        for c in range(4):
                            unit(l, u + c, 0, KD, gH, gL,
                                 before=norm_ready(l, n_norm) if c == 0 else None)
                            if c == 1:
                                stat(l, s_norm, ones)
                        first = 1
                    with pe.Fori(first, n // 2) as i:
                        for c in range(4):
                            unit(l, u + c, i, KD, gH, gL)
                    u += 2 * n

                    def hid(k):
                        pe.wait_ge(hid_l, risen(hid_l, l, f * FT + ft + k + 1))

                    for m in range(KD):
                        unit(l, u + m, 0, n, lambda k: hH[:, k, :], lambda k: hL[:, k, :],
                             before=hid if m == 0 else None)
                    u += KD
                    ft += n

            def turn(dst, src, k=P):
                return pe.transpose(dst, src, ident[0:k, 0:k])

            pe.sem_inc(unit_mm, risen(unit_mm, 0, 0))
            pe.wait_ge(consts, 1)
            pe.wait_ge(pro_par, 16 * L * 23)
            for l in range(L):
                turn(pT[:, l * P:l * P + NP_ROWS], ctab[0:NP_ROWS, l, :], NP_ROWS)
            for l in range(L):
                last = turn(pT[:, (2 + l) * P:(2 + l) * P + 4 * CONV_W],
                            ctab[0:4 * CONV_W, L + l, :], 4 * CONV_W)
            last.then_inc(pro_tr, 1)
            pe.wait_ge(pro_ld, 16 * TT)
            for k in range(KD):
                if k >= 4:
                    pe.wait_ge(pro_cp, k - 4 + 2)
                for a in range(TT):
                    last = turn(pg[:, k % 4, a * P:(a + 1) * P], xnat[:, a, k * P:(k + 1) * P])
                last.then_inc(pro_tr, 1)

            with pe.Fori(0, L) as l:
                ffn(l, 0, 0, 0, 0)

                unit(l, U_KV, 0, KD, gH, gL, before=norm_ready(l, 1))
                unit(l, U_KV + 1, 0, KD, gH, gL)
                stat(l, 1, ones)
                unit(l, U_KV + 2, 0, KD, gH, gL)
                pe.wait_ge(small, risen(small, l, 160))
                for g in range(GROUPS):
                    last = turn(pT[:, g * P:(g + 1) * P], wsn[:, g, :])
                last.then_inc(ws_tr, 1)
                unit(l, U_KV + 3, 0, KD, gH, gL)
                stat(l, 2, bdon)
                pe.wait_ge(blk_in, risen(blk_in, l, 1))
                pe.wait_ge(t_free, risen(t_free, l, 1))
                pe.wait_ge(evac, risen(evac, l, U_KV + 4))
                for a in range(TT):
                    last = turn(pT[:, a * P:(a + 1) * P], tb[:, 0, a * P:(a + 1) * P])
                last.then_inc(v_tr, 1)
                for i, w1 in ((0, w1k), (1, w1v)):
                    for g in range(KVG):
                        r = slice(g * DH, (g + 1) * DH)
                        for j in range(CMP_LEN):
                            last = mm(pS[r, 0, 32 * i:32 * i + NCMP], w1[r, j, :], blk[i][r, j, :],
                                      start=(j == 0), stop=(j == CMP_LEN - 1))
                last.then_inc(cmp1, 1)
                unit(l, U_KV + 4, 0, KD, gH, gL)
                unit(l, U_KV + 5, 0, KD, gH, gL)
                pe.wait_ge(cmp_act, risen(cmp_act, l, 1))
                stat(l, 3, bdon)
                for g in range(KVG):
                    r = slice(g * DH, (g + 1) * DH)
                    mm(pS[r, 1, 0:NCMP], w2[r, 0, :], hc[r, 0, 0:NCMP], start=True, stop=True)
                for g in range(KVG):
                    r = slice(g * DH, (g + 1) * DH)
                    last = mm(pS[0:NCMP, 1 - g, P:P + DH], hc[r, 1, 0:NCMP],
                              w2[r, 1, :], start=True, stop=True)
                last.then_inc(cmp2, 1)
                unit(l, U_QP, 0, KD, gH, gL)
                stat(l, 4, bdon, NCMP)
                pe.wait_ge(t_free, risen(t_free, l, 2))
                pe.wait_ge(evac, risen(evac, l, U_KV + 6))
                for a in range(TT):
                    last = turn(pT[:, a * P:(a + 1) * P], tb[:, 1, a * P:(a + 1) * P])
                last.then_inc(v_tr, 1)
                for j in range(1, PAIRS):
                    unit(l, U_QP + j, 0, KD, gH, gL)
                    stat(l, 5 + j - 1, bdon)
                for i in range(2):
                    unit(l, U_NG + i, 0, 4, lambda k: gxH[:, 4 * i + k, :],
                         lambda k: gxL[:, 4 * i + k, :])
                    if i == 0:
                        stat(l, 8, bdon)
                unit(l, U_CONV, 0, KD, gH, gL)
                pe.wait_ge(t_free, risen(t_free, l, 3))
                pe.wait_ge(ng_sig, risen(ng_sig, l, 1))
                for a in range(TT):
                    last = turn(pT[:, a * P:(a + 1) * P], hb[:, a * P:(a + 1) * P])
                last.then_inc(ng_tr, 1)
                for j in range(1, 8):
                    unit(l, U_CONV + j, 0, KD, gH, gL)
                for j in range(8):
                    unit(l, U_SGU + j, 0, KD, gH, gL)
                    if j == 6:
                        stat(l, 9, ones)
                pe.wait_ge(vn, risen(vn, l, 1))
                pe.wait_ge(t_free, risen(t_free, l, 4))
                for c in range(TT):
                    if c >= 1:
                        pe.wait_ge(sg_cp, risen(sg_cp, l, c))
                    for g in range(GROUPS):
                        last = turn(pT[:, g * P:(g + 1) * P], vG[:, g, c * P:(c + 1) * P])
                    last.then_inc(sg_tr, 1)
                    pe.wait_ge(sg_cp, risen(sg_cp, l, c + 1))
                    if c >= 1:
                        pe.wait_ge(sg_out, risen(sg_out, l, c))
                    for g in range(GROUPS):
                        last = mm(pS[:, 0, g * P:(g + 1) * P], sacc[:, g * P:(g + 1) * P],
                                  wsT[:, g, :], start=True, stop=True)
                    last.then_inc(sg_mm, 1)

                def scores(r):
                    j, c, e = rows[r]
                    h, n = slice(e * DH, (e + 1) * DH), (c + 1) * P
                    if r >= 1:
                        pe.wait_ge(s_out, risen(s_out, l, r))
                    for b in range(2):
                        last = mm(pS[:, b, 0:n], qT[h, j, c * P:(c + 1) * P], kT[h, b, 0:n],
                                  start=True, stop=True)
                    last.then_inc(s_mm, 1)

                def compressed(j):
                    if j >= 1:
                        pe.wait_ge(s_out, risen(s_out, l, 8 * j))
                    for e in range(KVG):
                        h = slice(e * DH, (e + 1) * DH)
                        for c in range(TT):
                            last = mm(pS[:, e, 32 * c:32 * c + NCMP], qT[h, j, c * P:(c + 1) * P],
                                      kcn[h, 0:NCMP], start=True, stop=True)
                    last.then_inc(c_s, 1)

                def compressed_turn(j):
                    pe.wait_ge(c_p, risen(c_p, l, j + 1))
                    for e in range(KVG):
                        for c in range(TT):
                            last = turn(pS[0:NCMP, e, c * P:(c + 1) * P], cs[:, 4 * e + c, :])
                    last.then_inc(c_tr, 1)

                def probs_turned(r, b0, b1, at):
                    j, c, e = rows[r]
                    for b in range(b0, b1):
                        for k in range(c + 1):
                            last = turn(pT[:, at:at + P], att[:, r % 2, b, k * P:(k + 1) * P])
                            at += P
                    last.then_inc(t_mm, 1)

                def n_turns(r):
                    return 12 * (r // 8) + (r % 8 + 1) + max(0, r % 8 - 3)

                def values(r):
                    j, c, e = rows[r]
                    o = pO[e * DH:(e + 1) * DH, 0:P]
                    v = slice(e * DH, (e + 1) * DH)
                    for b in range(2):
                        if b == 0 or c >= 2:
                            pe.wait_ge(t_out, risen(t_out, l, n_turns(r) - (b == 0 and c >= 2)))
                        for k in range(c + 1):
                            last = mm(o, vtok[:, k, b * P + e * DH:b * P + (e + 1) * DH],
                                      pt[:, b, k, :], start=(b == 0 and k == 0),
                                      stop=(b == 1 and k == c))
                        if b == 0:
                            mm(o, vcs[0:NCMP, v], ptc[0:NCMP, e, c * P:(c + 1) * P],
                               start=False, stop=False)
                    return last

                def branch_unit(r):
                    u = U_B + r
                    if r % 2 == 0:
                        unit(l, u, 0, KD, gH, gL)
                    else:
                        br, base = ("B", 0) if r < 16 else ("A", 4)

                        def ready(k):
                            pe.wait_ge(br_l, risen(br_l, l, base + k + 1))
                        unit(l, u, 0, KB, lambda k: hH[:, BR[br] + k, :],
                             lambda k: hL[:, BR[br] + k, :], before=ready if r % 16 == 1 else None)

                pe.wait_ge(q_ok, risen(q_ok, l, 1))
                pe.wait_ge(sg_out, risen(sg_out, l, TT))
                for r in range(R):
                    j, c, e = rows[r]
                    if r % 8 == 0:
                        compressed(j)
                        branch_unit(r)
                        if r == 16:
                            stat(l, 11, ones)
                        compressed_turn(j)
                        pe.wait_ge(c_cp, risen(c_cp, l, j + 1))
                        scores(r)
                    pe.wait_ge(p_in, risen(p_in, l, r + 1))
                    if r >= 1:
                        pe.wait_ge(t_out, risen(t_out, l, n_turns(r - 1)))
                    probs_turned(r, 0, 2 if c < 2 else 1, 0)
                    if r % 8 != 7:
                        scores(r + 1)
                    if r % 8 != 0:
                        branch_unit(r)
                    if c >= 2:
                        pe.wait_ge(t_out, risen(t_out, l, n_turns(r) - 1))
                        probs_turned(r, 1, 2, 0)
                    if e == 0:
                        pe.wait_ge(o_out, risen(o_out, l, r // 2))
                    last = values(r)
                    if e == 1:
                        last.then_inc(pv, 1)
                    if r == 15:
                        pe.wait_ge(o_out, risen(o_out, l, 8))
                        stat(l, 10, ones)

                for m in range(8):
                    unit(l, U_CM + m, 0, KD, gH, gL)

                def c_ready(k):
                    pe.wait_ge(br_l, risen(br_l, l, 8 + k + 1))
                for m in range(8):
                    unit(l, U_CO + m, 0, KB, lambda k: hH[:, BR["C"] + k, :],
                         lambda k: hL[:, BR["C"] + k, :], before=c_ready if m == 0 else None)
                    if m >= 4:
                        i = m - 4
                        bank = pT[:, :] if i % 2 == 0 else pS[:, 0, :]
                        pe.wait_ge(mem_sc, risen(mem_sc, l, 1))
                        if i >= 2:
                            pe.wait_ge(mem_l, risen(mem_l, l, i - 1))
                        for k in range(2):
                            for a in range(2):
                                at = (2 * k + a) * P
                                kk = 2 * i + k
                                last = turn(bank[:, at:at + P], memn[:, a, kk * P:(kk + 1) * P])
                        last.then_inc(mem_tr, 1)

                def mem_ready(k):
                    pe.wait_ge(mem_l, risen(mem_l, l, k // 2 + 1))
                for h in range(8):
                    unit(l, U_XKV + h, 0, KD, lambda k: memH[:, k, :], lambda k: memL[:, k, :], n=M,
                         before=mem_ready if h == 0 else None)
                    if h in (3, 5):
                        stat(l, 12 + (h == 5), ones)

                def m_ready(k):
                    pe.wait_ge(m_l, risen(m_l, l, k + 1))
                for m in range(8):
                    unit(l, U_WO + m, 0, KD, gH, gL, before=m_ready if m == 0 else None)
                    if m < 2:
                        pe.wait_ge(evac, risen(evac, l, U_XKV + 8))
                        pe.wait_ge(mem_l, risen(mem_l, l, 3))
                        if m == 1:
                            pe.wait_ge(xv_cp, risen(xv_cp, l, 1))
                        for a in range(2):
                            for hh in range(2):
                                last = turn(pT[:, (2 * a + hh) * P:(2 * a + hh + 1) * P],
                                            tb[:, m, hh * M + a * P:hh * M + (a + 1) * P])
                        last.then_inc(xv_tr, 1)
                for j in range(4):
                    unit(l, U_XQ + j, 0, KD, lambda k: hH[:, k, :], lambda k: hL[:, k, :],
                         before=norm_ready(l, 2) if j == 0 else None)
                    if j >= 1:
                        stat(l, 13 + j, ones)
                for s in (17, 18):
                    stat(l, s, ones)

                pe.wait_ge(xq_ok, risen(xq_ok, l, 1))

                def x_scores(r):
                    h, c = divmod(r, TT)
                    if r >= 2:
                        pe.wait_ge(xs_exp, risen(xs_exp, l, r - 1))
                    mm(pS[:, r % 2, 0:M], qT[:, h, c * P:(c + 1) * P], kx[:, h, :],
                       start=True, stop=True).then_inc(xs_mm, 1)

                x_scores(0)
                for r in range(XR):
                    h, c = divmod(r, TT)
                    if r + 1 < XR:
                        x_scores(r + 1)
                    pe.wait_ge(xp_in, risen(xp_in, l, r + 1))
                    if r >= 1:
                        pe.wait_ge(xt_out, risen(xt_out, l, r))
                    for a in range(2):
                        last = turn(pT[:, a * P:(a + 1) * P],
                                    att[:, r % 2, 0, a * P:(a + 1) * P])
                    last.then_inc(xt_mm, 1)
                    pe.wait_ge(xt_out, risen(xt_out, l, r + 1))
                    if c == 0 and h >= 1:
                        pe.wait_ge(xo_l, risen(xo_l, l, h))
                    for a in range(2):
                        last = mm(pO[:, c * P:(c + 1) * P], vx[:, a, h * P:(h + 1) * P],
                                  tmp3[:, r % 2, a * P:(a + 1) * P], start=(a == 0), stop=(a == 1))
                    if c == TT - 1:
                        last.then_inc(xpv, 1)

                def xo_ready(k):
                    pe.wait_ge(xo_l, risen(xo_l, l, k + 1))
                for m in range(8):
                    unit(l, U_XO + m, 0, 4, lambda k: hH[:, k, :], lambda k: hL[:, k, :],
                         before=xo_ready if m == 0 else None)
                ffn(l, U_F2, 1, 3, 19)

            pe.wait_ge(evac, risen(evac, L, 0))
            for a in range(TT):
                for hf in range(2):
                    n = 2 * a + hf
                    if n >= 4:
                        pe.wait_ge(fin_cp, n - 3)
                    for k in range(4):
                        last = turn(pg[:, n % 4, k * P:(k + 1) * P],
                                    xT[:, 4 * hf + k, a * P:(a + 1) * P])
                    last.then_inc(fin_tr, 1)

        def turns(r):
            return 12 * (r // 8) + (r % 8 + 1) + max(0, r % 8 - 3)

        @block.scalar
        def _(act):
            made = [0]

            def copy(o, i, **kw):
                return act.activation(o, i, ACT.Copy, **kw)

            def split(l, u, i=0):
                s = u % 2
                act.wait_ge(landed[s], risen(landed[s], l, 32 * (u // 2 + 1) + 64 * i))
                act.wait_ge(unit_mm, risen(unit_mm, l, u - 3 + 4 * i))
                copy(wH[:, u % 4, :, :], raw[:, s, :, :]).then_inc(split_h, 1)

            def ahead(l, u, i=0):
                if u + 3 < U:
                    assert made[0] == u + 3
                    made[0] += 1
                    split(l, u + 3, i)

            def norm(l, n, gain, dst, u0):
                for k in range(KD):
                    if u0 is not None:
                        ahead(l, u0 + k)
                    act.wait_ge(evac, risen(evac, l, 0 if u0 is None else u0 + k + 1))
                    copy(dst[:, k, :], xT[:, k, :], scale=col(gain + k)).then_inc(gx_h, 1)
                    act.wait_ge(sq_used, risen(sq_used, l, KD * n + k - 1))
                    act.activation(sq[:, k % 2, :], xT[:, k, :], ACT.Square).then_inc(sq_done, 1)

            def root(l, s, dst, scale, n=T):
                act.wait_ge(stat_mm, risen(stat_mm, l, s + 1))
                act.activation(dst[:, 0:n], pO[:, 0:n], ACT.Sqrt, bias=eps[:, 0:1],
                               scale=scale).then_inc(stat_rt, 1)

            def ffn(l, u, last_norm):
                for ch, n in enumerate(CH):
                    start = made[0]
                    with act.Fori(0, n // 2) as i:
                        for c in range(2):
                            ahead(l, u + 2 * c, i)
                            act.wait_ge(evac, risen(evac, l, u + 2 * c + 1 + 4 * i))
                            act.activation(sil, tb[:, 0, :], ACT.Silu).then_inc(silu, 1)
                            ahead(l, u + 2 * c + 1, i)
                            act.wait_ge(evac, risen(evac, l, u + 2 * c + 2 + 4 * i))
                            copy(hH[:, bass.ds(i * 2 + c, 1), :].rearrange("p a t -> p (a t)"),
                                 hb).then_inc(hid_h, 1)
                    made[0] = start + 2 * n
                    u += 2 * n
                    if ch == len(CH) - 1 and last_norm:
                        norm(l, *last_norm, u)
                    else:
                        for m in range(KD):
                            ahead(l, u + m)
                    u += KD

            act.wait_ge(consts, 1)
            with act.Fori(0, L) as l:
                for u in range(3):
                    split(l, u)
                made[0] = 3
                act.wait_ge(par_in, risen(par_in, l, 1))
                norm(l, 0, G_F1, gxH, None)
                root(l, 0, rstd, 1.0 / D)
                ffn(l, 0, (1, G_MIX, gxH))

                ahead(l, U_KV)
                ahead(l, U_KV + 1)
                root(l, 1, rstd, 1.0 / D)
                ahead(l, U_KV + 2)
                ahead(l, U_KV + 3)
                root(l, 2, rv, 1.0 / DH)
                act.wait_ge(cmp1, risen(cmp1, l, 1))
                act.activation(hc[:, :, 0:NCMP],
                               pS[:, 0, 0:64].rearrange("p (i n) -> p i n", i=2)[:, :, 0:NCMP],
                               ACT.Silu).then_inc(cmp_act, 1)
                ahead(l, U_KV + 4)
                ahead(l, U_KV + 5)
                root(l, 3, rv, 1.0 / DH)
                ahead(l, U_QP)
                root(l, 4, rv, 1.0 / DH, NCMP)
                for j in range(1, PAIRS):
                    ahead(l, U_QP + j)
                    root(l, 5 + j - 1, rv, 1.0 / DH)
                ahead(l, U_NG)
                root(l, 8, rv, 1.0 / DH)
                ahead(l, U_NG + 1)
                act.wait_ge(ng_in, risen(ng_in, l, 1))
                act.activation(hb, sr, ACT.Sigmoid).then_inc(ng_sig, 1)
                for j in range(4):
                    ahead(l, U_CONV + 2 * j)
                    ahead(l, U_CONV + 2 * j + 1)
                    act.wait_ge(evac, risen(evac, l, U_CONV + 2 * j + 2))
                    act.activation(sil, tb[:, 1, :], ACT.Sigmoid).then_inc(conv_sig, 1)
                for j in range(8):
                    ahead(l, U_SGU + j)
                    act.wait_ge(evac, risen(evac, l, U_SGU + j + 1))
                    dst = vG[:, j, :] if j < 4 else uG[:, j - 4, :]
                    act.activation(dst, tb[:, j % 2, :], ACT.Gelu_apprx_tanh).then_inc(gelu, 1)
                root(l, 9, rv, 1.0 / DS)
                act.wait_ge(sg_out, risen(sg_out, l, TT))
                for k in range(KB):
                    copy(hH[:, BR["B"] + k, :], uG[:, k, :]).then_inc(br_h, 1)

                def turned_out(r, b0, b1):
                    c = rows[r][1]
                    n = (c + 1) * P
                    act.wait_ge(t_mm, risen(t_mm, l, turns(r) - (1 if b1 == 1 else 0)))
                    copy(tmp3[:, b0:b1, 0:n],
                         pT[:, 0:(b1 - b0) * n].rearrange("p (b q) -> p b q", b=b1 - b0))\
                             .then_inc(t_out, 1)

                for r in range(R):
                    j, c, e = rows[r]
                    n = (c + 1) * P
                    if r % 8 == 0:
                        act.wait_ge(c_in, risen(c_in, l, j + 1))
                        act.activation(cs[:, :, :], cs[:, :, :], ACT.Exp).then_inc(c_exp, 1)
                        ahead(l, U_B + r)
                        if r == 16:
                            root(l, 11, rv, 1.0 / DC)
                        act.wait_ge(evac, risen(evac, l, U_B + r + 1))
                        act.activation(sq[:, 0, :], tb[:, 0, :], ACT.Sigmoid).then_inc(mg_sig, 1)
                    if r == 16:
                        for k in range(KB):
                            act.wait_ge(ln_sc, risen(ln_sc, l, k + 1))
                            act.activation(cacc[:, k, :], cacc[:, k, :], ACT.Silu,
                                           bias=col(P_LB + k), scale=col(P_LG + k))
                        act.drain()
                        for k in range(KB):
                            copy(hH[:, BR["A"] + k, :], cacc[:, k, :]).then_inc(br_h, 1)
                    act.wait_ge(s_out, risen(s_out, l, r + 1))
                    act.activation(att[:, r % 2, 0, 0:n], att[:, r % 2, 0, 0:n], ACT.Exp,
                                   bias=nmx[:, 0:1], accum_out=lsum[:, 0:1])
                    act.activation(att[:, r % 2, 1, 0:n], att[:, r % 2, 1, 0:n], ACT.Exp,
                                   bias=nmx[:, 1:2], accum_out=lsum[:, 1:2]).then_inc(s_exp, 1)
                    turned_out(r, 0, 2 if c < 2 else 1)
                    if r % 8 != 0:
                        ahead(l, U_B + r)
                        if r % 2 == 0:
                            act.wait_ge(evac, risen(evac, l, U_B + r + 1))
                            act.activation(sq[:, 0, :], tb[:, 0, :], ACT.Sigmoid)\
                                .then_inc(mg_sig, 1)
                    if c >= 2:
                        turned_out(r, 1, 2)
                act.wait_ge(o_out, risen(o_out, l, R // 2))
                act.wait_ge(evac, risen(evac, l, U_B + 16))
                for k in range(KB):
                    copy(hH[:, BR["C"] + k, :], qT[:, k, :]).then_inc(br_h, 1)
                for m in range(8):
                    ahead(l, U_CM + m)
                    act.wait_ge(evac, risen(evac, l, U_CM + m + 1))
                    act.activation(gC[:, m, :], tb[:, m % 2, :], ACT.Sigmoid).then_inc(mg_sig, 1)
                act.wait_ge(memld, risen(memld, l, 16))
                for a in range(2):
                    act.activation(tmp3[:, 0:2, :].rearrange("p a t -> p (a t)"), memn[:, a, :],
                                   ACT.Square, accum_out=mst[:, a:a + 1])
                    act.drain()
                act.activation(mst[:, :], mst[:, :], ACT.Sqrt, bias=eps[:, 0:1],
                               scale=1.0 / D).then_inc(mem_st, 1)
                for m in range(8):
                    ahead(l, U_CO + m)
                    act.wait_ge(m_in, risen(m_in, l, m + 1))
                    copy(gxH[:, m, :], mrg[:, m, :]).then_inc(m_h, 1)
                    if m >= 4:
                        i = m - 4
                        bank = pT[:, :] if i % 2 == 0 else pS[:, 0, :]
                        act.wait_ge(mem_tr, risen(mem_tr, l, i + 1))
                        for k in range(2):
                            kk = 2 * i + k
                            last = copy(memH[:, kk, :], bank[:, k * M:(k + 1) * M],
                                        scale=col(G_MEM + kk))
                        last.then_inc(mem_h, 1)
                for h in range(8):
                    ahead(l, U_XKV + h)
                    if h in (3, 5):
                        root(l, 12 + (h == 5), rv, 1.0 / XDH)
                norm(l, 2, G_X, hH, U_WO)
                for j in range(4):
                    ahead(l, U_XQ + j)
                    if j >= 1:
                        root(l, 13 + j, rstd if j == 1 else rv, 1.0 / (D if j == 1 else XDH))
                for s in (17, 18):
                    root(l, s, rv, 1.0 / XDH)

                def x_exp(r):
                    act.wait_ge(xs_max, risen(xs_max, l, r + 1))
                    act.activation(att[:, r % 2, 0, 0:M], pS[:, r % 2, 0:M], ACT.Exp,
                                   bias=cmx[:, r % 8:r % 8 + 1],
                                   accum_out=lsum[:, r % 2:r % 2 + 1]).then_inc(xs_exp, 1)

                x_exp(0)
                for r in range(XR):
                    h, c = divmod(r, TT)
                    if r + 1 < XR:
                        x_exp(r + 1)
                    act.wait_ge(xt_mm, risen(xt_mm, l, r + 1))
                    copy(tmp3[:, r % 2, 0:M], pT[:, 0:M]).then_inc(xt_out, 1)
                    if c == TT - 1:
                        act.wait_ge(xpv, risen(xpv, l, h + 1))
                        copy(hH[:, h, :], pO[:, :]).then_inc(xo_h, 1)
                norm(l, 3, G_F2, gxH, U_XO)
                root(l, 19, rstd, 1.0 / D)
                ffn(l, U_F2, None)

        @block.vector
        def _(dve):
            TTt, TS, STT = dve.tensor_tensor, dve.tensor_scalar, dve.scalar_tensor_tensor

            def ready(l, u, i=0):
                dve.wait_ge(unit_mm, risen(unit_mm, l, u + 1 + 4 * i))
                return pg[:, u % 4, :]

            def scaled(dst, l, u, by=None):
                bank = ready(l, u)
                return TTt(dst, bank, rstd[:, :] if by is None else by, ALU.mult).then_inc(evac, 1)

            def stat_given(s):
                dve.drain().then_inc(stat_in, 1)

            def root_of(l, s, dst, n=T):
                dve.wait_ge(stat_rt, risen(stat_rt, l, s + 1 if s < 10 else s))
                dve.reciprocal(dst[:, 0:n], dst[:, 0:n])
                dve.drain()

            def norm(l, n, dH, dL, gain, update):
                def tail(k):
                    dve.wait_ge(gx_h, risen(gx_h, l, KD * n + k + 1))
                    STT(dL[:, k, :], xT[:, k, :], col(gain + k), dH[:, k, :].bitcast(F32),
                        ALU.mult, ALU.subtract).then_inc(gx_l, 1)
                    if k:
                        dve.drain()
                    dve.wait_ge(sq_done, risen(sq_done, l, KD * n + k + 1))
                    if k == 0:
                        dve.tensor_copy(sacc[:, :], sq[:, 0, :]).then_inc(sq_used, 1)
                    else:
                        TTt(sacc[:, :], sacc[:, :], sq[:, k % 2, :], ALU.add).then_inc(sq_used, 1)
                for k in range(KD):
                    if update:
                        update(k)
                    if k >= 1:
                        tail(k - 1)
                tail(KD - 1)
                stat_given(None)

            def residual(l, u, by):
                def update(k):
                    bank = ready(l, u + k)
                    STT(xT[:, k, :], bank, by, xT[:, k, :], ALU.mult, ALU.add).then_inc(evac, 1)
                return update

            def ffn(l, u, f, last_norm):
                ft = 0
                for ch, n in enumerate(CH):
                    with dve.Fori(0, n // 2) as i:
                        for c in range(2):
                            hid = f * FT + ft + c + 1 + 2 * i
                            bank = ready(l, u + 2 * c, i)
                            TTt(tb[:, 0, :], bank, rstd[:, :], ALU.mult).then_inc(evac, 1)
                            dve.wait_ge(silu, risen(silu, l, hid))
                            TTt(sr, sil, rstd[:, :], ALU.mult)
                            dve.drain()
                            bank = ready(l, u + 2 * c + 1, i)
                            TTt(hb, bank, sr, ALU.mult).then_inc(evac, 1)
                            dve.wait_ge(hid_h, risen(hid_h, l, hid))
                            slot = bass.ds(i * 2 + c, 1)
                            flat = "p a t -> p (a t)"
                            TTt(hL[:, slot, :].rearrange(flat), hb,
                                hH[:, slot, :].rearrange(flat).bitcast(F32),
                                ALU.subtract).then_inc(hid_l, 1)
                    u += 2 * n
                    if ch == len(CH) - 1 and last_norm:
                        norm(l, *last_norm, residual(l, u, 0.5))
                    else:
                        for m in range(KD):
                            residual(l, u, 0.5)(m)
                    u += KD
                    ft += n

            dve.wait_ge(pro_tr, 1)
            for l in range(L):
                dve.tensor_copy(pall[:, l, 0:NP_ROWS], pT[:, l * P:l * P + NP_ROWS])
                dve.tensor_copy(pall[:, l, NP_ROWS:NPAR],
                                pT[:, (2 + l) * P:(2 + l) * P + 4 * CONV_W])
            dve.drain().then_inc(pro_cp, 1)
            for k in range(KD):
                dve.wait_ge(pro_tr, k + 2)
                dve.tensor_copy(xT[:, k, :], pg[:, k % 4, :]).then_inc(pro_cp, 1)
            dve.drain().then_inc(evac, risen(evac, 0, 0))
            dve.sem_inc(sq_used, risen(sq_used, 0, 0))
            dve.sem_inc(o_out, risen(o_out, 0, 0))

            with dve.Fori(0, L) as l:
                dve.tensor_copy(par[:, :], pall[:, bass.ds(l, 1), :]
                                .rearrange("p a c -> p (a c)")).then_inc(par_in, 1)
                dve.drain()
                TS(g8[:, 0:1], col(P_NQ), float(DH) ** -0.5, None, ALU.mult)
                TS(g8[:, 1:2], col(P_XQ), float(XDH) ** -0.5, None, ALU.mult)
                norm(l, 0, gxH, gxL, G_F1, None)
                root_of(l, 0, rstd)
                ffn(l, 0, 0, (1, gxH, gxL, G_MIX))

                root_of(l, 1, rstd)
                scaled(kvc[:, 0, :], l, U_KV)
                scaled(kvc[:, 1, :], l, U_KV + 1)
                dve.drain()
                for i in range(2):
                    src = kvc[:, i, :]
                    src = bass.AP(tensor=src.tensor, offset=src.offset,
                                  ap=[src.ap[0], [1, CMP_LEN], [CMP_STRIDE, NCMP]])
                    pe_ = par[:, P_PE + i * CMP_LEN:P_PE + (i + 1) * CMP_LEN]
                    pe_ = bass.AP(tensor=pe_.tensor, offset=pe_.offset,
                                  ap=[pe_.ap[0], [1, CMP_LEN], [0, NCMP]])
                    last = TTt(blk[i], src, pe_, ALU.add)
                last.then_inc(blk_in, 1)

                def squares(src, n=T):
                    dve.drain()
                    TTt(sacc[:, 0:n], src, src, ALU.mult)
                    stat_given(None)

                def normed(l, s, x_, g, n=T):
                    root_of(l, s, rv, n)
                    return STT(x_, x_, g, rv[:, 0:n], ALU.mult, ALU.mult)

                scaled(kT[:, 0, :], l, U_KV + 2)
                squares(kT[:, 0, :])
                dve.wait_ge(ws_tr, risen(ws_tr, l, 1))
                TTt(wsT[:, :, :], pT[:, :].rearrange("p (g t) -> p g t", g=4),
                    bass.AP(tensor=tri[:, :].tensor, offset=tri[:, :].offset,
                            ap=[tri[:, :].ap[0], [0, 4], [1, P]]), ALU.mult).then_inc(t_free, 1)
                scaled(tb[:, 0, :], l, U_KV + 3)
                normed(l, 2, kT[:, 0, :], col(P_NK + 1))
                dve.wait_ge(v_tr, risen(v_tr, l, 1))
                dve.tensor_copy(vtok[:, :, 0:P], pT[:, :].rearrange("p (a c) -> p a c", a=4))\
                    .then_inc(t_free, 1)
                scaled(kT[:, 1, :], l, U_KV + 4)
                squares(kT[:, 1, :])
                dve.wait_ge(cmp2, risen(cmp2, l, 1))
                dve.tensor_copy(kcn[:, 0:NCMP], pS[:, 1, 0:NCMP])
                for g in range(KVG):
                    dve.tensor_copy(vcs[0:NCMP, g * DH:(g + 1) * DH], pS[0:NCMP, 1 - g, P:P + DH])
                scaled(tb[:, 1, :], l, U_KV + 5)
                normed(l, 3, kT[:, 1, :], col(P_NK + 2))
                squares(kcn[:, 0:NCMP], NCMP)

                scaled(qT[:, 0, :], l, U_QP)
                normed(l, 4, kcn[:, 0:NCMP], col(P_NK), NCMP)
                squares(qT[:, 0, :])
                dve.wait_ge(v_tr, risen(v_tr, l, 2))
                dve.tensor_copy(vtok[:, :, P:2 * P], pT[:, :].rearrange("p (a c) -> p a c", a=4))\
                    .then_inc(t_free, 1)
                for j in range(1, PAIRS):
                    scaled(qT[:, j, :], l, U_QP + j)
                    normed(l, 4 + j, qT[:, j - 1, :], g8[:, 0:1])
                    squares(qT[:, j, :])
                NG = 3 * HEADS
                scaled(hb, l, U_NG)
                normed(l, 8, qT[:, PAIRS - 1, :], g8[:, 0:1])
                scaled(sr, l, U_NG + 1)
                dve.drain()
                TTt(sr, sr, hb, ALU.add).then_inc(ng_in, 1)

                dve.memset(cin[:, :, 0:CONV_W - 1], 0.0)
                for j in range(4):
                    scaled(tb[:, 0, :], l, U_CONV + 2 * j)
                    if j == 0:
                        dve.wait_ge(ng_tr, risen(ng_tr, l, 1))
                        dve.tensor_copy(gates[:, :, :], pT[:, :].rearrange("p (a c) -> p a c", a=4)
                                        [:, :, 0:NG])
                        dve.drain()
                        cmp0 = gates[:, 0, 0:NG:3]
                        TS(cmp0, cmp0, valid[:, 0:1], None, ALU.mult).then_inc(t_free, 1)
                    scaled(tb[:, 1, :], l, U_CONV + 2 * j + 1)
                    dve.wait_ge(conv_sig, risen(conv_sig, l, j + 1))
                    TTt(cin[:, j, CONV_W - 1:TP], tb[:, 0, :], sil, ALU.mult)
                    dve.drain()

                def conv_tap(k):
                    for j in range(4):
                        w, o = col(P_CW + j * CONV_W + k), cacc[:, j, :]
                        if k == 0:
                            TS(o, cin[:, j, 0:T], w, col(P_CB + j), ALU.mult, ALU.add)
                        else:
                            STT(o, cin[:, j, k:k + T], w, o, ALU.mult, ALU.add)
                    dve.drain()

                tap = 0
                for j in range(8):
                    if j >= 2:
                        dve.wait_ge(gelu, risen(gelu, l, j - 1))
                    scaled(tb[:, j % 2, :], l, U_SGU + j)
                    if j == 5:
                        for k in range(4):
                            dve.wait_ge(gelu, risen(gelu, l, k + 1))
                            TTt(sacc[:, :] if k == 0 else hb, vG[:, k, :], vG[:, k, :], ALU.mult)
                            dve.drain()
                            if k:
                                TTt(sacc[:, :], sacc[:, :], hb, ALU.add)
                                dve.drain()
                        stat_given(None)
                    else:
                        for _ in range(3 if j == 0 else 2):
                            if tap < CONV_W - 16:
                                conv_tap(tap)
                                tap += 1
                root_of(l, 9, rv)
                for k in range(4):
                    STT(vG[:, k, :], vG[:, k, :], col(P_SG + k), rv[:, :], ALU.mult, ALU.mult)
                dve.drain().then_inc(vn, 1)
                dve.wait_ge(gelu, risen(gelu, l, 8))
                for c in range(TT):
                    dve.wait_ge(sg_tr, risen(sg_tr, l, c + 1))
                    dve.tensor_copy(sacc[:, :], pT[:, :]).then_inc(sg_cp, 1)
                    dve.wait_ge(sg_mm, risen(sg_mm, l, c + 1))
                    TTt(hb, pS[:, 0, :], bbc[:, :, :].rearrange("p g t -> p (g t)"), ALU.add)
                    dve.drain()
                    uc = uG[:, :, c * P:(c + 1) * P]
                    TTt(uc, uc, hb.rearrange("p (g t) -> p g t", g=4), ALU.mult).then_inc(sg_out, 1)
                dve.drain().then_inc(q_ok, 1)
                for k in range(KB):
                    dve.wait_ge(br_h, risen(br_h, l, k + 1))
                    TTt(hL[:, BR["B"] + k, :], uG[:, k, :],
                        hH[:, BR["B"] + k, :].bitcast(F32), ALU.subtract).then_inc(br_l, 1)

                def row_scores(r):
                    j, c, e = rows[r]
                    n = (c + 1) * P
                    dve.wait_ge(s_mm, risen(s_mm, l, r + 1))
                    t = tab[:, T - n:T]
                    t = bass.AP(tensor=t.tensor, offset=t.offset, ap=[t.ap[0], [0, 2], [1, n]])
                    a = att[:, r % 2, :, 0:n]
                    STT(a, t, slope[j + 4 * e], pS[:, :, 0:n], ALU.mult, ALU.add)
                    dve.drain()
                    dve.tensor_reduce(nmx[:, :], a, AX_X, ALU.max, negate=True).then_inc(s_out, 1)

                def row_probs(r):
                    j, c, e = rows[r]
                    n, h = (c + 1) * P, j + 4 * e
                    dve.wait_ge(s_exp, risen(s_exp, l, r + 1))
                    dve.reciprocal(lw[:, :], lsum[:, :])
                    dve.drain()
                    TTt(lw[:, :], lw[:, :], gates[:, c, 3 * h + 1:3 * h + 3], ALU.mult)
                    dve.drain()
                    for b in range(2):
                        a = att[:, r % 2, b, 0:n]
                        last = TS(a, a, lw[:, b:b + 1], None, ALU.mult)
                    last.then_inc(p_in, 1)

                def per_row(t):
                    t = t[:, :]
                    return bass.AP(tensor=t.tensor, offset=t.offset,
                                   ap=[t.ap[0], [1, 8], [0, NCMP]])

                def pair_scores(j):
                    dve.wait_ge(c_s, risen(c_s, l, j + 1))
                    for e in range(KVG):
                        src = pS[:, e, 0:P].rearrange("p (c n) -> p c n", c=4)
                        STT(cs[:, 4 * e:4 * e + 4, :], tabc[:, :, :], slope[j + 4 * e],
                            src[:, :, 0:NCMP], ALU.mult, ALU.add)
                    dve.drain()
                    dve.tensor_reduce(cmx[:, :], cs[:, :, :], AX_X, ALU.max)
                    dve.drain()
                    TTt(cs[:, :, :], cs[:, :, :], per_row(cmx), ALU.subtract).then_inc(c_in, 1)

                def pair_probs(j):
                    dve.wait_ge(c_exp, risen(c_exp, l, j + 1))
                    dve.tensor_reduce(cw[:, :], cs[:, :, :], AX_X, ALU.add)
                    dve.drain()
                    dve.reciprocal(cw[:, :], cw[:, :])
                    dve.drain()
                    for e in range(KVG):
                        TTt(cw[:, 4 * e:4 * e + 4], cw[:, 4 * e:4 * e + 4],
                            gates[:, :, 3 * (j + 4 * e)], ALU.mult)
                    dve.drain()
                    TTt(cs[:, :, :], cs[:, :, :], per_row(cw), ALU.mult).then_inc(c_p, 1)

                def branch_unit(r):
                    u = U_B + r
                    if r % 2 == 0:
                        scaled(tb[:, 0, :], l, u)
                        return
                    dve.wait_ge(mg_sig, risen(mg_sig, l, (r + 1) // 2))
                    m = (r % 16) // 2
                    if r < 16:
                        scaled(mrg[:, m, :], l, u, by=sq[:, 0, :])
                    else:
                        scaled(hb, l, u, by=sq[:, 0, :])
                        dve.drain()
                        TTt(mrg[:, m, :], mrg[:, m, :], hb, ALU.add)

                def outputs(r):
                    j, c, e = rows[r]
                    dve.wait_ge(pv, risen(pv, l, r // 2 + 1))
                    dve.tensor_copy(qT[:, j, c * P:(c + 1) * P], pO[:, 0:P]).then_inc(o_out, 1)

                for r in range(R):
                    j, c, e = rows[r]
                    if r % 8 == 0:
                        if r:
                            branch_unit(r - 1)
                            outputs(r - 1)
                        if r == 16:
                            TTt(sacc[:, :], cacc[:, 0, :], cacc[:, 1, :], ALU.add)
                            dve.drain()
                            for k in (2, 3):
                                TTt(sacc[:, :], sacc[:, :], cacc[:, k, :], ALU.add)
                                dve.drain()
                            stat_given(None)
                        pair_scores(j)
                        if r == 16:
                            dve.wait_ge(stat_mm, risen(stat_mm, l, 11))
                            for k in range(KB):
                                STT(cacc[:, k, :], pO[:, :], -1.0 / DC, cacc[:, k, :], ALU.mult,
                                    ALU.add)
                            dve.drain()
                            for k in range(KB):
                                TTt(sacc[:, :] if k == 0 else hb, cacc[:, k, :], cacc[:, k, :],
                                    ALU.mult)
                                dve.drain()
                                if k:
                                    TTt(sacc[:, :], sacc[:, :], hb, ALU.add)
                                    dve.drain()
                            stat_given(None)
                        pair_probs(j)
                        branch_unit(r)
                        dve.wait_ge(c_tr, risen(c_tr, l, j + 1))
                        dve.tensor_copy(ptc[0:NCMP, :, :], pS[0:NCMP, :, :]).then_inc(c_cp, 1)
                        if r == 16:
                            root_of(l, 11, rv)
                            for k in range(KB):
                                TTt(cacc[:, k, :], cacc[:, k, :], rv[:, :], ALU.mult)\
                                    .then_inc(ln_sc, 1)
                    row_scores(r)
                    if r % 8 != 0 and (r - 1) % 8 != 0:
                        branch_unit(r - 1)
                    if tap < CONV_W:
                        conv_tap(tap)
                        tap += 1
                    row_probs(r)
                    if r % 8 != 0 and r % 2 == 0:
                        outputs(r - 1)
                    if r == 16:
                        for k in range(KB):
                            dve.wait_ge(br_h, risen(br_h, l, 4 + k + 1))
                            TTt(hL[:, BR["A"] + k, :], cacc[:, k, :],
                                hH[:, BR["A"] + k, :].bitcast(F32), ALU.subtract).then_inc(br_l, 1)
                branch_unit(R - 1)
                outputs(R - 1)

                for k in range(KB):
                    dve.wait_ge(br_h, risen(br_h, l, 8 + k + 1))
                    TTt(hL[:, BR["C"] + k, :], qT[:, k, :],
                        hH[:, BR["C"] + k, :].bitcast(F32), ALU.subtract).then_inc(br_l, 1)
                for m in range(8):
                    if m >= 2:
                        dve.wait_ge(mg_sig, risen(mg_sig, l, 16 + m - 1))
                    scaled(tb[:, m % 2, :], l, U_CM + m)

                def merged_low(m):
                    dve.wait_ge(m_h, risen(m_h, l, m + 1))
                    TTt(gxL[:, m, :], mrg[:, m, :], gxH[:, m, :].bitcast(F32), ALU.subtract)\
                        .then_inc(m_l, 1)

                def memory_low(i):
                    bank = pT[:, :] if i % 2 == 0 else pS[:, 0, :]
                    dve.wait_ge(mem_h, risen(mem_h, l, i + 1))
                    for k in range(2):
                        kk = 2 * i + k
                        last = STT(memL[:, kk, :], bank[:, k * M:(k + 1) * M], col(G_MEM + kk),
                                   memH[:, kk, :].bitcast(F32), ALU.mult, ALU.subtract)
                    last.then_inc(mem_l, 1)

                dve.wait_ge(mg_sig, risen(mg_sig, l, 24))
                for m in range(8):
                    part = tb[:, m % 2, :]
                    scaled(part, l, U_CO + m, by=gC[:, m, :])
                    dve.drain()
                    TTt(mrg[:, m, :], mrg[:, m, :], part, ALU.add).then_inc(m_in, 1)
                    if m >= 1:
                        merged_low(m - 1)
                    if m == 2:
                        dve.wait_ge(mem_st, risen(mem_st, l, 1))
                        dve.reciprocal(mst[:, :], mst[:, :])
                        dve.drain()
                        for a in range(2):
                            last = TS(memn[:, a, :], memn[:, a, :], mst[:, a:a + 1], None, ALU.mult)
                        last.then_inc(mem_sc, 1)
                    if m >= 4:
                        memory_low(m - 4)
                merged_low(7)

                for h in range(8):
                    bank = ready(l, U_XKV + h)
                    dst = kx[:, h, :] if h < 4 else tb[:, (h - 4) // 2,
                                                       ((h - 4) % 2) * M:((h - 4) % 2 + 1) * M]
                    dve.tensor_copy(dst, bank[:, 0:M]).then_inc(evac, 1)
                    if h in (3, 5):
                        normed(l, 12 + (h == 5), kT[:, (h == 5) * 1, :], col(P_XK))
                    if h in (1, 3):
                        squares(kT[:, h // 2, :])

                def w_out_update(k):
                    residual(l, U_WO, 1.0)(k)
                    if k in (1, 2):
                        i = k - 1
                        dve.wait_ge(xv_tr, risen(xv_tr, l, i + 1))
                        dve.tensor_copy(vx[:, :, 2 * i * P:2 * (i + 1) * P],
                                        pT[:, :].rearrange("p (a c) -> p a c", a=2))\
                                            .then_inc(xv_cp, 1)
                norm(l, 2, hH, hL, G_X, w_out_update)
                root_of(l, 14, rstd)
                for j in range(4):
                    scaled(qT[:, j, :], l, U_XQ + j)
                    if j:
                        normed(l, 14 + j, qT[:, j - 1, :], g8[:, 1:2])
                    squares(qT[:, j, :])
                normed(l, 18, qT[:, 3, :], g8[:, 1:2])
                dve.drain().then_inc(xq_ok, 1)

                def x_max(r):
                    dve.wait_ge(xs_mm, risen(xs_mm, l, r + 1))
                    dve.tensor_reduce(cmx[:, r % 8:r % 8 + 1], pS[:, r % 2, 0:M], AX_X,
                                      ALU.max, negate=True).then_inc(xs_max, 1)

                x_max(0)
                for r in range(XR):
                    h, c = divmod(r, TT)
                    if r + 1 < XR:
                        x_max(r + 1)
                    dve.wait_ge(xs_exp, risen(xs_exp, l, r + 1))
                    dve.reciprocal(lw[:, r % 2:r % 2 + 1], lsum[:, r % 2:r % 2 + 1])
                    dve.drain()
                    TS(att[:, r % 2, 0, 0:M], att[:, r % 2, 0, 0:M], lw[:, r % 2:r % 2 + 1],
                       None, ALU.mult).then_inc(xp_in, 1)
                    if c == TT - 1:
                        dve.wait_ge(xo_h, risen(xo_h, l, h + 1))
                        TTt(hL[:, h, :], pO[:, :], hH[:, h, :].bitcast(F32), ALU.subtract)\
                            .then_inc(xo_l, 1)
                norm(l, 3, gxH, gxL, G_F2, residual(l, U_XO, 1.0))
                root_of(l, 19, rstd)
                ffn(l, U_F2, 1, None)
                dve.drain()

            for n in range(2 * TT):
                a, hf = divmod(n, 2)
                dve.wait_ge(fin_tr, n + 1)
                dve.tensor_copy(xnat[:, a, hf * T:(hf + 1) * T], pg[:, n % 4, :])\
                   .then_inc(fin_cp, 1)


_INS = ['x', 'mem', 'norm_ffn1', 'ffn1_wi', 'ffn1_wo', 'norm_mix', 'w_in', 'conv_w', 'conv_b',
        'conv_ln_g', 'conv_ln_b', 'conv_out', 'sgu_norm', 'sgu_ws', 'sgu_b', 'sgu_out',
        'nsa_q_norm', 'nsa_k_norm', 'cmp_pe', 'cmp_w1', 'cmp_w2', 'nsa_out', 'w_out', 'norm_xattn',
        'mem_norm', 'xq', 'xkv', 'xq_norm', 'xk_norm', 'xo', 'norm_ffn2', 'ffn2_wi', 'ffn2_wo']


def kernel(**inputs):
    import numpy as np
    import concourse.bacc as bacc
    from concourse.bass_utils import run_bass_kernel_spmd

    nc = bacc.Bacc("TRN2", target_bir_lowering=False, num_devices=1,
                   dynamic_dma_scratch_size=1024)
    arrays, args = {}, []
    for name in _INS:
        a = np.ascontiguousarray(inputs[name])
        arrays[f"in_{name}"] = a
        args.append(nc.dram_tensor(f"in_{name}", a.shape, mybir.dt.from_np(a.dtype),
                                   kind="ExternalInput").ap())
    shape = arrays["in_x"].shape
    args.append(nc.dram_tensor("out_y", shape, F32, kind="ExternalOutput").ap())
    trunk(nc, *args)
    r = run_bass_kernel_spmd(nc, [arrays], core_ids=[0])
    return r.results[0]["out_y"]
```

```python
from contextlib import ExitStack

import concourse.bass as bass
from concourse import mybir

F32 = mybir.dt.float32
F32R = mybir.dt.float32r
BF16 = mybir.dt.bfloat16
ALU = mybir.AluOpType
ACT = mybir.ActivationFunctionType
AX_X = mybir.AxisListType.X

P = 128
EPS = 1e-6
NEG = -1e30


def trunk(nc, x, mem, norm_ffn1, ffn1_wi, ffn1_wo, norm_mix, w_in, conv_w, conv_b, conv_ln_g,
          conv_ln_b, conv_out, sgu_norm, sgu_ws, sgu_b, sgu_out, nsa_q_norm, nsa_k_norm, cmp_pe,
          cmp_w1, cmp_w2, nsa_out, w_out, norm_xattn, mem_norm, xq, xkv, xq_norm, xk_norm, xo,
          norm_ffn2, ffn2_wi, ffn2_wo, out):
    _, T, D = x.shape
    L = norm_ffn1.shape[0]
    M = mem.shape[1]
    F = ffn1_wo.shape[1]
    CONV_W, DC = conv_w.shape[1:]
    GROUPS, CHUNK = sgu_b.shape[1:]
    DS = sgu_norm.shape[1]
    DH = nsa_q_norm.shape[1]
    XDH = xq_norm.shape[1]
    CMP_LEN = cmp_pe.shape[2]
    HEADS = nsa_out.shape[1] // DH
    KVG = 2
    CMP_STRIDE = CMP_LEN // 2
    NCMP = (T - CMP_LEN) // CMP_STRIDE + 1
    assert T == 512 and D == 1024 and DC == 512 and DS == 512 and CHUNK == P and GROUPS == 4
    assert DH == 64 and HEADS == 8 and XDH == P and M == 256 and F % P == 0 and NCMP == 31
    KD = D // P
    KB = DC // P
    TT = T // P
    FT = F // P
    C_SGU, C_Q = 2 * DC, 2 * DC + 2 * DS
    C_KV = C_Q + HEADS * DH
    C_NG = C_KV + 6 * KVG * DH
    C_MG = C_NG + 3 * HEADS
    PAIRS = HEADS // KVG
    slope = [2.0 ** (-8.0 * (h + 1) / HEADS) for h in range(HEADS)]

    CH = [8, 8, FT - 16]
    FFN = 2 * FT + 3 * KD
    U_MIX = FFN
    U_KV, U_QP = U_MIX, U_MIX + 6
    U_NG = U_QP + 4
    U_CONV = U_NG + 2
    U_SGU = U_CONV + 8
    U_B = U_SGU + 8
    U_A = U_B + 16
    U_CM = U_A + 16
    U_CO = U_CM + 8
    U_WO = U_CO + 8
    U_XQ = U_WO + 8
    U_XKV = U_XQ + 4
    U_XO = U_XKV + 8
    U_F2 = U_XO + 8
    U = U_F2 + FFN
    assert U % 4 == 0

    ctx = ExitStack()
    with ctx:
        def sb(name, shape, dt=F32):
            return ctx.enter_context(nc.sbuf_tensor(name, shape, dt))

        raw = sb("raw", [P, 2, KD, P])
        wH = sb("wH", [P, 4, KD, P], F32R)
        wL = sb("wL", [P, 4, KD, P], F32R)
        xT = sb("xT", [P, KD, T])
        gxH = sb("gxH", [P, KD, T], F32R)
        gxL = sb("gxL", [P, KD, T], F32R)
        hH = sb("hH", [P, 8, T], F32R)
        hL = sb("hL", [P, 8, T], F32R)
        big = sb("big", [P, 8 * T])
        convb = sb("convb", [P, 4 * (T + CONV_W - 1) + 4 * T])
        qT = sb("qT", [P, 4, T])
        kT = sb("kT", [P, 2, T])
        VW = DH + 1
        vtok = sb("vtok", [P, 4, 4 * VW])
        KOFF = [sum(T - P * m for m in range(k)) for k in range(TT + 1)]
        prob = sb("prob", [P, 2 * KOFF[TT]])
        att = prob[:, 0:4 * T].rearrange("p (a b t) -> p a b t", a=2, b=2)
        kvc = att[:, 1, :, :]
        tmp3 = sb("tmp3", [P, 3, T])
        nmx = sb("nmx", [P, TT, 3 * HEADS])
        nmH = sb("nmH", [3 * HEADS, T], F32R)
        nmL = sb("nmL", [3 * HEADS, T], F32R)
        rstd = sb("rstd", [P, T])
        rv = sb("rv", [P, T])
        sacc = sb("sacc", [P, T])
        sq = sb("sq", [P, 2, T])
        tb = sb("tb", [P, 2, T])
        tab = sb("tab", [P, T])
        wsT = sb("wsT", [P, 4, P])
        wsn = sb("wsn", [P, 4, P])
        bbc = sb("bbc", [P, 4, P])
        ident = sb("ident", [P, P])
        ones = sb("ones", [P, P])
        bdon = sb("bdon", [P, P])
        tri = sb("tri", [P, P])
        tabc = sb("tabc", [P, 4, NCMP])
        valid = sb("valid", [P, 4])
        eps = sb("eps", [P, 1])
        w2 = sb("w2", [P, 2, DH])
        hc = sb("hc", [P, 2, 32])
        kcn = sb("kcn", [P, 32])
        vcs = sb("vcs", [32, KVG, VW])
        pos = sb("pos", [P, TT])
        cend = sb("cend", [32, 1])
        kbias = sb("kbias", [P, HEADS, TT])
        cbias = sb("cbias", [32, HEADS])
        qbias = sb("qbias", [P, TT, HEADS, 3])
        identB = sb("identB", [P, P], BF16)
        identR = sb("identR", [32, 3 * HEADS], F32R)
        maskT = sb("maskT", [P, P], BF16)
        maskC = sb("maskC", [32, T], BF16)
        gates = sb("gates", [P, TT, 3 * HEADS])
        cs = sb("cs", [P, 8, NCMP])
        ow = sb("ow", [P, 2, 6])
        g8 = sb("g8", [P, 2])
        mst = sb("mst", [P, 2])
        NP_ROWS = 126
        NPAR = NP_ROWS + 4 * CONV_W
        pall = sb("pall", [P, L, NPAR])
        par = sb("par", [P, NPAR])

        TP = T + CONV_W - 1
        cin = convb[:, 0:4 * TP].rearrange("p (j t) -> p j t", j=4)
        cacc = convb[:, 4 * TP:4 * TP + 4 * T].rearrange("p (j t) -> p j t", j=4)
        gC = convb[:, 0:8 * T].rearrange("p (j t) -> p j t", j=8)
        w1v = cacc.rearrange("p j t -> p (j t)").rearrange("p (j e) -> p j e", j=CMP_LEN)
        w1k = big[:, 0:4 * T].rearrange("p (j e) -> p j e", j=CMP_LEN)
        blk = [big[:, (4 + 2 * i) * T:(4 + 2 * i) * T + CMP_LEN * NCMP]
               .rearrange("p (j n) -> p j n", j=CMP_LEN) for i in range(2)]
        uG = big[:, 0:4 * T].rearrange("p (j t) -> p j t", j=4)
        vG = big[:, 4 * T:8 * T].rearrange("p (j t) -> p j t", j=4)
        mrg = big[:, :].rearrange("p (j t) -> p j t", j=8)
        xnat = big[:, :].rearrange("p (a d) -> p a d", a=TT)
        sil, sr, hb = tmp3[:, 0, :], tmp3[:, 1, :], tmp3[:, 2, :]
        memn = att[:, :, :, :].rearrange("p a b t -> p (a b t)").rearrange("p (a d) -> p a d", a=2)
        memH = gxH[:, 0:4, :].rearrange("p a t -> p (a t)").rearrange("p (k m) -> p k m", k=KD)
        memL = gxL[:, 0:4, :].rearrange("p a t -> p (a t)").rearrange("p (k m) -> p k m", k=KD)
        kx = kT[:, :, :].rearrange("p a t -> p (a t)").rearrange("p (h m) -> p h m", h=4)
        vx = vtok[:, :, :].rearrange("p a b -> p (a b)")[:, 0:8 * (XDH + 1)]\
            .rearrange("p (a h c) -> p a h c", a=2, h=4)
        vt = vtok[:, :, :].rearrange("p a (g c) -> p a g c", g=4)
        o8 = wsT
        oprod = sq[:, :, :].rearrange("p a t -> p (a t)")[:, 0:12 * DH]
        ctab = convb[:, 0:4 * P].rearrange("p (a c) -> p a c", a=4)

        G_F1, G_MIX, G_X, G_MEM, G_F2 = 0, 8, 16, 24, 32
        P_CB, P_LG, P_LB, P_SG = 40, 44, 48, 52
        P_XQ, P_XK, P_NQ, P_NK, P_PE, P_CW = 56, 57, 58, 59, 62, NP_ROWS

        def col(c, rows=slice(0, P)):
            return par[rows, c:c + 1]

        pg = ctx.enter_context(nc.psum_tensor("pg", [P, 4, T], F32))
        pA = ctx.enter_context(nc.psum_tensor("pA", [P, 4, T], F32))
        pS, pT, pO = pA[:, 0:2, :], pA[:, 2, :], pA[:, 3, :]

        NSTAT = 20
        NSC = HEADS * TT + PAIRS
        ITEMS = 3 * HEADS
        def item(i):
            return i // 6, i // 3 % 2, i % 3

        PAIR_AT = {6 * j + 8: j for j in range(PAIRS - 1)}
        order = ["nm", "mean"]
        for i in range(ITEMS):
            order += [(i, kt) for kt in range(1 if i % 3 == 0 else TT)]
            if i == 2:
                order.append("var")
            if i in PAIR_AT:
                order.append(("pair", PAIR_AT[i]))
        order.append(("pair", PAIRS - 1))
        STEP = {key: n for n, key in enumerate(order)}
        NSTEP = len(STEP)

        order = ["nm"]
        for h in range(4):
            order += [(h, 0), (h, 1)] + ([("turn", h - 2)] if h >= 2 else [])
        XSTEP = {key: n for n, key in enumerate(order + [("turn", 2), ("turn", 3)])}

        scored = [u for j in range(PAIRS) for u in
                  [(j, None, None)] + [(j, c, e) for c in range(TT) for e in range(KVG)]]

        rises = {}

        def sig(name, per_layer, lead=0):
            rises[name] = (per_layer, lead)
            return ctx.enter_context(nc.semaphore(name))

        def risen(s, layer, n):
            per_layer, lead = rises[s.name]
            return layer * per_layer + (lead + n)

        landed = [sig(f"landed{i}", 32 * (U // 2)) for i in range(2)]
        split_h = sig("split_h", U)
        split_l = sig("split_l", U, 2)
        unit_mm = sig("unit_mm", U, 4)
        evac = sig("evac", U, 4)
        gx_h = sig("gx_h", 4 * KD)
        gx_l = sig("gx_l", 4 * KD)
        sq_done = sig("sq_done", 4 * KD)
        sq_used = sig("sq_used", 4 * KD, 2)
        stat_in = sig("stat_in", NSTAT)
        stat_mm = sig("stat_mm", NSTAT - 2)
        stat_rt = sig("stat_rt", NSTAT - 2)
        silu = sig("silu", 2 * FT)
        hid_h = sig("hid_h", 2 * FT)
        hid_l = sig("hid_l", 2 * FT)
        small = sig("small", 16 * 10)
        memld = sig("memld", 16 * 1)
        blk_in = sig("blk_in", 1)
        cmp1 = sig("cmp1", 1)
        cmp_act = sig("cmp_act", 1)
        cmp2 = sig("cmp2", 1)
        ws_tr = sig("ws_tr", 1)
        v_tr = sig("v_tr", 2)
        t_free = sig("t_free", 4)
        ng_in = sig("ng_in", 1)
        ng_sig = sig("ng_sig", 1)
        ng_tr = sig("ng_tr", 1)
        conv_sig = sig("conv_sig", 4)
        gelu = sig("gelu", 8)
        vn = sig("vn", 1)
        sg_tr = sig("sg_tr", TT)
        sg_cp = sig("sg_cp", TT)
        sg_mm = sig("sg_mm", TT)
        sg_out = sig("sg_out", TT)
        ln_sc = sig("ln_sc", 4)
        br_h = sig("br_h", 8)
        br_l = sig("br_l", 12)
        mg_sig = sig("mg_sig", 24)
        s_mm = sig("s_mm", NSC)
        s_out = sig("s_out", NSC)
        nm_in = sig("nm_in", 1)
        nm_l = sig("nm_l", 1)
        st_mm = sig("st_mm", NSTEP)
        st_out = sig("st_out", NSTEP)
        pv = sig("pv", ITEMS)
        o_out = sig("o_out", HEADS)
        o_in = sig("o_in", HEADS)
        m_h = sig("m_h", 8)
        m_in = sig("m_in", 8)
        m_l = sig("m_l", 8)
        mem_st = sig("mem_st", 1)
        mem_sc = sig("mem_sc", 1)
        mem_tr = sig("mem_tr", 4)
        mem_h = sig("mem_h", 4)
        mem_l = sig("mem_l", 4)
        xv_tr = sig("xv_tr", 2)
        xv_cp = sig("xv_cp", 2)
        xs_mm = sig("xs_mm", 8)
        xs_out = sig("xs_out", 8)
        xnm_l = sig("xnm_l", 1)
        xst_mm = sig("xst_mm", len(XSTEP))
        xst_out = sig("xst_out", len(XSTEP))
        xpv = sig("xpv", 4)
        xo_out = sig("xo_out", 4)
        xo_l = sig("xo_l", 4)
        par_in = sig("par_in", 1)
        q_ok = sig("q_ok", 1)
        xk_ok = sig("xk_ok", 2)
        consts = ctx.enter_context(nc.semaphore("consts"))
        pro_ld = ctx.enter_context(nc.semaphore("pro_ld"))
        pro_par = ctx.enter_context(nc.semaphore("pro_par"))
        pro_tr = ctx.enter_context(nc.semaphore("pro_tr"))
        pro_cp = ctx.enter_context(nc.semaphore("pro_cp"))
        fin_tr = ctx.enter_context(nc.semaphore("fin_tr"))
        fin_cp = ctx.enter_context(nc.semaphore("fin_cp"))
        stored = ctx.enter_context(nc.semaphore("stored"))
        pconst = ctx.enter_context(nc.semaphore("pconst"))

        block = ctx.enter_context(nc.Block())

        BR = {"B": 4, "A": 0, "C": 4}
        B_LAG, A_LAG = 1, 4

        @block.sync
        def _(sp):
            for a in range(TT):
                sp.dma_start(xnat[:, a, :], x[0, a * P:(a + 1) * P, :]).then_inc(pro_ld, 16)

            def rows_of(ap, l, n, at):
                sp.dma_start(ctab[at:at + n, l, :], ap.rearrange("(a b) -> a b", b=P))\
                  .then_inc(pro_par, 16)

            for l in range(L):
                for g, at in ((norm_ffn1, G_F1), (norm_mix, G_MIX), (norm_xattn, G_X),
                              (mem_norm, G_MEM), (norm_ffn2, G_F2), (conv_b, P_CB),
                              (conv_ln_g, P_LG), (conv_ln_b, P_LB), (sgu_norm, P_SG),
                              (xq_norm, P_XQ), (xk_norm, P_XK)):
                    rows_of(g[l], l, g.shape[1] // P, at)
                for half in range(2):
                    cols = slice(half * DH, (half + 1) * DH)
                    sp.dma_start(ctab[P_NQ:P_NQ + 1, l, cols], nsa_q_norm[l:l + 1, :])\
                      .then_inc(pro_par, 16)
                    sp.dma_start(ctab[P_NK:P_NK + 3, l, cols], nsa_k_norm[l]).then_inc(pro_par, 16)
                    for i in range(2):
                        at = P_PE + i * CMP_LEN
                        sp.dma_start(ctab[at:at + CMP_LEN, l, cols], cmp_pe[l, i])\
                          .then_inc(pro_par, 16)
                for j in range(4):
                    sp.dma_start(ctab[j * CONV_W:(j + 1) * CONV_W, L + l, :],
                                 conv_w[l, :, j * P:(j + 1) * P]).then_inc(pro_par, 16)

            def k_rows(w):
                return w.rearrange("(k p) c -> p k c", p=P)

            def unit(l, u, i, src, kt=KD):
                s = u % 2
                sp.wait_ge(split_l, risen(split_l, l, u - 1 + 4 * i))
                half = kt // 2
                for h in (1, 0):
                    sp.dma_start(raw[:, s, h * half:(h + 1) * half, :], src(h, half))\
                        .then_inc(landed[s], 16)

            def cols_of(w, c0):
                def src(h, half):
                    return k_rows(w)[:, h * half:(h + 1) * half, c0:c0 + P]
                return src

            def at_col(w, c0, width=P):
                def src(h, half):
                    return k_rows(w)[:, h * half:(h + 1) * half, bass.ds(c0, width)]
                return src

            def ffn(l, u, wi, wo):
                ft = 0
                for n in CH:
                    with sp.Fori(0, n // 2) as i:
                        for c in range(4):
                            a, b = divmod(c, 2)
                            c0 = i * (2 * P) + (b * F + (ft + a) * P)
                            unit(l, u + c, i, at_col(wi, c0))
                    u += 2 * n
                    rows_ = wo[ft * P:(ft + n) * P, :]
                    with sp.Fori(0, KD // 4) as i:
                        for c in range(4):
                            unit(l, u + c, i, at_col(rows_, i * (4 * P) + c * P), n)
                    u += KD
                    ft += n

            with sp.Fori(0, L) as l:
                wi1, wo1, wi2, wo2 = ffn1_wi[l], ffn1_wo[l], ffn2_wi[l], ffn2_wo[l]
                win = w_in[l]
                ffn(l, 0, wi1, wo1)
                def load_small(dst, src):
                    sp.dma_start(dst, src).then_inc(small, 16)

                load_small(wsn[:, :, :], sgu_ws[l].rearrange("g t s -> t g s"))
                load_small(bbc[:, :, :].rearrange("p g t -> p (g t)"),
                           sgu_b[l].rearrange("g t -> (g t)").partition_broadcast(P))
                for half in range(2):
                    r = slice(half * DH, (half + 1) * DH)
                    for i, w1 in ((0, w1k), (1, w1v)):
                        load_small(w1[r, :, :], cmp_w1[l][i].rearrange("(j d) e -> d j e", d=DH))
                        load_small(w2[r, i, :], cmp_w2[l][i])
                for i in range(6):
                    unit(l, U_KV + i, 0, cols_of(win, C_KV + i * P))

                def pair_cols(j):
                    def src(h, half):
                        return k_rows(win)[:, :, C_Q + (j + 4 * h) * DH:C_Q + (j + 4 * h + 1) * DH]
                    return src

                for j in range(PAIRS):
                    u = U_QP + j
                    sp.wait_ge(split_l, risen(split_l, l, u - 1))
                    for h in range(2):
                        sp.dma_start(raw[:, u % 2, :, h * DH:(h + 1) * DH],
                                     pair_cols(j)(h, 0)).then_inc(landed[u % 2], 16)
                for i in range(2):
                    u = U_NG + i
                    sp.wait_ge(split_l, risen(split_l, l, u - 1))
                    for h in range(2):
                        k0 = 4 * i + 2 * h
                        sp.dma_start(raw[:, u % 2, 2 * h:2 * h + 2, :],
                                     k_rows(win)[:, k0:k0 + 2, C_NG:C_NG + P])\
                                         .then_inc(landed[u % 2], 16)
                for j in range(4):
                    unit(l, U_CONV + 2 * j, 0, cols_of(win, j * P))
                    unit(l, U_CONV + 2 * j + 1, 0, cols_of(win, DC + j * P))
                for j in range(4):
                    unit(l, U_SGU + j, 0, cols_of(win, C_SGU + DS + j * P))
                for j in range(4):
                    unit(l, U_SGU + 4 + j, 0, cols_of(win, C_SGU + j * P))
                for u0, w, br in ((U_B, sgu_out[l], 1), (U_A, conv_out[l], 0)):
                    with sp.Fori(0, KD // 2) as i:
                        for c in range(2):
                            unit(l, u0 + 2 * c, i,
                                 at_col(win, i * (2 * P) + (C_MG + br * D + c * P)))
                            unit(l, u0 + 2 * c + 1, i, at_col(w, i * (2 * P) + c * P), KB)
                with sp.Fori(0, KD // 4) as i:
                    for c in range(4):
                        unit(l, U_CM + c, i, at_col(win, i * (4 * P) + (C_MG + 2 * D + c * P)))
                sp.wait_ge(pv, risen(pv, l, ITEMS))
                sp.dma_start(memn, mem[0].rearrange("(a p) d -> p a d", p=P)).then_inc(memld, 16)
                for m in range(KD):
                    u = U_CO + m
                    sp.wait_ge(split_l, risen(split_l, l, u - 1))
                    for h in range(2):
                        half_rows = nsa_out[l][h * 4 * DH:(h + 1) * 4 * DH, m * P:(m + 1) * P]
                        sp.dma_start(raw[h * DH:(h + 1) * DH, u % 2, 0:4, :],
                                     half_rows.rearrange("(j d) c -> d j c", d=DH))\
                                         .then_inc(landed[u % 2], 16)
                for u0, w, n, kt in ((U_WO, w_out[l], 8, KD), (U_XQ, xq[l], 4, KD),
                                     (U_XKV, xkv[l], 8, KD), (U_XO, xo[l], 8, 4)):
                    with sp.Fori(0, n // 4) as i:
                        for c in range(4):
                            unit(l, u0 + c, i, at_col(w, i * (4 * P) + c * P), kt)
                ffn(l, U_F2, wi2, wo2)

            for a in range(TT):
                sp.wait_ge(fin_cp, 2 * (a + 1))
                sp.dma_start(out[0, a * P:(a + 1) * P, :], xnat[:, a, :]).then_inc(stored, 16)
            sp.wait_ge(stored, 16 * TT)

        @block.gpsimd
        def _(pool):
            pool.memset(ident[:, :], 0.0)
            pool.memset(ones[:, :], 1.0)
            pool.memset(bdon[:, :], 0.0)
            pool.memset(tri[:, :], 1.0)
            pool.memset(valid[:, :], 1.0)
            pool.memset(eps[:, :], EPS)
            pool.memset(vcs[:, :, :], 1.0)
            pool.memset(tb[:, 0, 0:P], 0.0)
            pool.memset(tb[:, 1, :], 0.0)
            pool.iota(pos[:, :], pattern=[[P, TT]], base=0, channel_multiplier=1,
                      allow_small_or_imprecise_dtypes=True)
            pool.iota(cend[:, :], pattern=[[0, 1]], base=CMP_LEN - 1,
                      channel_multiplier=CMP_STRIDE, allow_small_or_imprecise_dtypes=True)
            pool.iota(tab[:, :], pattern=[[1, T]], base=-(T - P), channel_multiplier=-1,
                      allow_small_or_imprecise_dtypes=True)
            pool.iota(tabc[:, :, :], pattern=[[-P, 4], [CMP_STRIDE, NCMP]], base=CMP_LEN - 1,
                      channel_multiplier=-1, allow_small_or_imprecise_dtypes=True)
            pool.drain().then_inc(pconst, 1)
            pool.wait_ge(pconst, 1)
            pool.memset(bdon[0:DH, 0:DH], 1.0)
            pool.drain().then_inc(pconst, 1)
            pool.wait_ge(pconst, 2)
            pool.memset(bdon[DH:P, DH:P], 1.0)
            pool.drain().then_inc(pconst, 1)
            pool.wait_ge(pconst, 3)
            pool.affine_select(out=ident[:, :], in_=ident[:, :], compare_op=ALU.not_equal, fill=1.0,
                               base=0, pattern=[[-1, P]], channel_multiplier=1)
            pool.affine_select(out=tri[:, :], in_=tri[:, :], compare_op=ALU.is_ge, fill=0.0,
                               base=0, pattern=[[1, P]], channel_multiplier=-1)
            pool.affine_select(out=tb[:, 0, 0:P], in_=tb[:, 0, 0:P], compare_op=ALU.is_ge,
                               fill=NEG, base=0, pattern=[[1, P]], channel_multiplier=-1)
            pool.affine_select(out=tb[:, 1, :], in_=tb[:, 1, :], compare_op=ALU.is_ge, fill=NEG,
                               base=-(CMP_LEN - 1), pattern=[[1, T]],
                               channel_multiplier=-CMP_STRIDE)
            pool.affine_select(out=tab[:, :], in_=tab[:, :], compare_op=ALU.is_ge, fill=NEG,
                               base=T - P, pattern=[[-1, T]], channel_multiplier=1)
            pool.affine_select(out=tabc[:, :, :], in_=tabc[:, :, :], compare_op=ALU.is_ge, fill=NEG,
                               base=-(CMP_LEN - 1), pattern=[[P, 4], [-CMP_STRIDE, NCMP]],
                               channel_multiplier=1)
            pool.affine_select(out=valid[:, 0:1], in_=valid[:, 0:1], compare_op=ALU.is_ge, fill=0.0,
                               base=-(CMP_LEN - 1), pattern=[[1, 1]], channel_multiplier=1)
            pool.drain().then_inc(consts, 1)
            pool.sem_inc(split_l, risen(split_l, 0, 0))

            with pool.Fori(0, L * U // 4) as g:
                for s in range(4):
                    pool.wait_ge(split_h, g * 4 + (s + 1))
                    pool.tensor_tensor(wL[:, s, :, :], raw[:, s % 2, :, :],
                                       wH[:, s, :, :].bitcast(F32), ALU.subtract)\
                        .then_inc(split_l, 1)

        @block.tensor
        def _(pe):
            mm = pe.matmul

            def unit(l, u, i, kt, rh, rl, n=T, before=None):
                s = u % 4
                pe.wait_ge(split_l, risen(split_l, l, u + 1 + 4 * i))
                pe.wait_ge(evac, risen(evac, l, u - 3 + 4 * i))
                o = pg[:, s, 0:n]
                for k in range(kt):
                    if before:
                        before(k)
                    mm(o, wH[:, s, k, :], rh(k), start=(k == 0), stop=False)
                    mm(o, wH[:, s, k, :], rl(k), start=False, stop=False)
                    last = mm(o, wL[:, s, k, :], rh(k), start=False, stop=(k == kt - 1))
                last.then_inc(unit_mm, 1)

            def stat(l, s, weights, n=T):
                pe.wait_ge(stat_in, risen(stat_in, l, s + 1))
                mm(pO[:, 0:n], weights[:, :], sacc[:, 0:n], start=True, stop=True)\
                    .then_inc(stat_mm, 1)

            gH, gL = (lambda k: gxH[:, k, :]), (lambda k: gxL[:, k, :])

            def norm_ready(l, n):
                def before(k):
                    pe.wait_ge(gx_l, risen(gx_l, l, KD * n + k + 1))
                return before

            def ffn(l, u, f, n_norm, s_norm):
                ft = 0
                for ch, n in enumerate(CH):
                    first = 0
                    if ch == 0:
                        for c in range(4):
                            unit(l, u + c, 0, KD, gH, gL,
                                 before=norm_ready(l, n_norm) if c == 0 else None)
                            if c == 1:
                                stat(l, s_norm, ones)
                        first = 1
                    with pe.Fori(first, n // 2) as i:
                        for c in range(4):
                            unit(l, u + c, i, KD, gH, gL)
                    u += 2 * n

                    def hid(k):
                        pe.wait_ge(hid_l, risen(hid_l, l, f * FT + ft + k + 1))

                    for m in range(KD):
                        unit(l, u + m, 0, n, lambda k: hH[:, k, :], lambda k: hL[:, k, :],
                             before=hid if m == 0 else None)
                    u += KD
                    ft += n

            def turn(dst, src, k=P):
                return pe.transpose(dst, src, ident[0:k, 0:k])

            pe.sem_inc(unit_mm, risen(unit_mm, 0, 0))
            pe.wait_ge(consts, 1)
            pe.wait_ge(pro_par, 16 * L * 23)
            for l in range(L):
                turn(pT[:, l * P:l * P + NP_ROWS], ctab[0:NP_ROWS, l, :], NP_ROWS)
            for l in range(L):
                last = turn(pT[:, (2 + l) * P:(2 + l) * P + 4 * CONV_W],
                            ctab[0:4 * CONV_W, L + l, :], 4 * CONV_W)
            last.then_inc(pro_tr, 1)
            pe.wait_ge(pro_ld, 16 * TT)
            for k in range(KD):
                if k >= 4:
                    pe.wait_ge(pro_cp, k - 4 + 2)
                for a in range(TT):
                    last = turn(pg[:, k % 4, a * P:(a + 1) * P], xnat[:, a, k * P:(k + 1) * P])
                last.then_inc(pro_tr, 1)

            with pe.Fori(0, L) as l:
                ffn(l, 0, 0, 0, 0)

                unit(l, U_KV, 0, KD, gH, gL, before=norm_ready(l, 1))
                unit(l, U_KV + 1, 0, KD, gH, gL)
                stat(l, 1, ones)
                unit(l, U_KV + 2, 0, KD, gH, gL)
                pe.wait_ge(small, risen(small, l, 160))
                for g in range(GROUPS):
                    last = turn(pT[:, g * P:(g + 1) * P], wsn[:, g, :])
                last.then_inc(ws_tr, 1)
                unit(l, U_KV + 3, 0, KD, gH, gL)
                stat(l, 2, bdon)
                pe.wait_ge(blk_in, risen(blk_in, l, 1))
                pe.wait_ge(t_free, risen(t_free, l, 1))
                pe.wait_ge(evac, risen(evac, l, U_KV + 4))
                for a in range(TT):
                    last = turn(pT[:, a * P:(a + 1) * P], tb[:, 0, a * P:(a + 1) * P])
                last.then_inc(v_tr, 1)
                for i, w1 in ((0, w1k), (1, w1v)):
                    for g in range(KVG):
                        r = slice(g * DH, (g + 1) * DH)
                        for j in range(CMP_LEN):
                            last = mm(pS[r, 0, 32 * i:32 * i + NCMP], w1[r, j, :], blk[i][r, j, :],
                                      start=(j == 0), stop=(j == CMP_LEN - 1))
                last.then_inc(cmp1, 1)
                unit(l, U_KV + 4, 0, KD, gH, gL)
                unit(l, U_KV + 5, 0, KD, gH, gL)
                pe.wait_ge(cmp_act, risen(cmp_act, l, 1))
                stat(l, 3, bdon)
                for g in range(KVG):
                    r = slice(g * DH, (g + 1) * DH)
                    mm(pS[r, 1, 0:NCMP], w2[r, 0, :], hc[r, 0, 0:NCMP], start=True, stop=True)
                for g in range(KVG):
                    r = slice(g * DH, (g + 1) * DH)
                    last = mm(pS[0:NCMP, 1 - g, P:P + DH], hc[r, 1, 0:NCMP],
                              w2[r, 1, :], start=True, stop=True)
                last.then_inc(cmp2, 1)
                unit(l, U_QP, 0, KD, gH, gL)
                stat(l, 4, bdon, NCMP)
                pe.wait_ge(t_free, risen(t_free, l, 2))
                pe.wait_ge(evac, risen(evac, l, U_KV + 6))
                for a in range(TT):
                    last = turn(pT[:, a * P:(a + 1) * P], tb[:, 1, a * P:(a + 1) * P])
                last.then_inc(v_tr, 1)
                for j in range(1, PAIRS):
                    unit(l, U_QP + j, 0, KD, gH, gL)
                    stat(l, 5 + j - 1, bdon)
                for i in range(2):
                    unit(l, U_NG + i, 0, 4, lambda k: gxH[:, 4 * i + k, :],
                         lambda k: gxL[:, 4 * i + k, :])
                    if i == 0:
                        stat(l, 8, bdon)
                unit(l, U_CONV, 0, KD, gH, gL)
                pe.wait_ge(t_free, risen(t_free, l, 3))
                pe.wait_ge(ng_sig, risen(ng_sig, l, 1))
                for a in range(TT):
                    last = turn(pT[:, a * P:(a + 1) * P], hb[:, a * P:(a + 1) * P])
                last.then_inc(ng_tr, 1)
                for j in range(1, 8):
                    unit(l, U_CONV + j, 0, KD, gH, gL)
                for j in range(8):
                    unit(l, U_SGU + j, 0, KD, gH, gL)
                    if j == 6:
                        stat(l, 9, ones)
                pe.wait_ge(vn, risen(vn, l, 1))
                pe.wait_ge(t_free, risen(t_free, l, 4))
                for c in range(TT):
                    if c >= 1:
                        pe.wait_ge(sg_cp, risen(sg_cp, l, c))
                    for g in range(GROUPS):
                        last = turn(pT[:, g * P:(g + 1) * P], vG[:, g, c * P:(c + 1) * P])
                    last.then_inc(sg_tr, 1)
                    pe.wait_ge(sg_cp, risen(sg_cp, l, c + 1))
                    if c >= 1:
                        pe.wait_ge(sg_out, risen(sg_out, l, c))
                    for g in range(GROUPS):
                        last = mm(pS[:, 0, g * P:(g + 1) * P], sacc[:, g * P:(g + 1) * P],
                                  wsT[:, g, :], start=True, stop=True)
                    last.then_inc(sg_mm, 1)

                def scores(q):
                    j, c, e = scored[q]
                    bank = pA[:, 2 * (q % 2):2 * (q % 2) + 2, :]
                    if q >= 2:
                        pe.wait_ge(s_out, risen(s_out, l, q - 1))
                    if c is None:
                        for e in range(KVG):
                            h = slice(e * DH, (e + 1) * DH)
                            for c in range(TT):
                                last = mm(bank[:, e, 32 * c:32 * c + NCMP],
                                          qT[h, j, c * P:(c + 1) * P], kcn[h, 0:NCMP],
                                          start=True, stop=True)
                    else:
                        h, n = slice(e * DH, (e + 1) * DH), (c + 1) * P
                        for b in range(2):
                            last = mm(bank[:, b, 0:n], qT[h, j, c * P:(c + 1) * P], kT[h, b, 0:n],
                                      start=True, stop=True)
                    last.then_inc(s_mm, 1)

                def branch_unit(u, br, base):
                    if u % 2 == 0:
                        unit(l, u, 0, KD, gH, gL)
                    else:
                        def ready(k):
                            pe.wait_ge(br_l, risen(br_l, l, base + k + 1))
                        unit(l, u, 0, KB, lambda k: hH[:, BR[br] + k, :],
                             lambda k: hL[:, BR[br] + k, :],
                             before=ready if u % 16 == (U_B + 1) % 16 else None)

                pe.wait_ge(q_ok, risen(q_ok, l, 1))
                pe.wait_ge(sg_out, risen(sg_out, l, TT))
                for q in range(NSC):
                    scores(q)
                    if q % 2 and 0 <= q // 2 - B_LAG < 16:
                        branch_unit(U_B + q // 2 - B_LAG, "B", 0)

                def free(key):
                    n = STEP[key]
                    if n >= 2:
                        pe.wait_ge(st_out, risen(st_out, l, n - 1))
                    return pA[:, n % 2, :]

                def all_of(col, m):
                    one = identR[0:3 * HEADS, col:col + 1]
                    return bass.AP(tensor=one.tensor, offset=one.offset, ap=[one.ap[0], [0, m]])

                def step(i, kt):
                    j, e, b = item(i)
                    r = slice(e * DH, (e + 1) * DH)
                    cols = slice(kt * P, T)
                    n = T - kt * P
                    bank = free((i, kt))
                    col_ = 3 * (j + 4 * e) + b
                    mm(bank[:, 0:n], all_of(col_, P), nmH[:, cols], start=True, stop=False)
                    if b == 0:
                        m = NCMP
                        mm(bank[0:m, 0:n], kcn[r, 0:m], qT[r, j, cols], start=False, stop=False)
                        mm(bank[0:m, 0:n], identB[0:m, 0:m], maskC[0:m, :], start=False,
                           stop=False)
                    else:
                        mm(bank[:, 0:n], kT[r, b - 1, kt * P:(kt + 1) * P], qT[r, j, cols],
                           start=False, stop=False)
                        mm(bank[:, 0:P], identB[:, :], maskT[:, :], start=False, stop=False)
                    mm(bank[:, 0:n], all_of(col_, P), nmL[:, cols], start=False, stop=True)\
                        .then_inc(st_mm, 1)

                def values(i):
                    j, e, b = item(i)
                    if b == 0 and i:
                        pe.wait_ge(o_out, risen(o_out, l, i // 3))
                    pe.wait_ge(st_out, risen(st_out, l, STEP[i, 0 if b == 0 else TT - 1] + 1))
                    p0 = (i % 2) * KOFF[TT]
                    for qt in range(TT):
                        at = (qt % 2 * 3 + b) * VW
                        o = pA[:, 2 + qt // 2, at:at + VW]
                        if b == 0:
                            last = mm(o, prob[0:NCMP, p0 + qt * P:p0 + (qt + 1) * P],
                                      vcs[0:NCMP, e, :], start=True, stop=True)
                        else:
                            for kt in range(qt + 1):
                                at = p0 + KOFF[kt] + (qt - kt) * P
                                last = mm(o, prob[:, at:at + P], vt[:, kt, 2 * (b - 1) + e, :],
                                          start=(kt == 0), stop=(kt == qt))
                    last.then_inc(pv, 1)

                def pair_turned(j):
                    pe.wait_ge(o_in, risen(o_in, l, 2 * j + 2))
                    bank = free(("pair", j))
                    for c in range(TT):
                        last = turn(bank[:, c * P:(c + 1) * P], o8[:, c, :])
                    last.then_inc(st_mm, 1)

                pe.wait_ge(s_out, risen(s_out, l, NSC))
                pe.wait_ge(nm_in, risen(nm_in, l, 1))
                bank = free("nm")
                for c in range(TT):
                    last = turn(bank[0:3 * HEADS, c * P:(c + 1) * P], nmx[:, c, :])
                last.then_inc(st_mm, 1)
                pe.wait_ge(stat_in, risen(stat_in, l, 11))
                mm(free("mean"), ones[:, :], sacc[:, :], start=True, stop=True).then_inc(st_mm, 1)
                pe.wait_ge(nm_l, risen(nm_l, l, 1))
                for i in range(ITEMS):
                    for kt in range(1 if i % 3 == 0 else TT):
                        step(i, kt)
                    if i == 2:
                        bank = free("var")
                        pe.wait_ge(stat_in, risen(stat_in, l, 12))
                        mm(bank, ones[:, :], sacc[:, :], start=True, stop=True).then_inc(st_mm, 1)
                    if i in PAIR_AT:
                        pair_turned(PAIR_AT[i])
                    if 0 <= i - A_LAG < 16:
                        branch_unit(U_A + i - A_LAG, "A", 4)
                    if i:
                        values(i - 1)
                values(ITEMS - 1)
                pair_turned(PAIRS - 1)

                for m in range(8):
                    unit(l, U_CM + m, 0, KD, gH, gL)

                def c_ready(k):
                    pe.wait_ge(br_l, risen(br_l, l, 8 + k + 1))
                for m in range(8):
                    unit(l, U_CO + m, 0, KB, lambda k: hH[:, BR["C"] + k, :],
                         lambda k: hL[:, BR["C"] + k, :], before=c_ready if m == 0 else None)

                def m_ready(k):
                    pe.wait_ge(m_l, risen(m_l, l, k + 1))
                for m in range(8):
                    unit(l, U_WO + m, 0, KD, gH, gL, before=m_ready if m == 0 else None)
                for j in range(4):
                    bank = pT[:, :] if j % 2 == 0 else pS[:, 0, :]
                    pe.wait_ge(mem_sc, risen(mem_sc, l, 1))
                    if j >= 2:
                        pe.wait_ge(mem_l, risen(mem_l, l, j - 1))
                    for k in range(2):
                        for a in range(2):
                            at = (2 * k + a) * P
                            kk = 2 * j + k
                            last = turn(bank[:, at:at + P], memn[:, a, kk * P:(kk + 1) * P])
                    last.then_inc(mem_tr, 1)
                    unit(l, U_XQ + j, 0, KD, lambda k: hH[:, k, :], lambda k: hL[:, k, :],
                         before=norm_ready(l, 2) if j == 0 else None)
                    if j >= 1:
                        stat(l, 11 + j, ones)

                def x_scores(h):
                    for half in range(2):
                        n = 2 * h + half
                        if n >= 2:
                            pe.wait_ge(xs_out, risen(xs_out, l, n - 1))
                        for c in range(2):
                            at = (2 * half + c) * P
                            last = mm(pS[:, half, c * M:(c + 1) * M], qT[:, h, at:at + P],
                                      kx[:, h, :], start=True, stop=True)
                        last.then_inc(xs_mm, 1)

                def mem_ready(k):
                    pe.wait_ge(mem_l, risen(mem_l, l, k // 2 + 1))
                XSTAT = {0: 15, 1: 16, 3: 17, 5: 18}
                for h in range(8):
                    unit(l, U_XKV + h, 0, KD, lambda k: memH[:, k, :], lambda k: memL[:, k, :], n=M,
                         before=mem_ready if h == 0 else None)
                    if h in XSTAT:
                        stat(l, XSTAT[h], ones)
                    if h >= 6:
                        i = h - 6
                        pe.wait_ge(xk_ok, risen(xk_ok, l, i + 1))
                        if i == 0:
                            pe.wait_ge(mem_l, risen(mem_l, l, 4))
                        x_scores(2 * i)
                        x_scores(2 * i + 1)
                        pe.wait_ge(evac, risen(evac, l, U_XKV + 6 + 2 * i))
                        if i == 1:
                            pe.wait_ge(xv_cp, risen(xv_cp, l, 1))
                        for a in range(2):
                            for hh in range(2):
                                last = turn(pT[:, (2 * a + hh) * P:(2 * a + hh + 1) * P],
                                            tb[:, i, hh * M + a * P:hh * M + (a + 1) * P])
                        last.then_inc(xv_tr, 1)

                def x_free(key):
                    n = XSTEP[key]
                    if n >= 2:
                        pe.wait_ge(xst_out, risen(xst_out, l, n - 1))
                    return pA[:, n % 2, :]

                def x_values(h):
                    pe.wait_ge(xst_out, risen(xst_out, l, XSTEP[h, 1] + 1))
                    if h >= 1:
                        pe.wait_ge(xo_out, risen(xo_out, l, h))
                    for c in range(TT):
                        at = c % 2 * (XDH + 1)
                        for a in range(2):
                            p0 = (h % 2 * 2 + a) * T + c * P
                            last = mm(pA[:, 2 + c // 2, at:at + XDH + 1], prob[:, p0:p0 + P],
                                      vx[:, a, h, :], start=(a == 0), stop=(a == 1))
                    last.then_inc(xpv, 1)

                def x_turned(h):
                    pe.wait_ge(xo_out, risen(xo_out, l, h + 1))
                    bank = x_free(("turn", h))
                    for c in range(TT):
                        last = turn(bank[:, c * P:(c + 1) * P], o8[:, c, :])
                    last.then_inc(xst_mm, 1)

                pe.wait_ge(xs_out, risen(xs_out, l, 8))
                bank = x_free("nm")
                for c in range(TT):
                    last = turn(bank[0:3 * HEADS, c * P:(c + 1) * P], nmx[:, c, :])
                last.then_inc(xst_mm, 1)
                pe.wait_ge(xv_cp, risen(xv_cp, l, 2))
                pe.wait_ge(xnm_l, risen(xnm_l, l, 1))
                for h in range(4):
                    for a in range(2):
                        bank = x_free((h, a))
                        mm(bank, all_of(h, P), nmH[:, :], start=True, stop=False)
                        mm(bank, kx[:, h, a * P:(a + 1) * P], qT[:, h, :], start=False, stop=False)
                        mm(bank, all_of(h, P), nmL[:, :], start=False, stop=True)\
                            .then_inc(xst_mm, 1)
                    if h >= 2:
                        x_turned(h - 2)
                    if h >= 1:
                        x_values(h - 1)
                x_turned(2)
                x_values(3)
                x_turned(3)

                def xo_ready(k):
                    pe.wait_ge(xo_l, risen(xo_l, l, k + 1))
                for m in range(8):
                    unit(l, U_XO + m, 0, 4, lambda k: hH[:, k, :], lambda k: hL[:, k, :],
                         before=xo_ready if m == 0 else None)
                ffn(l, U_F2, 1, 3, 19)

            pe.wait_ge(evac, risen(evac, L, 0))
            for a in range(TT):
                for hf in range(2):
                    n = 2 * a + hf
                    if n >= 4:
                        pe.wait_ge(fin_cp, n - 3)
                    for k in range(4):
                        last = turn(pg[:, n % 4, k * P:(k + 1) * P],
                                    xT[:, 4 * hf + k, a * P:(a + 1) * P])
                    last.then_inc(fin_tr, 1)

        @block.scalar
        def _(act):
            made = [0]

            def copy(o, i, **kw):
                return act.activation(o, i, ACT.Copy, **kw)

            def split(l, u, i=0):
                s = u % 2
                act.wait_ge(landed[s], risen(landed[s], l, 32 * (u // 2 + 1) + 64 * i))
                act.wait_ge(unit_mm, risen(unit_mm, l, u - 3 + 4 * i))
                copy(wH[:, u % 4, :, :], raw[:, s, :, :]).then_inc(split_h, 1)

            def ahead(l, u, i=0):
                if u + 3 < U:
                    assert made[0] == u + 3
                    made[0] += 1
                    split(l, u + 3, i)

            def norm(l, n, gain, dst, u0):
                for k in range(KD):
                    if u0 is not None:
                        ahead(l, u0 + k)
                    act.wait_ge(evac, risen(evac, l, 0 if u0 is None else u0 + k + 1))
                    copy(dst[:, k, :], xT[:, k, :], scale=col(gain + k)).then_inc(gx_h, 1)
                    act.wait_ge(sq_used, risen(sq_used, l, KD * n + k - 1))
                    act.activation(sq[:, k % 2, :], xT[:, k, :], ACT.Square).then_inc(sq_done, 1)

            def root(l, s, dst, scale, n=T):
                act.wait_ge(stat_mm, risen(stat_mm, l, s + 1 if s < 10 else s - 1))
                act.activation(dst[:, 0:n], pO[:, 0:n], ACT.Sqrt, bias=eps[:, 0:1],
                               scale=scale).then_inc(stat_rt, 1)

            def ffn(l, u, last_norm):
                for ch, n in enumerate(CH):
                    start = made[0]
                    with act.Fori(0, n // 2) as i:
                        for c in range(2):
                            ahead(l, u + 2 * c, i)
                            act.wait_ge(evac, risen(evac, l, u + 2 * c + 1 + 4 * i))
                            act.activation(sil, tb[:, 0, :], ACT.Silu).then_inc(silu, 1)
                            ahead(l, u + 2 * c + 1, i)
                            act.wait_ge(evac, risen(evac, l, u + 2 * c + 2 + 4 * i))
                            copy(hH[:, bass.ds(i * 2 + c, 1), :].rearrange("p a t -> p (a t)"),
                                 hb).then_inc(hid_h, 1)
                    made[0] = start + 2 * n
                    u += 2 * n
                    if ch == len(CH) - 1 and last_norm:
                        norm(l, *last_norm, u)
                    else:
                        for m in range(KD):
                            ahead(l, u + m)
                    u += KD

            act.wait_ge(consts, 1)
            with act.Fori(0, L) as l:
                for u in range(3):
                    split(l, u)
                made[0] = 3
                act.wait_ge(par_in, risen(par_in, l, 1))
                norm(l, 0, G_F1, gxH, None)
                root(l, 0, rstd, 1.0 / D)
                ffn(l, 0, (1, G_MIX, gxH))

                ahead(l, U_KV)
                ahead(l, U_KV + 1)
                root(l, 1, rstd, 1.0 / D)
                ahead(l, U_KV + 2)
                ahead(l, U_KV + 3)
                root(l, 2, rv, 1.0 / DH)
                act.wait_ge(cmp1, risen(cmp1, l, 1))
                act.activation(hc[:, :, 0:NCMP],
                               pS[:, 0, 0:64].rearrange("p (i n) -> p i n", i=2)[:, :, 0:NCMP],
                               ACT.Silu).then_inc(cmp_act, 1)
                ahead(l, U_KV + 4)
                ahead(l, U_KV + 5)
                root(l, 3, rv, 1.0 / DH)
                ahead(l, U_QP)
                root(l, 4, rv, 1.0 / DH, NCMP)
                for j in range(1, PAIRS):
                    ahead(l, U_QP + j)
                    root(l, 5 + j - 1, rv, 1.0 / DH)
                ahead(l, U_NG)
                root(l, 8, rv, 1.0 / DH)
                ahead(l, U_NG + 1)
                act.wait_ge(ng_in, risen(ng_in, l, 1))
                act.activation(hb, sr, ACT.Sigmoid).then_inc(ng_sig, 1)
                for j in range(4):
                    ahead(l, U_CONV + 2 * j)
                    ahead(l, U_CONV + 2 * j + 1)
                    act.wait_ge(evac, risen(evac, l, U_CONV + 2 * j + 2))
                    act.activation(sil, tb[:, 1, :], ACT.Sigmoid).then_inc(conv_sig, 1)
                for j in range(8):
                    ahead(l, U_SGU + j)
                    act.wait_ge(evac, risen(evac, l, U_SGU + j + 1))
                    dst = vG[:, j, :] if j < 4 else uG[:, j - 4, :]
                    act.activation(dst, tb[:, j % 2, :], ACT.Gelu_apprx_tanh).then_inc(gelu, 1)
                root(l, 9, rv, 1.0 / DS)
                act.wait_ge(sg_out, risen(sg_out, l, TT))
                for k in range(KB):
                    copy(hH[:, BR["B"] + k, :], uG[:, k, :]).then_inc(br_h, 1)

                def merge_gate(u):
                    act.wait_ge(evac, risen(evac, l, u + 1))
                    act.activation(sr, tb[:, 0, :], ACT.Sigmoid).then_inc(mg_sig, 1)

                for m in range(16):
                    ahead(l, U_B + m)
                    if m % 2 == 0:
                        merge_gate(U_B + m)

                def taken(key):
                    act.wait_ge(st_mm, risen(st_mm, l, STEP[key] + 1))
                    return pA[:, STEP[key] % 2, :]

                def pair_out(j):
                    bank = taken(("pair", j))
                    copy(qT[:, j, :], bank)
                    copy(hH[:, BR["C"] + j, :], bank).then_inc(st_out, 1)

                copy(nmH[:, :], taken("nm")[0:3 * HEADS, :]).then_inc(st_out, 1)
                copy(sil, taken("mean"), scale=-1.0 / DC).then_inc(st_out, 1)
                for i in range(ITEMS):
                    j, e, b = item(i)
                    p0 = (i % 2) * KOFF[TT]
                    if i >= 2:
                        act.wait_ge(pv, risen(pv, l, i - 1))
                    for kt in range(1 if b == 0 else TT):
                        bank = taken((i, kt))
                        if b == 0:
                            act.activation(prob[0:NCMP, p0:p0 + T], bank[0:NCMP, :], ACT.Exp,
                                           bias=cbias[0:NCMP, j + 4 * e:j + 4 * e + 1])\
                                               .then_inc(st_out, 1)
                        else:
                            n = T - kt * P
                            at = p0 + KOFF[kt]
                            act.activation(prob[:, at:at + n], bank[:, 0:n], ACT.Exp,
                                           bias=kbias[:, j + 4 * e, kt:kt + 1]).then_inc(st_out, 1)
                    if i == 2:
                        act.activation(rv[:, :], taken("var"), ACT.Sqrt, bias=eps[:, 0:1],
                                       scale=1.0 / DC).then_inc(st_out, 1)
                    if i == 3:
                        for k in range(KB):
                            act.wait_ge(ln_sc, risen(ln_sc, l, k + 1))
                            act.activation(cacc[:, k, :], cacc[:, k, :], ACT.Silu,
                                           bias=col(P_LB + k), scale=col(P_LG + k))
                        act.drain()
                        for k in range(KB):
                            copy(hH[:, BR["A"] + k, :], cacc[:, k, :]).then_inc(br_h, 1)
                    if i in PAIR_AT:
                        pair_out(PAIR_AT[i])
                    if 0 <= i - A_LAG < 16:
                        ahead(l, U_A + i - A_LAG)
                        if (i - A_LAG) % 2 == 0:
                            merge_gate(U_A + i - A_LAG)
                pair_out(PAIRS - 1)
                for m in range(8):
                    ahead(l, U_CM + m)
                    act.wait_ge(evac, risen(evac, l, U_CM + m + 1))
                    act.activation(gC[:, m, :], tb[:, m % 2, :], ACT.Sigmoid).then_inc(mg_sig, 1)
                act.wait_ge(memld, risen(memld, l, 16))
                for a in range(2):
                    act.activation(tmp3[:, 0:2, :].rearrange("p a t -> p (a t)"), memn[:, a, :],
                                   ACT.Square, accum_out=mst[:, a:a + 1])
                    act.drain()
                act.activation(mst[:, :], mst[:, :], ACT.Sqrt, bias=eps[:, 0:1],
                               scale=1.0 / D).then_inc(mem_st, 1)
                for m in range(8):
                    ahead(l, U_CO + m)
                    act.wait_ge(m_in, risen(m_in, l, m + 1))
                    copy(gxH[:, m, :], mrg[:, m, :]).then_inc(m_h, 1)
                norm(l, 2, G_X, hH, U_WO)
                for j in range(4):
                    ahead(l, U_XQ + j)
                    if j == 0:
                        act.wait_ge(unit_mm, risen(unit_mm, l, U_WO + 8))
                    bank = pT[:, :] if j % 2 == 0 else pS[:, 0, :]
                    act.wait_ge(mem_tr, risen(mem_tr, l, j + 1))
                    for k in range(2):
                        kk = 2 * j + k
                        last = copy(memH[:, kk, :], bank[:, k * M:(k + 1) * M],
                                    scale=col(G_MEM + kk))
                    last.then_inc(mem_h, 1)
                    if j >= 1:
                        root(l, 11 + j, rstd if j == 1 else rv, 1.0 / (D if j == 1 else XDH))
                for h in range(8):
                    ahead(l, U_XKV + h)
                    if h in (0, 1, 3, 5):
                        root(l, {0: 15, 1: 16, 3: 17, 5: 18}[h], rv, 1.0 / XDH)

                def x_taken(key):
                    act.wait_ge(xst_mm, risen(xst_mm, l, XSTEP[key] + 1))
                    return pA[:, XSTEP[key] % 2, :]

                def x_out(h):
                    bank = x_taken(("turn", h))
                    copy(qT[:, h, :], bank)
                    copy(hH[:, h, :], bank).then_inc(xst_out, 1)

                copy(nmH[:, :], x_taken("nm")[0:3 * HEADS, :]).then_inc(xst_out, 1)
                for h in range(4):
                    if h >= 2:
                        act.wait_ge(xpv, risen(xpv, l, h - 1))
                    for a in range(2):
                        p0 = (h % 2 * 2 + a) * T
                        act.activation(prob[:, p0:p0 + T], x_taken((h, a)), ACT.Exp)\
                            .then_inc(xst_out, 1)
                    if h >= 2:
                        x_out(h - 2)
                x_out(2)
                x_out(3)
                norm(l, 3, G_F2, gxH, U_XO)
                root(l, 19, rstd, 1.0 / D)
                ffn(l, U_F2, None)

        @block.vector
        def _(dve):
            TTt, TS, STT = dve.tensor_tensor, dve.tensor_scalar, dve.scalar_tensor_tensor

            def ready(l, u, i=0):
                dve.wait_ge(unit_mm, risen(unit_mm, l, u + 1 + 4 * i))
                return pg[:, u % 4, :]

            def scaled(dst, l, u, by=None):
                bank = ready(l, u)
                return TTt(dst, bank, rstd[:, :] if by is None else by, ALU.mult).then_inc(evac, 1)

            def stat_given(s):
                dve.drain().then_inc(stat_in, 1)

            def root_of(l, s, dst, n=T):
                dve.wait_ge(stat_rt, risen(stat_rt, l, s + 1 if s < 10 else s - 1))
                dve.reciprocal(dst[:, 0:n], dst[:, 0:n])
                dve.drain()

            def norm(l, n, dH, dL, gain, update):
                def tail(k):
                    dve.wait_ge(gx_h, risen(gx_h, l, KD * n + k + 1))
                    STT(dL[:, k, :], xT[:, k, :], col(gain + k), dH[:, k, :].bitcast(F32),
                        ALU.mult, ALU.subtract).then_inc(gx_l, 1)
                    if k:
                        dve.drain()
                    dve.wait_ge(sq_done, risen(sq_done, l, KD * n + k + 1))
                    if k == 0:
                        dve.tensor_copy(sacc[:, :], sq[:, 0, :]).then_inc(sq_used, 1)
                    else:
                        TTt(sacc[:, :], sacc[:, :], sq[:, k % 2, :], ALU.add).then_inc(sq_used, 1)
                for k in range(KD):
                    if update:
                        update(k)
                    if k >= 1:
                        tail(k - 1)
                tail(KD - 1)
                stat_given(None)

            def residual(l, u, by):
                def update(k):
                    bank = ready(l, u + k)
                    STT(xT[:, k, :], bank, by, xT[:, k, :], ALU.mult, ALU.add).then_inc(evac, 1)
                return update

            def ffn(l, u, f, last_norm):
                ft = 0
                for ch, n in enumerate(CH):
                    with dve.Fori(0, n // 2) as i:
                        for c in range(2):
                            hid = f * FT + ft + c + 1 + 2 * i
                            bank = ready(l, u + 2 * c, i)
                            TTt(tb[:, 0, :], bank, rstd[:, :], ALU.mult).then_inc(evac, 1)
                            dve.wait_ge(silu, risen(silu, l, hid))
                            TTt(sr, sil, rstd[:, :], ALU.mult)
                            dve.drain()
                            bank = ready(l, u + 2 * c + 1, i)
                            TTt(hb, bank, sr, ALU.mult).then_inc(evac, 1)
                            dve.wait_ge(hid_h, risen(hid_h, l, hid))
                            slot = bass.ds(i * 2 + c, 1)
                            flat = "p a t -> p (a t)"
                            TTt(hL[:, slot, :].rearrange(flat), hb,
                                hH[:, slot, :].rearrange(flat).bitcast(F32),
                                ALU.subtract).then_inc(hid_l, 1)
                    u += 2 * n
                    if ch == len(CH) - 1 and last_norm:
                        norm(l, *last_norm, residual(l, u, 0.5))
                    else:
                        for m in range(KD):
                            residual(l, u, 0.5)(m)
                    u += KD
                    ft += n

            dve.wait_ge(pro_tr, 1)
            for l in range(L):
                dve.tensor_copy(pall[:, l, 0:NP_ROWS], pT[:, l * P:l * P + NP_ROWS])
                dve.tensor_copy(pall[:, l, NP_ROWS:NPAR],
                                pT[:, (2 + l) * P:(2 + l) * P + 4 * CONV_W])
            dve.drain().then_inc(pro_cp, 1)
            for k in range(KD):
                dve.wait_ge(pro_tr, k + 2)
                dve.tensor_copy(xT[:, k, :], pg[:, k % 4, :]).then_inc(pro_cp, 1)
            dve.wait_ge(consts, 1)
            dve.tensor_copy(identB[:, :], ident[:, :])
            dve.tensor_copy(identR[0:3 * HEADS, :], ident[0:3 * HEADS, 0:3 * HEADS])
            dve.tensor_copy(maskT[:, :], tb[:, 0, 0:P])
            dve.tensor_copy(maskC[:, :], tb[0:32, 1, :])
            for h in range(HEADS):
                TS(kbias[:, h, :], pos[:, :], slope[h], None, ALU.mult)
                TS(cbias[:, h:h + 1], cend[:, :], slope[h], None, ALU.mult)
                for b in range(3):
                    TS(qbias[:, :, h, b], pos[:, :], -slope[h], None, ALU.mult)
            dve.drain().then_inc(evac, risen(evac, 0, 0))
            dve.sem_inc(sq_used, risen(sq_used, 0, 0))

            with dve.Fori(0, L) as l:
                dve.tensor_copy(par[:, :], pall[:, bass.ds(l, 1), :]
                                .rearrange("p a c -> p (a c)")).then_inc(par_in, 1)
                dve.drain()
                TS(g8[:, 0:1], col(P_NQ), float(DH) ** -0.5, None, ALU.mult)
                TS(g8[:, 1:2], col(P_XQ), float(XDH) ** -0.5, None, ALU.mult)
                norm(l, 0, gxH, gxL, G_F1, None)
                root_of(l, 0, rstd)
                ffn(l, 0, 0, (1, gxH, gxL, G_MIX))

                root_of(l, 1, rstd)
                scaled(kvc[:, 0, :], l, U_KV)
                scaled(kvc[:, 1, :], l, U_KV + 1)
                dve.drain()
                for i in range(2):
                    src = kvc[:, i, :]
                    src = bass.AP(tensor=src.tensor, offset=src.offset,
                                  ap=[src.ap[0], [1, CMP_LEN], [CMP_STRIDE, NCMP]])
                    pe_ = par[:, P_PE + i * CMP_LEN:P_PE + (i + 1) * CMP_LEN]
                    pe_ = bass.AP(tensor=pe_.tensor, offset=pe_.offset,
                                  ap=[pe_.ap[0], [1, CMP_LEN], [0, NCMP]])
                    last = TTt(blk[i], src, pe_, ALU.add)
                last.then_inc(blk_in, 1)

                def squares(src, n=T):
                    dve.drain()
                    TTt(sacc[:, 0:n], src, src, ALU.mult)
                    stat_given(None)

                def normed(l, s, x_, g, n=T):
                    root_of(l, s, rv, n)
                    return STT(x_, x_, g, rv[:, 0:n], ALU.mult, ALU.mult)

                scaled(kT[:, 0, :], l, U_KV + 2)
                squares(kT[:, 0, :])
                dve.wait_ge(ws_tr, risen(ws_tr, l, 1))
                TTt(wsT[:, :, :], pT[:, :].rearrange("p (g t) -> p g t", g=4),
                    bass.AP(tensor=tri[:, :].tensor, offset=tri[:, :].offset,
                            ap=[tri[:, :].ap[0], [0, 4], [1, P]]), ALU.mult).then_inc(t_free, 1)
                scaled(tb[:, 0, :], l, U_KV + 3)
                normed(l, 2, kT[:, 0, :], col(P_NK + 1))
                dve.wait_ge(v_tr, risen(v_tr, l, 1))
                dve.tensor_copy(vt[:, :, 0:2, 0:DH],
                                pT.rearrange("p (a g c) -> p a g c", a=4, g=2)).then_inc(t_free, 1)
                dve.memset(vt[:, :, :, DH:VW], 1.0)
                scaled(kT[:, 1, :], l, U_KV + 4)
                squares(kT[:, 1, :])
                dve.wait_ge(cmp2, risen(cmp2, l, 1))
                dve.tensor_copy(kcn[:, 0:NCMP], pS[:, 1, 0:NCMP])
                for g in range(KVG):
                    dve.tensor_copy(vcs[0:NCMP, g, 0:DH], pS[0:NCMP, 1 - g, P:P + DH])
                scaled(tb[:, 1, :], l, U_KV + 5)
                normed(l, 3, kT[:, 1, :], col(P_NK + 2))
                squares(kcn[:, 0:NCMP], NCMP)

                scaled(qT[:, 0, :], l, U_QP)
                normed(l, 4, kcn[:, 0:NCMP], col(P_NK), NCMP)
                squares(qT[:, 0, :])
                dve.wait_ge(v_tr, risen(v_tr, l, 2))
                dve.tensor_copy(vt[:, :, 2:4, 0:DH],
                                pT.rearrange("p (a g c) -> p a g c", a=4, g=2)).then_inc(t_free, 1)
                for j in range(1, PAIRS):
                    scaled(qT[:, j, :], l, U_QP + j)
                    normed(l, 4 + j, qT[:, j - 1, :], g8[:, 0:1])
                    squares(qT[:, j, :])
                NG = 3 * HEADS
                scaled(hb, l, U_NG)
                normed(l, 8, qT[:, PAIRS - 1, :], g8[:, 0:1])
                scaled(sr, l, U_NG + 1)
                dve.drain()
                TTt(sr, sr, hb, ALU.add).then_inc(ng_in, 1)

                dve.memset(cin[:, :, 0:CONV_W - 1], 0.0)
                for j in range(4):
                    scaled(tb[:, 0, :], l, U_CONV + 2 * j)
                    if j == 0:
                        dve.wait_ge(ng_tr, risen(ng_tr, l, 1))
                        dve.tensor_copy(gates[:, :, :], pT[:, :].rearrange("p (a c) -> p a c", a=4)
                                        [:, :, 0:NG])
                        dve.drain()
                        cmp0 = gates[:, 0, 0:NG:3]
                        TS(cmp0, cmp0, valid[:, 0:1], None, ALU.mult).then_inc(t_free, 1)
                    scaled(tb[:, 1, :], l, U_CONV + 2 * j + 1)
                    dve.wait_ge(conv_sig, risen(conv_sig, l, j + 1))
                    TTt(cin[:, j, CONV_W - 1:TP], tb[:, 0, :], sil, ALU.mult)
                    dve.drain()

                def conv_tap(k):
                    for j in range(4):
                        w, o = col(P_CW + j * CONV_W + k), cacc[:, j, :]
                        if k == 0:
                            TS(o, cin[:, j, 0:T], w, col(P_CB + j), ALU.mult, ALU.add)
                        else:
                            STT(o, cin[:, j, k:k + T], w, o, ALU.mult, ALU.add)
                    dve.drain()

                tap = 0
                for j in range(8):
                    if j >= 2:
                        dve.wait_ge(gelu, risen(gelu, l, j - 1))
                    scaled(tb[:, j % 2, :], l, U_SGU + j)
                    if j == 5:
                        for k in range(4):
                            dve.wait_ge(gelu, risen(gelu, l, k + 1))
                            TTt(sacc[:, :] if k == 0 else hb, vG[:, k, :], vG[:, k, :], ALU.mult)
                            dve.drain()
                            if k:
                                TTt(sacc[:, :], sacc[:, :], hb, ALU.add)
                                dve.drain()
                        stat_given(None)
                    else:
                        for _ in range(3 if j == 0 else 2):
                            if tap < CONV_W - 16:
                                conv_tap(tap)
                                tap += 1
                root_of(l, 9, rv)
                for k in range(4):
                    STT(vG[:, k, :], vG[:, k, :], col(P_SG + k), rv[:, :], ALU.mult, ALU.mult)
                dve.drain().then_inc(vn, 1)
                dve.wait_ge(gelu, risen(gelu, l, 8))
                for c in range(TT):
                    dve.wait_ge(sg_tr, risen(sg_tr, l, c + 1))
                    dve.tensor_copy(sacc[:, :], pT[:, :]).then_inc(sg_cp, 1)
                    dve.wait_ge(sg_mm, risen(sg_mm, l, c + 1))
                    TTt(hb, pS[:, 0, :], bbc[:, :, :].rearrange("p g t -> p (g t)"), ALU.add)
                    dve.drain()
                    uc = uG[:, :, c * P:(c + 1) * P]
                    TTt(uc, uc, hb.rearrange("p (g t) -> p g t", g=4), ALU.mult).then_inc(sg_out, 1)
                dve.drain().then_inc(q_ok, 1)
                for k in range(KB):
                    dve.wait_ge(br_h, risen(br_h, l, k + 1))
                    TTt(hL[:, BR["B"] + k, :], uG[:, k, :],
                        hH[:, BR["B"] + k, :].bitcast(F32), ALU.subtract).then_inc(br_l, 1)

                def unit_max(q):
                    j, c, e = scored[q]
                    bank = pA[:, 2 * (q % 2):2 * (q % 2) + 2, :]
                    dve.wait_ge(s_mm, risen(s_mm, l, q + 1))
                    if c is None:
                        for e in range(KVG):
                            src = bank[:, e, 0:P].rearrange("p (c n) -> p c n", c=4)
                            last = STT(cs[:, 4 * e:4 * e + 4, :], tabc[:, :, :], slope[j + 4 * e],
                                       src[:, :, 0:NCMP], ALU.mult, ALU.add)
                        last.then_inc(s_out, 1)
                        dve.drain()
                        for e in range(KVG):
                            dve.tensor_reduce(nmx[:, :, 3 * (j + 4 * e)],
                                              cs[:, 4 * e:4 * e + 4, :], AX_X, ALU.max,
                                              negate=True)
                        return
                    n, h = (c + 1) * P, j + 4 * e
                    t = tab[:, T - n:T]
                    t = bass.AP(tensor=t.tensor, offset=t.offset, ap=[t.ap[0], [0, 2], [1, n]])
                    a = att[:, q % 2, :, 0:n]
                    STT(a, t, slope[h], bank[:, :, 0:n], ALU.mult, ALU.add).then_inc(s_out, 1)
                    dve.drain()
                    dve.tensor_reduce(nmx[:, c, 3 * h + 1:3 * h + 3], a, AX_X, ALU.max,
                                      negate=True)

                def branch_unit(u, add):
                    if u % 2 == 0:
                        scaled(tb[:, 0, :], l, u)
                        return
                    m = (u - U_B) % 16 // 2
                    dve.wait_ge(mg_sig, risen(mg_sig, l, (u - U_B) // 2 + 1))
                    if add:
                        scaled(hb, l, u, by=sr)
                        dve.drain()
                        TTt(mrg[:, m, :], mrg[:, m, :], hb, ALU.add)
                    else:
                        scaled(mrg[:, m, :], l, u, by=sr)

                for q in range(NSC):
                    unit_max(q)
                    if q % 2 and 0 <= q // 2 - B_LAG < 16:
                        branch_unit(U_B + q // 2 - B_LAG, False)
                    if q % 2 == 0 and tap < CONV_W:
                        conv_tap(tap)
                        tap += 1
                assert tap == CONV_W
                dve.drain()
                TTt(nmx[:, :, :], nmx[:, :, :],
                    qbias[:, :, :, :].rearrange("p c h b -> p c (h b)"), ALU.add).then_inc(nm_in, 1)

                TTt(sacc[:, :], cacc[:, 0, :], cacc[:, 1, :], ALU.add)
                dve.drain()
                for k in (2, 3):
                    TTt(sacc[:, :], sacc[:, :], cacc[:, k, :], ALU.add)
                    dve.drain()
                stat_given(None)
                dve.wait_ge(st_out, risen(st_out, l, STEP["nm"] + 1))
                TTt(nmL[:, :], pA[0:3 * HEADS, STEP["nm"] % 2, :], nmH[:, :].bitcast(F32),
                    ALU.subtract).then_inc(nm_l, 1)
                dve.wait_ge(st_out, risen(st_out, l, STEP["mean"] + 1))
                for k in range(KB):
                    TTt(cacc[:, k, :], cacc[:, k, :], sil, ALU.add)
                dve.drain()
                for k in range(KB):
                    TTt(sacc[:, :] if k == 0 else hb, cacc[:, k, :], cacc[:, k, :], ALU.mult)
                    dve.drain()
                    if k:
                        TTt(sacc[:, :], sacc[:, :], hb, ALU.add)
                        dve.drain()
                stat_given(None)
                dve.wait_ge(st_out, risen(st_out, l, STEP["var"] + 1))
                dve.reciprocal(rv[:, :], rv[:, :])
                dve.drain()
                for k in range(KB):
                    TTt(cacc[:, k, :], cacc[:, k, :], rv[:, :], ALU.mult).then_inc(ln_sc, 1)

                def outputs(n):
                    j, e = n // 2, n % 2
                    h = j + 4 * e
                    dve.wait_ge(pv, risen(pv, l, 3 * n + 3))
                    banks = pA[:, 2:4, 0:6 * VW].rearrange("p a (m c) -> p a m c", m=6)
                    TS(ow[:, :, :], banks[:, :, :, DH], 1e-30, None, ALU.max)
                    dve.drain()
                    dve.reciprocal(ow[:, :, :], ow[:, :, :])
                    dve.drain()
                    w = ow[:, :, :].rearrange("p a m -> p (a m)")
                    w4 = w.rearrange("p (c b) -> p c b", c=TT)
                    TTt(w4, w4, gates[:, :, 3 * h:3 * h + 3], ALU.mult)
                    dve.drain()
                    prod = oprod.rearrange("p (a m c) -> p a m c", a=2, m=6)
                    w = bass.AP(tensor=w.tensor, offset=w.offset,
                                ap=[w.ap[0], [6, 2], [1, 6], [0, DH]])
                    TTt(prod, banks[:, :, :, 0:DH], w, ALU.mult).then_inc(o_out, 1)
                    dve.drain()
                    if e == 0 and j >= 1:
                        dve.wait_ge(st_mm, risen(st_mm, l, STEP["pair", j - 1] + 1))
                    dve.tensor_reduce(o8[:, :, e * DH:(e + 1) * DH],
                                      oprod.rearrange("p (c b d) -> p c d b", c=TT, b=3),
                                      AX_X, ALU.add).then_inc(o_in, 1)

                def pair_low(j):
                    dve.wait_ge(st_out, risen(st_out, l, STEP["pair", j] + 1))
                    TTt(hL[:, BR["C"] + j, :], qT[:, j, :],
                        hH[:, BR["C"] + j, :].bitcast(F32), ALU.subtract).then_inc(br_l, 1)

                for i in range(3, ITEMS + 1):
                    if 0 <= i - A_LAG < 16:
                        branch_unit(U_A + i - A_LAG, True)
                    if i % 3 == 0:
                        outputs(i // 3 - 1)
                    if i == 3:
                        for k in range(KB):
                            dve.wait_ge(br_h, risen(br_h, l, 4 + k + 1))
                            TTt(hL[:, BR["A"] + k, :], cacc[:, k, :],
                                hH[:, BR["A"] + k, :].bitcast(F32), ALU.subtract).then_inc(br_l, 1)
                    if i - 1 in PAIR_AT:
                        pair_low(PAIR_AT[i - 1])
                pair_low(PAIRS - 1)

                for m in range(8):
                    if m >= 2:
                        dve.wait_ge(mg_sig, risen(mg_sig, l, 16 + m - 1))
                    scaled(tb[:, m % 2, :], l, U_CM + m)

                def merged_low(m):
                    dve.wait_ge(m_h, risen(m_h, l, m + 1))
                    TTt(gxL[:, m, :], mrg[:, m, :], gxH[:, m, :].bitcast(F32), ALU.subtract)\
                        .then_inc(m_l, 1)

                def memory_low(i):
                    bank = pT[:, :] if i % 2 == 0 else pS[:, 0, :]
                    dve.wait_ge(mem_h, risen(mem_h, l, i + 1))
                    for k in range(2):
                        kk = 2 * i + k
                        last = STT(memL[:, kk, :], bank[:, k * M:(k + 1) * M], col(G_MEM + kk),
                                   memH[:, kk, :].bitcast(F32), ALU.mult, ALU.subtract)
                    last.then_inc(mem_l, 1)

                dve.wait_ge(mg_sig, risen(mg_sig, l, 24))
                for m in range(8):
                    part = tb[:, m % 2, :]
                    scaled(part, l, U_CO + m, by=gC[:, m, :])
                    dve.drain()
                    TTt(mrg[:, m, :], mrg[:, m, :], part, ALU.add).then_inc(m_in, 1)
                    if m >= 1:
                        merged_low(m - 1)
                    if m == 2:
                        dve.wait_ge(mem_st, risen(mem_st, l, 1))
                        dve.reciprocal(mst[:, :], mst[:, :])
                        dve.drain()
                        for a in range(2):
                            last = TS(memn[:, a, :], memn[:, a, :], mst[:, a:a + 1], None, ALU.mult)
                        last.then_inc(mem_sc, 1)
                merged_low(7)

                norm(l, 2, hH, hL, G_X, residual(l, U_WO, 1.0))
                root_of(l, 12, rstd)
                for j in range(4):
                    scaled(qT[:, j, :], l, U_XQ + j)
                    memory_low(j)
                    if j:
                        normed(l, 12 + j, qT[:, j - 1, :], g8[:, 1:2])
                    squares(qT[:, j, :])

                def x_max(h):
                    for half in range(2):
                        dve.wait_ge(xs_mm, risen(xs_mm, l, 2 * h + half + 1))
                        dve.tensor_reduce(nmx[:, 2 * half:2 * half + 2, h],
                                          pS[:, half, :].rearrange("p (c m) -> p c m", c=2),
                                          AX_X, ALU.max, negate=True).then_inc(xs_out, 1)

                for h in range(8):
                    bank = ready(l, U_XKV + h)
                    dst = kx[:, h, :] if h < 4 else tb[:, (h - 4) // 2,
                                                       ((h - 4) % 2) * M:((h - 4) % 2 + 1) * M]
                    dve.tensor_copy(dst, bank[:, 0:M]).then_inc(evac, 1)
                    if h == 1:
                        normed(l, 16, qT[:, 3, :], g8[:, 1:2])
                        squares(kT[:, 0, :])
                    if h in (3, 5):
                        normed(l, 17 + (h == 5), kT[:, (h == 5) * 1, :], col(P_XK))
                        dve.drain().then_inc(xk_ok, 1)
                    if h == 3:
                        squares(kT[:, 1, :])
                    if h == 4:
                        dve.memset(vx[:, :, :, XDH:XDH + 1], 1.0)
                    if h >= 6:
                        x_max(2 * (h - 6))
                        x_max(2 * (h - 6) + 1)
                        i = h - 6
                        dve.wait_ge(xv_tr, risen(xv_tr, l, i + 1))
                        dve.tensor_copy(vx[:, :, 2 * i:2 * i + 2, 0:XDH],
                                        pT.rearrange("p (a h c) -> p a h c", a=2, h=2))\
                                            .then_inc(xv_cp, 1)

                dve.wait_ge(xst_out, risen(xst_out, l, XSTEP["nm"] + 1))
                TTt(nmL[:, :], pA[0:3 * HEADS, XSTEP["nm"] % 2, :], nmH[:, :].bitcast(F32),
                    ALU.subtract).then_inc(xnm_l, 1)

                def x_low(h):
                    dve.wait_ge(xst_out, risen(xst_out, l, XSTEP["turn", h] + 1))
                    TTt(hL[:, h, :], qT[:, h, :], hH[:, h, :].bitcast(F32), ALU.subtract)\
                        .then_inc(xo_l, 1)

                for h in range(4):
                    dve.wait_ge(xpv, risen(xpv, l, h + 1))
                    banks = pA[:, 2:4, 0:2 * (XDH + 1)].rearrange("p a (m c) -> p a m c", m=2)
                    w = ow[:, :, 0:2]
                    dve.reciprocal(w, banks[:, :, :, XDH])
                    dve.drain()
                    w = bass.AP(tensor=w.tensor, offset=w.offset,
                                ap=[w.ap[0], [6, 2], [1, 2], [0, XDH]])
                    TTt(o8[:, :, :].rearrange("p (a m) c -> p a m c", a=2),
                        banks[:, :, :, 0:XDH], w, ALU.mult).then_inc(xo_out, 1)
                    if h >= 1:
                        x_low(h - 1)
                x_low(3)
                norm(l, 3, gxH, gxL, G_F2, residual(l, U_XO, 1.0))
                root_of(l, 19, rstd)
                ffn(l, U_F2, 1, None)
                dve.drain()

            for n in range(2 * TT):
                a, hf = divmod(n, 2)
                dve.wait_ge(fin_tr, n + 1)
                dve.tensor_copy(xnat[:, a, hf * T:(hf + 1) * T], pg[:, n % 4, :])\
                   .then_inc(fin_cp, 1)


_INS = ['x', 'mem', 'norm_ffn1', 'ffn1_wi', 'ffn1_wo', 'norm_mix', 'w_in', 'conv_w', 'conv_b',
        'conv_ln_g', 'conv_ln_b', 'conv_out', 'sgu_norm', 'sgu_ws', 'sgu_b', 'sgu_out',
        'nsa_q_norm', 'nsa_k_norm', 'cmp_pe', 'cmp_w1', 'cmp_w2', 'nsa_out', 'w_out', 'norm_xattn',
        'mem_norm', 'xq', 'xkv', 'xq_norm', 'xk_norm', 'xo', 'norm_ffn2', 'ffn2_wi', 'ffn2_wo']


def kernel(**inputs):
    import numpy as np
    import concourse.bacc as bacc
    from concourse.bass_utils import run_bass_kernel_spmd

    nc = bacc.Bacc("TRN2", target_bir_lowering=False, num_devices=1,
                   dynamic_dma_scratch_size=1024)
    arrays, args = {}, []
    for name in _INS:
        a = np.ascontiguousarray(inputs[name])
        arrays[f"in_{name}"] = a
        args.append(nc.dram_tensor(f"in_{name}", a.shape, mybir.dt.from_np(a.dtype),
                                   kind="ExternalInput").ap())
    shape = arrays["in_x"].shape
    args.append(nc.dram_tensor("out_y", shape, F32, kind="ExternalOutput").ap())
    trunk(nc, *args)
    r = run_bass_kernel_spmd(nc, [arrays], core_ids=[0])
    return r.results[0]["out_y"]
```

```python
from contextlib import ExitStack

import concourse.bass as bass
from concourse import mybir

F32 = mybir.dt.float32
F32R = mybir.dt.float32r
BF16 = mybir.dt.bfloat16
ALU = mybir.AluOpType
ACT = mybir.ActivationFunctionType
AX_X = mybir.AxisListType.X

P = 128
EPS = 1e-6
NEG = -1e30


def trunk(nc, x, mem, norm_ffn1, ffn1_wi, ffn1_wo, norm_mix, w_in, conv_w, conv_b, conv_ln_g,
          conv_ln_b, conv_out, sgu_norm, sgu_ws, sgu_b, sgu_out, nsa_q_norm, nsa_k_norm, cmp_pe,
          cmp_w1, cmp_w2, nsa_out, w_out, norm_xattn, mem_norm, xq, xkv, xq_norm, xk_norm, xo,
          norm_ffn2, ffn2_wi, ffn2_wo, out):
    _, T, D = x.shape
    L = norm_ffn1.shape[0]
    M = mem.shape[1]
    F = ffn1_wo.shape[1]
    CONV_W, DC = conv_w.shape[1:]
    GROUPS, CHUNK = sgu_b.shape[1:]
    DS = sgu_norm.shape[1]
    DH = nsa_q_norm.shape[1]
    XDH = xq_norm.shape[1]
    CMP_LEN = cmp_pe.shape[2]
    HEADS = nsa_out.shape[1] // DH
    KVG = 2
    CMP_STRIDE = CMP_LEN // 2
    NCMP = (T - CMP_LEN) // CMP_STRIDE + 1
    assert T == 512 and D == 1024 and DC == 512 and DS == 512 and CHUNK == P and GROUPS == 4
    assert DH == 64 and HEADS == 8 and XDH == P and M == 256 and F % P == 0 and NCMP == 31
    KD = D // P
    KB = DC // P
    TT = T // P
    FT = F // P
    C_SGU, C_Q = 2 * DC, 2 * DC + 2 * DS
    C_KV = C_Q + HEADS * DH
    C_NG = C_KV + 6 * KVG * DH
    C_MG = C_NG + 3 * HEADS
    PAIRS = HEADS // KVG
    slope = [2.0 ** (-8.0 * (h + 1) / HEADS) for h in range(HEADS)]

    CH = [8, 8, FT - 16]
    FFN = 2 * FT + 3 * KD
    U_MIX = FFN
    U_KV, U_QP = U_MIX, U_MIX + 6
    U_NG = U_QP + 4
    U_CONV = U_NG + 2
    U_SGU = U_CONV + 8
    U_B = U_SGU + 8
    U_A = U_B + 16
    U_C = U_A + 16
    U_WO = U_C + 16
    U_XQ = U_WO + 8
    U_XKV = U_XQ + 4
    U_XO = U_XKV + 8
    U_F2 = U_XO + 8
    U = U_F2 + FFN
    assert U % 4 == 0

    ctx = ExitStack()
    with ctx:
        def sb(name, shape, dt=F32):
            return ctx.enter_context(nc.sbuf_tensor(name, shape, dt))

        raw = sb("raw", [P, 2, KD, P])
        wH = sb("wH", [P, 4, KD, P], F32R)
        wL = sb("wL", [P, 4, KD, P], F32R)
        xT = sb("xT", [P, KD, T])
        gxH = sb("gxH", [P, KD, T], F32R)
        gxL = sb("gxL", [P, KD, T], F32R)
        hH = sb("hH", [P, 8, T], F32R)
        hL = sb("hL", [P, 8, T], F32R)
        big = sb("big", [P, 8 * T])
        convb = sb("convb", [P, 4 * (T + CONV_W - 1) + 4 * T])
        qT = sb("qT", [P, 4, T])
        kT = sb("kT", [P, 2, T])
        VW = DH + 1
        vtok = sb("vtok", [P, 4, 4 * VW])
        KOFF = [sum(T - P * m for m in range(k)) for k in range(TT + 1)]
        prob = sb("prob", [P, 2 * KOFF[TT]])
        att = prob[:, 0:4 * T].rearrange("p (a b t) -> p a b t", a=2, b=2)
        kvc = att[:, 1, :, :]
        tmp3 = sb("tmp3", [P, 3, T])
        nmx = sb("nmx", [P, TT, 3 * HEADS])
        nmHL = sb("nmHL", [P, T], F32R)
        nmH, nmL = nmHL[0:3 * HEADS, :], nmHL[32:32 + 3 * HEADS, :]
        rstd = sb("rstd", [P, T])
        rv = sb("rv", [P, T])
        sacc = sb("sacc", [P, T])
        sq = sb("sq", [P, 2, T])
        tb = sb("tb", [P, 2, T])
        tab = sb("tab", [P, T])
        wsT = sb("wsT", [P, 4, P])
        wsn = sb("wsn", [P, 4, P])
        bbc = sb("bbc", [P, 4, P])
        ident = sb("ident", [P, P])
        ones = sb("ones", [P, P])
        bdon = sb("bdon", [P, P])
        tri = sb("tri", [P, P])
        tabc = sb("tabc", [P, 4, NCMP])
        valid = sb("valid", [P, 4])
        eps = sb("eps", [P, 1])
        w2 = sb("w2", [P, 2, DH])
        hc = sb("hc", [P, 2, 32])
        kcn = sb("kcn", [P, P])
        vcs = sb("vcs", [32, KVG, VW])
        pos = sb("pos", [P, TT])
        cend = sb("cend", [32, 1])
        kbias = sb("kbias", [P, HEADS, TT])
        cbias = sb("cbias", [32, HEADS])
        qbias = sb("qbias", [P, TT, HEADS, 3])
        identB = sb("identB", [P, P], BF16)
        identR = sb("identR", [P, 3 * HEADS], F32R)
        maskT = sb("maskT", [P, P], BF16)
        maskC = sb("maskC", [32, T], BF16)
        gates = sb("gates", [P, TT, 3 * HEADS])
        cs = sb("cs", [P, 8, NCMP])
        ow = sb("ow", [P, 2, 6])
        g8 = sb("g8", [P, 2])
        mst = sb("mst", [P, 2])
        NP_ROWS = 126
        NPAR = NP_ROWS + 4 * CONV_W
        pall = sb("pall", [P, L, NPAR])
        par = sb("par", [P, NPAR])

        TP = T + CONV_W - 1
        cin = convb[:, 0:4 * TP].rearrange("p (j t) -> p j t", j=4)
        cacc = convb[:, 4 * TP:4 * TP + 4 * T].rearrange("p (j t) -> p j t", j=4)
        w1v = cacc.rearrange("p j t -> p (j t)").rearrange("p (j e) -> p j e", j=CMP_LEN)
        w1k = big[:, 0:4 * T].rearrange("p (j e) -> p j e", j=CMP_LEN)
        blk = [big[:, (4 + 2 * i) * T:(4 + 2 * i) * T + CMP_LEN * NCMP]
               .rearrange("p (j n) -> p j n", j=CMP_LEN) for i in range(2)]
        uG = big[:, 0:4 * T].rearrange("p (j t) -> p j t", j=4)
        vG = big[:, 4 * T:8 * T].rearrange("p (j t) -> p j t", j=4)
        mrg = big[:, :].rearrange("p (j t) -> p j t", j=8)
        xnat = big[:, :].rearrange("p (a d) -> p a d", a=TT)
        sil, sr, hb = tmp3[:, 0, :], tmp3[:, 1, :], tmp3[:, 2, :]
        memn = att[:, :, :, :].rearrange("p a b t -> p (a b t)").rearrange("p (a d) -> p a d", a=2)
        memH = hH[:, 0:4, :].rearrange("p a t -> p (a t)").rearrange("p (k m) -> p k m", k=KD)
        memL = hL[:, 0:4, :].rearrange("p a t -> p (a t)").rearrange("p (k m) -> p k m", k=KD)
        kx = kT[:, :, :].rearrange("p a t -> p (a t)").rearrange("p (h m) -> p h m", h=4)
        vx = vtok[:, :, :].rearrange("p a b -> p (a b)")[:, 0:8 * (XDH + 1)]\
            .rearrange("p (a h c) -> p a h c", a=2, h=4)
        vt = vtok[:, :, :].rearrange("p a (g c) -> p a g c", g=4)
        o8 = wsT
        oprod = sq[:, :, :].rearrange("p a t -> p (a t)")[:, 0:12 * DH]
        def merged_tile(h, gx, k):
            return (h if k < 4 else gx)[:, k, :]

        def xnorm_tile(h, gx, k):
            return (gx if k < 4 else h)[:, k, :]

        ctab = convb[:, 0:4 * P].rearrange("p (a c) -> p a c", a=4)

        G_F1, G_MIX, G_X, G_MEM, G_F2 = 0, 8, 16, 24, 32
        P_CB, P_LG, P_LB, P_SG = 40, 44, 48, 52
        P_XQ, P_XK, P_NQ, P_NK, P_PE, P_CW = 56, 57, 58, 59, 62, NP_ROWS

        def col(c, rows=slice(0, P)):
            return par[rows, c:c + 1]

        pg = ctx.enter_context(nc.psum_tensor("pg", [P, 4, T], F32))
        pA = ctx.enter_context(nc.psum_tensor("pA", [P, 4, T], F32))
        pS, pT, pO = pA[:, 0:2, :], pA[:, 2, :], pA[:, 3, :]

        NSTAT = 20
        NSC = HEADS * TT + PAIRS
        ITEMS = 3 * HEADS
        def item(i):
            return i // 6, i // 3 % 2, i % 3

        PAIR_AT = {6 * j + 8: j for j in range(PAIRS - 1)}
        order = ["nm", "mean"]
        for i in range(ITEMS):
            order += [(i, kt) for kt in range(1 if i % 3 == 0 else TT)]
            if i == 2:
                order.append("var")
            if i in PAIR_AT:
                order.append(("pair", PAIR_AT[i]))
        order.append(("pair", PAIRS - 1))
        STEP = {key: n for n, key in enumerate(order)}
        NSTEP = len(STEP)

        order = ["nm"]
        for h in range(4):
            order += [(h, 0), (h, 1)] + ([("turn", h - 2)] if h >= 2 else [])
        XSTEP = {key: n for n, key in enumerate(order + [("turn", 2), ("turn", 3)])}

        scored = [u for j in range(PAIRS) for u in
                  [(j, None, None)] + [(j, c, e) for c in range(TT) for e in range(KVG)]]

        rises = {}

        def sig(name, per_layer, lead=0):
            rises[name] = (per_layer, lead)
            return ctx.enter_context(nc.semaphore(name))

        def risen(s, layer, n):
            per_layer, lead = rises[s.name]
            return layer * per_layer + (lead + n)

        landed = [sig(f"landed{i}", 32 * (U // 2)) for i in range(2)]
        split_h = sig("split_h", U)
        split_l = sig("split_l", U, 2)
        unit_mm = sig("unit_mm", U, 4)
        evac = sig("evac", U, 4)
        gx_h = sig("gx_h", 4 * KD)
        gx_l = sig("gx_l", 4 * KD)
        sq_done = sig("sq_done", 4 * KD)
        sq_used = sig("sq_used", 4 * KD, 2)
        stat_in = sig("stat_in", NSTAT)
        stat_mm = sig("stat_mm", NSTAT - 2)
        stat_rt = sig("stat_rt", NSTAT - 2)
        silu = sig("silu", 2 * FT)
        hid_h = sig("hid_h", 2 * FT)
        hid_l = sig("hid_l", 2 * FT)
        small = sig("small", 16 * 10)
        memld = sig("memld", 16 * 1)
        blk_in = sig("blk_in", 1)
        cmp1 = sig("cmp1", 1)
        cmp_act = sig("cmp_act", 1)
        cmp2 = sig("cmp2", 1)
        ws_tr = sig("ws_tr", 1)
        v_tr = sig("v_tr", 2)
        t_free = sig("t_free", 4)
        ng_in = sig("ng_in", 1)
        ng_sig = sig("ng_sig", 1)
        ng_tr = sig("ng_tr", 1)
        conv_sig = sig("conv_sig", 4)
        cin_in = sig("cin_in", 1)
        conv_in = sig("conv_in", 1)
        gelu = sig("gelu", 8)
        vn = sig("vn", 1)
        sg_tr = sig("sg_tr", TT)
        sg_cp = sig("sg_cp", TT)
        sg_mm = sig("sg_mm", TT)
        sg_out = sig("sg_out", TT)
        ln_sc = sig("ln_sc", 4)
        br_h = sig("br_h", 8)
        br_l = sig("br_l", 12)
        mg_sig = sig("mg_sig", 24)
        s_mm = sig("s_mm", NSC)
        s_out = sig("s_out", NSC)
        nm_in = sig("nm_in", 1)
        nm_l = sig("nm_l", 1)
        st_mm = sig("st_mm", NSTEP)
        st_out = sig("st_out", NSTEP)
        pv = sig("pv", ITEMS)
        o_out = sig("o_out", HEADS)
        o_in = sig("o_in", HEADS)
        m_h = sig("m_h", 8)
        m_in = sig("m_in", 8)
        m_l = sig("m_l", 8)
        mem_st = sig("mem_st", 1)
        mem_sc = sig("mem_sc", 1)
        mem_tr = sig("mem_tr", 4)
        mem_h = sig("mem_h", 4)
        mem_l = sig("mem_l", 4)
        xv_tr = sig("xv_tr", 2)
        xv_cp = sig("xv_cp", 2)
        xs_mm = sig("xs_mm", 8)
        xs_out = sig("xs_out", 8)
        xnm_l = sig("xnm_l", 1)
        xst_mm = sig("xst_mm", len(XSTEP))
        xst_out = sig("xst_out", len(XSTEP))
        xpv = sig("xpv", 4)
        xo_out = sig("xo_out", 4)
        xo_l = sig("xo_l", 4)
        par_in = sig("par_in", 1)
        q_ok = sig("q_ok", 1)
        xk_ok = sig("xk_ok", 2)
        consts = ctx.enter_context(nc.semaphore("consts"))
        pro_ld = ctx.enter_context(nc.semaphore("pro_ld"))
        pro_par = ctx.enter_context(nc.semaphore("pro_par"))
        pro_tr = ctx.enter_context(nc.semaphore("pro_tr"))
        pro_cp = ctx.enter_context(nc.semaphore("pro_cp"))
        fin_tr = ctx.enter_context(nc.semaphore("fin_tr"))
        fin_cp = ctx.enter_context(nc.semaphore("fin_cp"))
        stored = ctx.enter_context(nc.semaphore("stored"))
        pconst = ctx.enter_context(nc.semaphore("pconst"))

        block = ctx.enter_context(nc.Block())

        BR = {"B": 4, "A": 0, "C": 4}
        CT = KB - 1
        B_LAG, A_LAG = 2, 4

        @block.sync
        def _(sp):
            for a in range(TT):
                sp.dma_start(xnat[:, a, :], x[0, a * P:(a + 1) * P, :]).then_inc(pro_ld, 16)

            for g, at in ((norm_ffn1, G_F1), (norm_mix, G_MIX), (norm_xattn, G_X),
                          (mem_norm, G_MEM), (norm_ffn2, G_F2), (conv_b, P_CB),
                          (conv_ln_g, P_LG), (conv_ln_b, P_LB), (sgu_norm, P_SG),
                          (xq_norm, P_XQ), (xk_norm, P_XK)):
                n = g.shape[1] // P
                sp.dma_start(ctab[at:at + n, 0:L, :], g.rearrange("l (a b) -> a l b", b=P))\
                  .then_inc(pro_par, 16)
            for half in range(2):
                cols = slice(half * DH, (half + 1) * DH)
                for g, at in ((nsa_q_norm.rearrange("l (a c) -> a l c", a=1), P_NQ),
                              (nsa_k_norm.rearrange("l a c -> a l c"), P_NK),
                              (cmp_pe.rearrange("l i a c -> i a l c")[0], P_PE),
                              (cmp_pe.rearrange("l i a c -> i a l c")[1], P_PE + CMP_LEN)):
                    n = g.shape[0]
                    sp.dma_start(ctab[at:at + n, 0:L, cols], g).then_inc(pro_par, 16)
            for j in range(4):
                sp.dma_start(ctab[j * CONV_W:(j + 1) * CONV_W, L:2 * L, :],
                             conv_w[:, :, j * P:(j + 1) * P].rearrange("l k c -> k l c"))\
                  .then_inc(pro_par, 16)

            def k_rows(w):
                return w.rearrange("(k p) c -> p k c", p=P)

            def unit(l, u, i, src, kt=KD):
                s = u % 2
                sp.wait_ge(split_l, risen(split_l, l, u - 1 + 4 * i))
                half = kt // 2
                for h in (1, 0):
                    sp.dma_start(raw[:, s, h * half:(h + 1) * half, :], src(h, half))\
                        .then_inc(landed[s], 16)

            def cols_of(w, c0):
                def src(h, half):
                    return k_rows(w)[:, h * half:(h + 1) * half, c0:c0 + P]
                return src

            def at_col(w, c0, width=P):
                def src(h, half):
                    return k_rows(w)[:, h * half:(h + 1) * half, bass.ds(c0, width)]
                return src

            def ffn(l, u, wi, wo):
                ft = 0
                for n in CH:
                    with sp.Fori(0, n // 2) as i:
                        for c in range(4):
                            a, b = divmod(c, 2)
                            c0 = i * (2 * P) + (b * F + (ft + a) * P)
                            unit(l, u + c, i, at_col(wi, c0))
                    u += 2 * n
                    rows_ = wo[ft * P:(ft + n) * P, :]
                    with sp.Fori(0, KD // 4) as i:
                        for c in range(4):
                            unit(l, u + c, i, at_col(rows_, i * (4 * P) + c * P), n)
                    u += KD
                    ft += n

            with sp.Fori(0, L) as l:
                wi1, wo1, wi2, wo2 = ffn1_wi[l], ffn1_wo[l], ffn2_wi[l], ffn2_wo[l]
                win = w_in[l]
                ffn(l, 0, wi1, wo1)
                def load_small(dst, src):
                    sp.dma_start(dst, src).then_inc(small, 16)

                load_small(wsn[:, :, :], sgu_ws[l].rearrange("g t s -> t g s"))
                load_small(bbc[:, :, :].rearrange("p g t -> p (g t)"),
                           sgu_b[l].rearrange("g t -> (g t)").partition_broadcast(P))
                for half in range(2):
                    r = slice(half * DH, (half + 1) * DH)
                    for i, w1 in ((0, w1k), (1, w1v)):
                        load_small(w1[r, :, :], cmp_w1[l][i].rearrange("(j d) e -> d j e", d=DH))
                        load_small(w2[r, i, :], cmp_w2[l][i])
                for i in range(6):
                    unit(l, U_KV + i, 0, cols_of(win, C_KV + i * P))

                def pair_cols(j):
                    def src(h, half):
                        return k_rows(win)[:, :, C_Q + (j + 4 * h) * DH:C_Q + (j + 4 * h + 1) * DH]
                    return src

                for j in range(PAIRS):
                    u = U_QP + j
                    sp.wait_ge(split_l, risen(split_l, l, u - 1))
                    for h in range(2):
                        sp.dma_start(raw[:, u % 2, :, h * DH:(h + 1) * DH],
                                     pair_cols(j)(h, 0)).then_inc(landed[u % 2], 16)
                for i in range(2):
                    u = U_NG + i
                    sp.wait_ge(split_l, risen(split_l, l, u - 1))
                    for h in range(2):
                        k0 = 4 * i + 2 * h
                        sp.dma_start(raw[:, u % 2, 2 * h:2 * h + 2, :],
                                     k_rows(win)[:, k0:k0 + 2, C_NG:C_NG + P])\
                                         .then_inc(landed[u % 2], 16)
                for j in range(4):
                    unit(l, U_CONV + 2 * j, 0, cols_of(win, j * P))
                    unit(l, U_CONV + 2 * j + 1, 0, cols_of(win, DC + j * P))
                for j in range(4):
                    unit(l, U_SGU + j, 0, cols_of(win, C_SGU + DS + j * P))
                for j in range(4):
                    unit(l, U_SGU + 4 + j, 0, cols_of(win, C_SGU + j * P))
                for u0, w, br in ((U_B, sgu_out[l], 1), (U_A, conv_out[l], 0)):
                    with sp.Fori(0, KD // 2) as i:
                        for c in range(2):
                            unit(l, u0 + 2 * c, i,
                                 at_col(win, i * (2 * P) + (C_MG + br * D + c * P)))
                            unit(l, u0 + 2 * c + 1, i, at_col(w, i * (2 * P) + c * P), KB)
                for m in range(KD):
                    unit(l, U_C + 2 * m, 0, cols_of(win, C_MG + 2 * D + m * P))
                    u = U_C + 2 * m + 1
                    sp.wait_ge(split_l, risen(split_l, l, u - 1))
                    for h in range(2):
                        half_rows = nsa_out[l][h * 4 * DH:(h + 1) * 4 * DH, m * P:(m + 1) * P]
                        sp.dma_start(raw[h * DH:(h + 1) * DH, u % 2, 0:4, :],
                                     half_rows.rearrange("(j d) c -> d j c", d=DH))\
                                         .then_inc(landed[u % 2], 16)
                    if m == 2:
                        sp.wait_ge(pv, risen(pv, l, ITEMS))
                        sp.dma_start(memn, mem[0].rearrange("(a p) d -> p a d", p=P))\
                            .then_inc(memld, 16)
                for u0, w, n, kt in ((U_WO, w_out[l], 8, KD), (U_XQ, xq[l], 4, KD),
                                     (U_XKV, xkv[l], 8, KD), (U_XO, xo[l], 8, 4)):
                    with sp.Fori(0, n // 4) as i:
                        for c in range(4):
                            unit(l, u0 + c, i, at_col(w, i * (4 * P) + c * P), kt)
                ffn(l, U_F2, wi2, wo2)

            for a in range(TT):
                sp.wait_ge(fin_cp, 2 * (a + 1))
                sp.dma_start(out[0, a * P:(a + 1) * P, :], xnat[:, a, :]).then_inc(stored, 16)
            sp.wait_ge(stored, 16 * TT)

        @block.gpsimd
        def _(pool):
            pool.memset(ident[:, :], 0.0)
            pool.memset(ones[:, :], 1.0)
            pool.memset(bdon[:, :], 0.0)
            pool.memset(tri[:, :], 1.0)
            pool.memset(valid[:, :], 1.0)
            pool.memset(eps[:, :], EPS)
            pool.memset(vcs[:, :, :], 1.0)
            pool.memset(kcn[:, :], 0.0)
            pool.memset(sacc[:, :], 0.0)
            pool.memset(tb[:, 0, 0:P], 0.0)
            pool.memset(tb[:, 1, :], 0.0)
            pool.iota(pos[:, :], pattern=[[P, TT]], base=0, channel_multiplier=1,
                      allow_small_or_imprecise_dtypes=True)
            pool.iota(cend[:, :], pattern=[[0, 1]], base=CMP_LEN - 1,
                      channel_multiplier=CMP_STRIDE, allow_small_or_imprecise_dtypes=True)
            pool.iota(tab[:, :], pattern=[[1, T]], base=-(T - P), channel_multiplier=-1,
                      allow_small_or_imprecise_dtypes=True)
            pool.iota(tabc[:, :, :], pattern=[[-P, 4], [CMP_STRIDE, NCMP]], base=CMP_LEN - 1,
                      channel_multiplier=-1, allow_small_or_imprecise_dtypes=True)
            pool.drain().then_inc(pconst, 1)
            pool.wait_ge(pconst, 1)
            pool.memset(bdon[0:DH, 0:DH], 1.0)
            pool.drain().then_inc(pconst, 1)
            pool.wait_ge(pconst, 2)
            pool.memset(bdon[DH:P, DH:P], 1.0)
            pool.drain().then_inc(pconst, 1)
            pool.wait_ge(pconst, 3)
            pool.affine_select(out=ident[:, :], in_=ident[:, :], compare_op=ALU.not_equal, fill=1.0,
                               base=0, pattern=[[-1, P]], channel_multiplier=1)
            pool.affine_select(out=tri[:, :], in_=tri[:, :], compare_op=ALU.is_ge, fill=0.0,
                               base=0, pattern=[[1, P]], channel_multiplier=-1)
            pool.affine_select(out=tb[:, 0, 0:P], in_=tb[:, 0, 0:P], compare_op=ALU.is_ge,
                               fill=NEG, base=0, pattern=[[1, P]], channel_multiplier=-1)
            pool.affine_select(out=tb[:, 1, :], in_=tb[:, 1, :], compare_op=ALU.is_ge, fill=NEG,
                               base=-(CMP_LEN - 1), pattern=[[1, T]],
                               channel_multiplier=-CMP_STRIDE)
            pool.affine_select(out=tab[:, :], in_=tab[:, :], compare_op=ALU.is_ge, fill=NEG,
                               base=T - P, pattern=[[-1, T]], channel_multiplier=1)
            pool.affine_select(out=tabc[:, :, :], in_=tabc[:, :, :], compare_op=ALU.is_ge, fill=NEG,
                               base=-(CMP_LEN - 1), pattern=[[P, 4], [-CMP_STRIDE, NCMP]],
                               channel_multiplier=1)
            pool.affine_select(out=valid[:, 0:1], in_=valid[:, 0:1], compare_op=ALU.is_ge, fill=0.0,
                               base=-(CMP_LEN - 1), pattern=[[1, 1]], channel_multiplier=1)
            pool.drain().then_inc(consts, 1)
            pool.sem_inc(split_l, risen(split_l, 0, 0))

            def low(l, s, i=0):
                pool.wait_ge(split_h, risen(split_h, l, s + 1 + 4 * i))
                pool.tensor_tensor(wL[:, s % 4, :, :], raw[:, s % 2, :, :],
                                   wH[:, s % 4, :, :].bitcast(F32), ALU.subtract)\
                                       .then_inc(split_l, 1)

            def lows(l, first, last):
                with pool.Fori(0, (last - first) // 4) as i:
                    for s in range(4):
                        low(l, first + s, i)

            with pool.Fori(0, L) as l:
                lows(l, 0, U_SGU + 4)
                pool.wait_ge(cin_in, risen(cin_in, l, 1))
                k, o, term = 0, cacc[:, CT, :], prob[:, 4 * T:5 * T]
                for u in range(U_SGU + 4, U_A):
                    low(l, u)
                    for _ in range(2 if U_B <= u < U_B + 11 else 1):
                        if k == CONV_W:
                            break
                        w = col(P_CW + CT * CONV_W + k)
                        if k == 0:
                            pool.tensor_scalar(o, cin[:, CT, 0:T], w, col(P_CB + CT), ALU.mult,
                                               ALU.add)
                        else:
                            pool.tensor_scalar(term, cin[:, CT, k:k + T], w, None, ALU.mult)
                            pool.drain()
                            pool.tensor_tensor(o, o, term, ALU.add)
                        pool.drain()
                        k += 1
                pool.drain().then_inc(conv_in, 1)
                assert k == CONV_W
                lows(l, U_A, U)

        @block.tensor
        def _(pe):
            mm = pe.matmul

            def unit(l, u, i, kt, rh, rl, n=T, before=None):
                s = u % 4
                pe.wait_ge(split_l, risen(split_l, l, u + 1 + 4 * i))
                pe.wait_ge(evac, risen(evac, l, u - 3 + 4 * i))
                o = pg[:, s, 0:n]
                for k in range(kt):
                    if before:
                        before(k)
                    mm(o, wH[:, s, k, :], rh(k), start=(k == 0), stop=False)
                    mm(o, wH[:, s, k, :], rl(k), start=False, stop=False)
                    last = mm(o, wL[:, s, k, :], rh(k), start=False, stop=(k == kt - 1))
                last.then_inc(unit_mm, 1)

            def stat(l, s, weights, n=T):
                pe.wait_ge(stat_in, risen(stat_in, l, s + 1))
                mm(pO[:, 0:n], weights[:, :], sacc[:, 0:n], start=True, stop=True)\
                    .then_inc(stat_mm, 1)

            gH, gL = (lambda k: gxH[:, k, :]), (lambda k: gxL[:, k, :])

            def norm_ready(l, n):
                def before(k):
                    pe.wait_ge(gx_l, risen(gx_l, l, KD * n + k + 1))
                return before

            def ffn(l, u, f, n_norm, s_norm):
                ft = 0
                for ch, n in enumerate(CH):
                    first = 0
                    if ch == 0:
                        for c in range(4):
                            unit(l, u + c, 0, KD, gH, gL,
                                 before=norm_ready(l, n_norm) if c == 0 else None)
                            if c == 1:
                                stat(l, s_norm, ones)
                        first = 1
                    with pe.Fori(first, n // 2) as i:
                        for c in range(4):
                            unit(l, u + c, i, KD, gH, gL)
                    u += 2 * n

                    def hid(k):
                        pe.wait_ge(hid_l, risen(hid_l, l, f * FT + ft + k + 1))

                    for m in range(KD):
                        unit(l, u + m, 0, n, lambda k: hH[:, k, :], lambda k: hL[:, k, :],
                             before=hid if m == 0 else None)
                    u += KD
                    ft += n

            def turn(dst, src, k=P):
                return pe.transpose(dst, src, ident[0:k, 0:k])

            pe.sem_inc(unit_mm, risen(unit_mm, 0, 0))
            pe.wait_ge(consts, 1)
            pe.wait_ge(pro_ld, 16 * TT)
            for k in range(KD):
                if k >= 4:
                    pe.wait_ge(pro_cp, k - 4 + 1)
                for a in range(TT):
                    last = turn(pg[:, k % 4, a * P:(a + 1) * P], xnat[:, a, k * P:(k + 1) * P])
                last.then_inc(pro_tr, 1)
            pe.wait_ge(pro_par, 16 * (11 + 8 + 4))
            for l in range(L):
                turn(pT[:, l * P:l * P + NP_ROWS], ctab[0:NP_ROWS, l, :], NP_ROWS)
            for l in range(L):
                last = turn(pT[:, (2 + l) * P:(2 + l) * P + 4 * CONV_W],
                            ctab[0:4 * CONV_W, L + l, :], 4 * CONV_W)
            last.then_inc(pro_tr, 1)

            with pe.Fori(0, L) as l:
                ffn(l, 0, 0, 0, 0)

                unit(l, U_KV, 0, KD, gH, gL, before=norm_ready(l, 1))
                unit(l, U_KV + 1, 0, KD, gH, gL)
                stat(l, 1, ones)
                unit(l, U_KV + 2, 0, KD, gH, gL)
                pe.wait_ge(small, risen(small, l, 160))
                for g in range(GROUPS):
                    last = turn(pT[:, g * P:(g + 1) * P], wsn[:, g, :])
                last.then_inc(ws_tr, 1)
                unit(l, U_KV + 3, 0, KD, gH, gL)
                stat(l, 2, bdon)
                pe.wait_ge(blk_in, risen(blk_in, l, 1))
                pe.wait_ge(t_free, risen(t_free, l, 1))
                pe.wait_ge(evac, risen(evac, l, U_KV + 4))
                for a in range(TT):
                    last = turn(pT[:, a * P:(a + 1) * P], tb[:, 0, a * P:(a + 1) * P])
                last.then_inc(v_tr, 1)
                for i, w1 in ((0, w1k), (1, w1v)):
                    for g in range(KVG):
                        r = slice(g * DH, (g + 1) * DH)
                        for j in range(CMP_LEN):
                            last = mm(pS[r, 0, 32 * i:32 * i + NCMP], w1[r, j, :], blk[i][r, j, :],
                                      start=(j == 0), stop=(j == CMP_LEN - 1))
                last.then_inc(cmp1, 1)
                unit(l, U_KV + 4, 0, KD, gH, gL)
                unit(l, U_KV + 5, 0, KD, gH, gL)
                pe.wait_ge(cmp_act, risen(cmp_act, l, 1))
                stat(l, 3, bdon)
                for g in range(KVG):
                    r = slice(g * DH, (g + 1) * DH)
                    mm(pS[r, 1, 0:NCMP], w2[r, 0, :], hc[r, 0, 0:NCMP], start=True, stop=True)
                for g in range(KVG):
                    r = slice(g * DH, (g + 1) * DH)
                    last = mm(pS[0:NCMP, 1 - g, P:P + DH], hc[r, 1, 0:NCMP],
                              w2[r, 1, :], start=True, stop=True)
                last.then_inc(cmp2, 1)
                unit(l, U_QP, 0, KD, gH, gL)
                stat(l, 4, bdon, NCMP)
                pe.wait_ge(t_free, risen(t_free, l, 2))
                pe.wait_ge(evac, risen(evac, l, U_KV + 6))
                for a in range(TT):
                    last = turn(pT[:, a * P:(a + 1) * P], tb[:, 1, a * P:(a + 1) * P])
                last.then_inc(v_tr, 1)
                for j in range(1, PAIRS):
                    unit(l, U_QP + j, 0, KD, gH, gL)
                    stat(l, 5 + j - 1, bdon)
                for i in range(2):
                    unit(l, U_NG + i, 0, 4, lambda k: gxH[:, 4 * i + k, :],
                         lambda k: gxL[:, 4 * i + k, :])
                stat(l, 8, bdon)
                unit(l, U_CONV, 0, KD, gH, gL)
                pe.wait_ge(t_free, risen(t_free, l, 3))
                pe.wait_ge(ng_sig, risen(ng_sig, l, 1))
                for a in range(TT):
                    last = turn(pT[:, a * P:(a + 1) * P], hb[:, a * P:(a + 1) * P])
                last.then_inc(ng_tr, 1)
                for j in range(1, 8):
                    unit(l, U_CONV + j, 0, KD, gH, gL)
                for j in range(8):
                    unit(l, U_SGU + j, 0, KD, gH, gL)
                    if j == 5:
                        stat(l, 9, ones)
                def v_turned(c):
                    if c >= 2:
                        pe.wait_ge(sg_cp, risen(sg_cp, l, c - 1))
                    bank = pA[:, 2 + c % 2, :]
                    for g in range(GROUPS):
                        last = turn(bank[:, g * P:(g + 1) * P], vG[:, g, c * P:(c + 1) * P])
                    last.then_inc(sg_tr, 1)

                pe.wait_ge(vn, risen(vn, l, 1))
                pe.wait_ge(t_free, risen(t_free, l, 4))
                v_turned(0)
                for c in range(TT):
                    if c + 1 < TT:
                        v_turned(c + 1)
                    pe.wait_ge(sg_cp, risen(sg_cp, l, c + 1))
                    if c >= 2:
                        pe.wait_ge(sg_out, risen(sg_out, l, c - 1))
                    for g in range(GROUPS):
                        last = mm(pS[:, c % 2, g * P:(g + 1) * P], sq[:, c % 2, g * P:(g + 1) * P],
                                  wsT[:, g, :], start=True, stop=True)
                    last.then_inc(sg_mm, 1)

                def scores(q):
                    j, c, e = scored[q]
                    bank = pA[:, 2 * (q % 2):2 * (q % 2) + 2, :]
                    if q >= 2:
                        pe.wait_ge(s_out, risen(s_out, l, q - 1))
                    if c is None:
                        for e in range(KVG):
                            h = slice(e * DH, (e + 1) * DH)
                            for c in range(TT):
                                last = mm(bank[:, e, 32 * c:32 * c + NCMP],
                                          qT[h, j, c * P:(c + 1) * P], kcn[h, 0:NCMP],
                                          start=True, stop=True)
                    else:
                        h, n = slice(e * DH, (e + 1) * DH), (c + 1) * P
                        for b in range(2):
                            last = mm(bank[:, b, 0:n], qT[h, j, c * P:(c + 1) * P], kT[h, b, 0:n],
                                      start=True, stop=True)
                    last.then_inc(s_mm, 1)

                def branch_unit(u, br, base):
                    if u % 2 == 0:
                        unit(l, u, 0, KD, gH, gL)
                    else:
                        def ready(k):
                            pe.wait_ge(br_l, risen(br_l, l, base + k + 1))
                        unit(l, u, 0, KB, lambda k: hH[:, BR[br] + k, :],
                             lambda k: hL[:, BR[br] + k, :],
                             before=ready if u % 16 == (U_B + 1) % 16 else None)

                branch_unit(U_B, "B", 0)
                pe.wait_ge(q_ok, risen(q_ok, l, 1))
                pe.wait_ge(sg_out, risen(sg_out, l, TT))
                for q in range(NSC):
                    scores(q)
                    if q % 2 and 1 <= q // 2 - B_LAG < 16:
                        branch_unit(U_B + q // 2 - B_LAG, "B", 0)

                def free(key):
                    n = STEP[key]
                    if n >= 2:
                        pe.wait_ge(st_out, risen(st_out, l, n - 1))
                    return pA[:, n % 2, :]

                def all_of(col, m):
                    one = identR[:, col:col + 1]
                    return bass.AP(tensor=one.tensor, offset=one.offset, ap=[one.ap[0], [0, m]])

                def step(i, kt):
                    j, e, b = item(i)
                    r = slice(e * DH, (e + 1) * DH)
                    cols = slice(kt * P, T)
                    n = T - kt * P
                    bank = free((i, kt))
                    col_ = 3 * (j + 4 * e) + b
                    mm(bank[:, 0:n], all_of(col_, P), nmHL[:, cols], start=True, stop=False)
                    if b == 0:
                        m = NCMP
                        mm(bank[0:m, 0:n], identB[0:m, 0:m], maskC[0:m, :], start=False,
                           stop=False)
                        last = mm(bank[:, 0:n], kcn[r, :], qT[r, j, cols], start=False, stop=True)
                    else:
                        mm(bank[:, 0:P], identB[:, :], maskT[:, :], start=False, stop=False)
                        last = mm(bank[:, 0:n], kT[r, b - 1, kt * P:(kt + 1) * P],
                                  qT[r, j, cols], start=False, stop=True)
                    last.then_inc(st_mm, 1)

                def values(i):
                    j, e, b = item(i)
                    if b == 0 and i:
                        pe.wait_ge(o_out, risen(o_out, l, i // 3))
                    pe.wait_ge(st_out, risen(st_out, l, STEP[i, 0 if b == 0 else TT - 1] + 1))
                    p0 = (i % 2) * KOFF[TT]
                    for qt in range(TT):
                        at = (qt % 2 * 3 + b) * VW
                        o = pA[:, 2 + qt // 2, at:at + VW]
                        if b == 0:
                            last = mm(o, prob[0:NCMP, p0 + qt * P:p0 + (qt + 1) * P],
                                      vcs[0:NCMP, e, :], start=True, stop=True)
                        else:
                            for kt in range(qt + 1):
                                at = p0 + KOFF[kt] + (qt - kt) * P
                                last = mm(o, prob[:, at:at + P], vt[:, kt, 2 * (b - 1) + e, :],
                                          start=(kt == 0), stop=(kt == qt))
                    last.then_inc(pv, 1)

                def pair_turned(j):
                    pe.wait_ge(o_in, risen(o_in, l, 2 * j + 2))
                    bank = free(("pair", j))
                    for c in range(TT):
                        last = turn(bank[:, c * P:(c + 1) * P], o8[:, c, :])
                    last.then_inc(st_mm, 1)

                pe.wait_ge(s_out, risen(s_out, l, NSC))
                pe.wait_ge(nm_in, risen(nm_in, l, 1))
                bank = free("nm")
                for c in range(TT):
                    last = turn(bank[0:3 * HEADS, c * P:(c + 1) * P], nmx[:, c, :])
                last.then_inc(st_mm, 1)
                pe.wait_ge(stat_in, risen(stat_in, l, 11))
                mm(free("mean"), ones[:, :], sacc[:, :], start=True, stop=True).then_inc(st_mm, 1)
                pe.wait_ge(nm_l, risen(nm_l, l, 1))
                for i in range(ITEMS):
                    for kt in range(1 if i % 3 == 0 else TT):
                        step(i, kt)
                    if i == 2:
                        bank = free("var")
                        pe.wait_ge(stat_in, risen(stat_in, l, 12))
                        mm(bank, ones[:, :], sacc[:, :], start=True, stop=True).then_inc(st_mm, 1)
                    if i in PAIR_AT:
                        pair_turned(PAIR_AT[i])
                    if 0 <= i - A_LAG < 16:
                        branch_unit(U_A + i - A_LAG, "A", 4)
                    if i:
                        values(i - 1)
                values(ITEMS - 1)
                unit(l, U_C, 0, KD, gH, gL)
                pair_turned(PAIRS - 1)

                for m in range(8):
                    if m:
                        unit(l, U_C + 2 * m, 0, KD, gH, gL)

                    def c_ready(k):
                        pe.wait_ge(br_l, risen(br_l, l, 8 + k + 1))
                    unit(l, U_C + 2 * m + 1, 0, KB, lambda k: hH[:, BR["C"] + k, :],
                         lambda k: hL[:, BR["C"] + k, :], before=c_ready if m == 0 else None)

                def m_ready(k):
                    pe.wait_ge(m_l, risen(m_l, l, k + 1))
                for m in range(8):
                    unit(l, U_WO + m, 0, KD, lambda k: merged_tile(hH, gxH, k),
                         lambda k: merged_tile(hL, gxL, k), before=m_ready if m == 0 else None)
                pe.wait_ge(mem_sc, risen(mem_sc, l, 1))
                for i in range(4):
                    for k in range(2):
                        for a in range(2):
                            at = (2 * k + a) * P
                            kk = 2 * i + k
                            last = turn(pA[:, i, at:at + P], memn[:, a, kk * P:(kk + 1) * P])
                    last.then_inc(mem_tr, 1)
                for j in range(4):
                    unit(l, U_XQ + j, 0, KD, lambda k: xnorm_tile(hH, gxH, k),
                         lambda k: xnorm_tile(hL, gxL, k),
                         before=norm_ready(l, 2) if j == 0 else None)
                    if j == 1:
                        pe.wait_ge(mem_l, risen(mem_l, l, 4))
                    if j >= 1:
                        stat(l, 11 + j, ones)

                def x_scores(h):
                    for half in range(2):
                        n = 2 * h + half
                        if n >= 2:
                            pe.wait_ge(xs_out, risen(xs_out, l, n - 1))
                        for c in range(2):
                            at = (2 * half + c) * P
                            last = mm(pS[:, half, c * M:(c + 1) * M], qT[:, h, at:at + P],
                                      kx[:, h, :], start=True, stop=True)
                        last.then_inc(xs_mm, 1)

                def mem_ready(k):
                    pe.wait_ge(mem_l, risen(mem_l, l, k // 2 + 1))
                XSTAT = {1: 15, 2: 16, 3: 17, 5: 18}
                for h in range(8):
                    unit(l, U_XKV + h, 0, KD, lambda k: memH[:, k, :], lambda k: memL[:, k, :], n=M,
                         before=mem_ready if h == 0 else None)
                    if h in XSTAT:
                        stat(l, XSTAT[h], ones)
                    if h >= 6:
                        i = h - 6
                        pe.wait_ge(xk_ok, risen(xk_ok, l, i + 1))
                        if i == 0:
                            pe.wait_ge(mem_l, risen(mem_l, l, 4))
                        x_scores(2 * i)
                        x_scores(2 * i + 1)
                        pe.wait_ge(evac, risen(evac, l, U_XKV + 6 + 2 * i))
                        if i == 1:
                            pe.wait_ge(xv_cp, risen(xv_cp, l, 1))
                        for a in range(2):
                            for hh in range(2):
                                last = turn(pT[:, (2 * a + hh) * P:(2 * a + hh + 1) * P],
                                            tb[:, i, hh * M + a * P:hh * M + (a + 1) * P])
                        last.then_inc(xv_tr, 1)

                def x_free(key):
                    n = XSTEP[key]
                    if n >= 2:
                        pe.wait_ge(xst_out, risen(xst_out, l, n - 1))
                    return pA[:, n % 2, :]

                def x_values(h):
                    pe.wait_ge(xst_out, risen(xst_out, l, XSTEP[h, 1] + 1))
                    if h >= 1:
                        pe.wait_ge(xo_out, risen(xo_out, l, h))
                    for c in range(TT):
                        at = c % 2 * (XDH + 1)
                        for a in range(2):
                            p0 = (h % 2 * 2 + a) * T + c * P
                            last = mm(pA[:, 2 + c // 2, at:at + XDH + 1], prob[:, p0:p0 + P],
                                      vx[:, a, h, :], start=(a == 0), stop=(a == 1))
                    last.then_inc(xpv, 1)

                def x_turned(h):
                    pe.wait_ge(xo_out, risen(xo_out, l, h + 1))
                    bank = x_free(("turn", h))
                    for c in range(TT):
                        last = turn(bank[:, c * P:(c + 1) * P], o8[:, c, :])
                    last.then_inc(xst_mm, 1)

                pe.wait_ge(xs_out, risen(xs_out, l, 8))
                bank = x_free("nm")
                for c in range(TT):
                    last = turn(bank[0:3 * HEADS, c * P:(c + 1) * P], nmx[:, c, :])
                last.then_inc(xst_mm, 1)
                pe.wait_ge(xv_cp, risen(xv_cp, l, 2))
                pe.wait_ge(xnm_l, risen(xnm_l, l, 1))
                for h in range(4):
                    for a in range(2):
                        bank = x_free((h, a))
                        mm(bank, all_of(h, P), nmHL[:, :], start=True, stop=False)
                        mm(bank, kx[:, h, a * P:(a + 1) * P], qT[:, h, :], start=False,
                           stop=True).then_inc(xst_mm, 1)
                    if h >= 2:
                        x_turned(h - 2)
                    if h >= 1:
                        x_values(h - 1)
                x_turned(2)
                x_values(3)
                x_turned(3)

                def xo_ready(k):
                    pe.wait_ge(xo_l, risen(xo_l, l, k + 1))
                for m in range(8):
                    unit(l, U_XO + m, 0, 4, lambda k: hH[:, k, :], lambda k: hL[:, k, :],
                         before=xo_ready if m == 0 else None)
                ffn(l, U_F2, 1, 3, 19)

            pe.wait_ge(evac, risen(evac, L, 0))
            for a in range(TT):
                for hf in range(2):
                    n = 2 * a + hf
                    if n >= 4:
                        pe.wait_ge(fin_cp, n - 3)
                    for k in range(4):
                        last = turn(pg[:, n % 4, k * P:(k + 1) * P],
                                    xT[:, 4 * hf + k, a * P:(a + 1) * P])
                    last.then_inc(fin_tr, 1)

        @block.scalar
        def _(act):
            made = [0]

            def copy(o, i, **kw):
                return act.activation(o, i, ACT.Copy, **kw)

            def split(l, u, i=0):
                s = u % 2
                act.wait_ge(landed[s], risen(landed[s], l, 32 * (u // 2 + 1) + 64 * i))
                act.wait_ge(unit_mm, risen(unit_mm, l, u - 3 + 4 * i))
                copy(wH[:, u % 4, :, :], raw[:, s, :, :]).then_inc(split_h, 1)

            def ahead(l, u, i=0):
                if u + 3 < U:
                    assert made[0] == u + 3
                    made[0] += 1
                    split(l, u + 3, i)

            def gx_tile(k):
                return gxH[:, k, :]

            def norm(l, n, gain, dst, u0):
                def high(k):
                    act.wait_ge(evac, risen(evac, l, 0 if u0 is None else u0 + k + 1))
                    copy(dst(k), xT[:, k, :], scale=col(gain + k)).then_inc(gx_h, 1)

                def square(k):
                    act.wait_ge(sq_used, risen(sq_used, l, KD * n + k - 1))
                    act.activation(sq[:, k % 2, :], xT[:, k, :], ACT.Square).then_inc(sq_done, 1)

                if u0 is None:
                    for k in range(KD):
                        high(k)
                for k in range(KD):
                    if u0 is not None:
                        ahead(l, u0 + k)
                        high(k)
                    square(k)

            def root(l, s, dst, scale, n=T):
                act.wait_ge(stat_mm, risen(stat_mm, l, s + 1 if s < 10 else s - 1))
                act.activation(dst[:, 0:n], pO[:, 0:n], ACT.Sqrt, bias=eps[:, 0:1],
                               scale=scale).then_inc(stat_rt, 1)

            def ffn(l, u, last_norm):
                for ch, n in enumerate(CH):
                    start = made[0]
                    with act.Fori(0, n // 2) as i:
                        for c in range(2):
                            ahead(l, u + 2 * c, i)
                            act.wait_ge(evac, risen(evac, l, u + 2 * c + 1 + 4 * i))
                            act.activation(sil, tb[:, 0, :], ACT.Silu).then_inc(silu, 1)
                            ahead(l, u + 2 * c + 1, i)
                            act.wait_ge(evac, risen(evac, l, u + 2 * c + 2 + 4 * i))
                            copy(hH[:, bass.ds(i * 2 + c, 1), :].rearrange("p a t -> p (a t)"),
                                 hb).then_inc(hid_h, 1)
                    made[0] = start + 2 * n
                    u += 2 * n
                    if ch == len(CH) - 1 and last_norm:
                        norm(l, *last_norm, u)
                    else:
                        for m in range(KD):
                            ahead(l, u + m)
                    u += KD

            act.wait_ge(consts, 1)
            with act.Fori(0, L) as l:
                for u in range(3):
                    split(l, u)
                made[0] = 3
                act.wait_ge(par_in, risen(par_in, l, 1))
                norm(l, 0, G_F1, gx_tile, None)
                root(l, 0, rstd, 1.0 / D)
                ffn(l, 0, (1, G_MIX, gx_tile))

                ahead(l, U_KV)
                ahead(l, U_KV + 1)
                root(l, 1, rstd, 1.0 / D)
                ahead(l, U_KV + 2)
                ahead(l, U_KV + 3)
                root(l, 2, rv, 1.0 / DH)
                act.wait_ge(cmp1, risen(cmp1, l, 1))
                act.activation(hc[:, :, 0:NCMP],
                               pS[:, 0, 0:64].rearrange("p (i n) -> p i n", i=2)[:, :, 0:NCMP],
                               ACT.Silu).then_inc(cmp_act, 1)
                ahead(l, U_KV + 4)
                ahead(l, U_KV + 5)
                root(l, 3, rv, 1.0 / DH)
                ahead(l, U_QP)
                root(l, 4, rv, 1.0 / DH, NCMP)
                for j in range(1, PAIRS):
                    ahead(l, U_QP + j)
                    root(l, 5 + j - 1, rv, 1.0 / DH)
                ahead(l, U_NG)
                ahead(l, U_NG + 1)
                root(l, 8, rv, 1.0 / DH)
                act.wait_ge(ng_in, risen(ng_in, l, 1))
                act.activation(hb, sr, ACT.Sigmoid).then_inc(ng_sig, 1)
                for j in range(4):
                    ahead(l, U_CONV + 2 * j)
                    ahead(l, U_CONV + 2 * j + 1)
                    act.wait_ge(evac, risen(evac, l, U_CONV + 2 * j + 2))
                    act.activation(sil, tb[:, 1, :], ACT.Sigmoid).then_inc(conv_sig, 1)
                for j in range(8):
                    ahead(l, U_SGU + j)
                    act.wait_ge(evac, risen(evac, l, U_SGU + j + 1))
                    dst = vG[:, j, :] if j < 4 else uG[:, j - 4, :]
                    act.activation(dst, tb[:, j % 2, :], ACT.Gelu_apprx_tanh).then_inc(gelu, 1)
                    if j == 5:
                        root(l, 9, rv, 1.0 / DS)
                for c in range(TT):
                    act.wait_ge(sg_tr, risen(sg_tr, l, c + 1))
                    if c >= 2:
                        act.wait_ge(sg_mm, risen(sg_mm, l, c - 1))
                    copy(sq[:, c % 2, :], pA[:, 2 + c % 2, :]).then_inc(sg_cp, 1)
                act.wait_ge(sg_out, risen(sg_out, l, TT))
                for k in range(KB):
                    copy(hH[:, BR["B"] + k, :], uG[:, k, :]).then_inc(br_h, 1)

                def merge_gate(u):
                    act.wait_ge(evac, risen(evac, l, u + 1))
                    act.activation(sr, tb[:, 0, :], ACT.Sigmoid).then_inc(mg_sig, 1)

                for m in range(16):
                    ahead(l, U_B + m)
                    if m % 2 == 0:
                        merge_gate(U_B + m)

                def taken(key):
                    act.wait_ge(st_mm, risen(st_mm, l, STEP[key] + 1))
                    return pA[:, STEP[key] % 2, :]

                def pair_out(j):
                    bank = taken(("pair", j))
                    copy(qT[:, j, :], bank)
                    copy(hH[:, BR["C"] + j, :], bank).then_inc(st_out, 1)

                copy(nmH[:, :], taken("nm")[0:3 * HEADS, :]).then_inc(st_out, 1)
                copy(sil, taken("mean"), scale=-1.0 / DC).then_inc(st_out, 1)
                for i in range(ITEMS):
                    j, e, b = item(i)
                    p0 = (i % 2) * KOFF[TT]
                    if i >= 2:
                        act.wait_ge(pv, risen(pv, l, i - 1))
                    for kt in range(1 if b == 0 else TT):
                        bank = taken((i, kt))
                        if b == 0:
                            act.activation(prob[0:NCMP, p0:p0 + T], bank[0:NCMP, :], ACT.Exp,
                                           bias=cbias[0:NCMP, j + 4 * e:j + 4 * e + 1])\
                                               .then_inc(st_out, 1)
                        else:
                            n = T - kt * P
                            at = p0 + KOFF[kt]
                            act.activation(prob[:, at:at + n], bank[:, 0:n], ACT.Exp,
                                           bias=kbias[:, j + 4 * e, kt:kt + 1]).then_inc(st_out, 1)
                    if i == 2:
                        act.activation(rv[:, :], taken("var"), ACT.Sqrt, bias=eps[:, 0:1],
                                       scale=1.0 / DC).then_inc(st_out, 1)
                    if i == 4:
                        for k in range(KB):
                            act.wait_ge(ln_sc, risen(ln_sc, l, k + 1))
                            act.activation(cacc[:, k, :], cacc[:, k, :], ACT.Silu,
                                           bias=col(P_LB + k), scale=col(P_LG + k))
                        act.drain()
                        for k in range(KB):
                            copy(hH[:, BR["A"] + k, :], cacc[:, k, :]).then_inc(br_h, 1)
                    if i in PAIR_AT:
                        pair_out(PAIR_AT[i])
                    if 0 <= i - A_LAG < 16:
                        ahead(l, U_A + i - A_LAG)
                        if (i - A_LAG) % 2 == 0:
                            merge_gate(U_A + i - A_LAG)
                pair_out(PAIRS - 1)
                def merged_high(m):
                    if m == 4:
                        act.wait_ge(unit_mm, risen(unit_mm, l, U_C + 15))
                    act.wait_ge(m_in, risen(m_in, l, m + 1))
                    copy(merged_tile(hH, gxH, m), mrg[:, m, :]).then_inc(m_h, 1)

                for m in range(8):
                    ahead(l, U_C + 2 * m)
                    merge_gate(U_C + 2 * m)
                    if 1 <= m <= 4:
                        merged_high(m - 1)
                    ahead(l, U_C + 2 * m + 1)
                    if m == 5:
                        act.wait_ge(memld, risen(memld, l, 16))
                        for a in range(2):
                            act.activation(sq[:, :, :].rearrange("p a t -> p (a t)"),
                                           memn[:, a, :], ACT.Square, accum_out=mst[:, a:a + 1])
                            act.drain()
                        act.activation(mst[:, :], mst[:, :], ACT.Sqrt, bias=eps[:, 0:1],
                                       scale=1.0 / D).then_inc(mem_st, 1)
                for m in range(4, 8):
                    merged_high(m)
                norm(l, 2, G_X, lambda k: xnorm_tile(hH, gxH, k), U_WO)
                for i in range(4):
                    act.wait_ge(mem_tr, risen(mem_tr, l, i + 1))
                    for k in range(2):
                        kk = 2 * i + k
                        last = copy(memH[:, kk, :], pA[:, i, k * M:(k + 1) * M],
                                    scale=col(G_MEM + kk))
                    last.then_inc(mem_h, 1)
                for j in range(4):
                    ahead(l, U_XQ + j)
                    if j >= 1:
                        root(l, 11 + j, rstd if j == 1 else rv, 1.0 / (D if j == 1 else XDH))
                for h in range(8):
                    ahead(l, U_XKV + h)
                    if h in (1, 2, 3, 5):
                        root(l, {1: 15, 2: 16, 3: 17, 5: 18}[h], rv, 1.0 / XDH)

                def x_taken(key):
                    act.wait_ge(xst_mm, risen(xst_mm, l, XSTEP[key] + 1))
                    return pA[:, XSTEP[key] % 2, :]

                def x_out(h):
                    bank = x_taken(("turn", h))
                    copy(qT[:, h, :], bank)
                    copy(hH[:, h, :], bank).then_inc(xst_out, 1)

                copy(nmH[:, :], x_taken("nm")[0:3 * HEADS, :]).then_inc(xst_out, 1)
                for h in range(4):
                    if h >= 2:
                        act.wait_ge(xpv, risen(xpv, l, h - 1))
                    for a in range(2):
                        p0 = (h % 2 * 2 + a) * T
                        act.activation(prob[:, p0:p0 + T], x_taken((h, a)), ACT.Exp)\
                            .then_inc(xst_out, 1)
                    if h >= 2:
                        x_out(h - 2)
                x_out(2)
                x_out(3)
                norm(l, 3, G_F2, gx_tile, U_XO)
                root(l, 19, rstd, 1.0 / D)
                ffn(l, U_F2, None)

        @block.vector
        def _(dve):
            TTt, TS, STT = dve.tensor_tensor, dve.tensor_scalar, dve.scalar_tensor_tensor

            def ready(l, u, i=0):
                dve.wait_ge(unit_mm, risen(unit_mm, l, u + 1 + 4 * i))
                return pg[:, u % 4, :]

            def scaled(dst, l, u, by=None):
                bank = ready(l, u)
                return TTt(dst, bank, rstd[:, :] if by is None else by, ALU.mult).then_inc(evac, 1)

            def stat_given(s):
                dve.drain().then_inc(stat_in, 1)

            def root_of(l, s, dst, n=T):
                dve.wait_ge(stat_rt, risen(stat_rt, l, s + 1 if s < 10 else s - 1))
                dve.reciprocal(dst[:, 0:n], dst[:, 0:n])
                dve.drain()

            def norm(l, n, dH, dL, gain, update):
                def low(k):
                    dve.wait_ge(gx_h, risen(gx_h, l, KD * n + k + 1))
                    STT(dL(k), xT[:, k, :], col(gain + k), dH(k).bitcast(F32),
                        ALU.mult, ALU.subtract).then_inc(gx_l, 1)

                def add(k):
                    if k:
                        dve.drain()
                    dve.wait_ge(sq_done, risen(sq_done, l, KD * n + k + 1))
                    if k == 0:
                        dve.tensor_copy(sacc[:, :], sq[:, 0, :]).then_inc(sq_used, 1)
                    else:
                        TTt(sacc[:, :], sacc[:, :], sq[:, k % 2, :], ALU.add).then_inc(sq_used, 1)
                if update:
                    for k in range(KD):
                        update(k)
                        if k >= 1:
                            low(k - 1)
                        if k >= 2:
                            add(k - 2)
                    low(KD - 1)
                    add(KD - 2)
                    add(KD - 1)
                else:
                    for k in range(KD):
                        low(k)
                    for k in range(KD):
                        add(k)
                stat_given(None)

            def gx_high(k):
                return gxH[:, k, :]

            def gx_low(k):
                return gxL[:, k, :]

            def residual(l, u, by):
                def update(k):
                    bank = ready(l, u + k)
                    STT(xT[:, k, :], bank, by, xT[:, k, :], ALU.mult, ALU.add).then_inc(evac, 1)
                return update

            def ffn(l, u, f, last_norm):
                ft = 0
                for ch, n in enumerate(CH):
                    with dve.Fori(0, n // 2) as i:
                        for c in range(2):
                            hid = f * FT + ft + c + 1 + 2 * i
                            bank = ready(l, u + 2 * c, i)
                            TTt(tb[:, 0, :], bank, rstd[:, :], ALU.mult).then_inc(evac, 1)
                            dve.wait_ge(silu, risen(silu, l, hid))
                            TTt(sr, sil, rstd[:, :], ALU.mult)
                            dve.drain()
                            bank = ready(l, u + 2 * c + 1, i)
                            TTt(hb, bank, sr, ALU.mult).then_inc(evac, 1)
                            dve.wait_ge(hid_h, risen(hid_h, l, hid))
                            slot = bass.ds(i * 2 + c, 1)
                            flat = "p a t -> p (a t)"
                            TTt(hL[:, slot, :].rearrange(flat), hb,
                                hH[:, slot, :].rearrange(flat).bitcast(F32),
                                ALU.subtract).then_inc(hid_l, 1)
                    u += 2 * n
                    if ch == len(CH) - 1 and last_norm:
                        norm(l, *last_norm, residual(l, u, 0.5))
                    else:
                        for m in range(KD):
                            residual(l, u, 0.5)(m)
                    u += KD
                    ft += n

            for k in range(KD):
                dve.wait_ge(pro_tr, k + 1)
                dve.tensor_copy(xT[:, k, :], pg[:, k % 4, :]).then_inc(pro_cp, 1)
            dve.wait_ge(pro_tr, KD + 1)
            for l in range(L):
                dve.tensor_copy(pall[:, l, 0:NP_ROWS], pT[:, l * P:l * P + NP_ROWS])
                dve.tensor_copy(pall[:, l, NP_ROWS:NPAR],
                                pT[:, (2 + l) * P:(2 + l) * P + 4 * CONV_W])
            dve.wait_ge(consts, 1)
            dve.tensor_copy(identB[:, :], ident[:, :])
            dve.tensor_copy(nmHL[:, :], sacc[:, :])
            dve.tensor_copy(identR[:, :], sacc[:, 0:3 * HEADS])
            dve.drain()
            for r in (0, 32):
                dve.tensor_copy(identR[r:r + 3 * HEADS, :], ident[r:r + 3 * HEADS, r:r + 3 * HEADS])
            dve.tensor_copy(maskT[:, :], tb[:, 0, 0:P])
            dve.tensor_copy(maskC[:, :], tb[0:32, 1, :])
            for h in range(HEADS):
                TS(kbias[:, h, :], pos[:, :], slope[h], None, ALU.mult)
                TS(cbias[:, h:h + 1], cend[:, :], slope[h], None, ALU.mult)
                for b in range(3):
                    TS(qbias[:, :, h, b], pos[:, :], -slope[h], None, ALU.mult)
            dve.drain().then_inc(evac, risen(evac, 0, 0))
            dve.sem_inc(sq_used, risen(sq_used, 0, 0))

            with dve.Fori(0, L) as l:
                dve.tensor_copy(par[:, :], pall[:, bass.ds(l, 1), :]
                                .rearrange("p a c -> p (a c)")).then_inc(par_in, 1)
                dve.drain()
                TS(g8[:, 0:1], col(P_NQ), float(DH) ** -0.5, None, ALU.mult)
                TS(g8[:, 1:2], col(P_XQ), float(XDH) ** -0.5, None, ALU.mult)
                norm(l, 0, gx_high, gx_low, G_F1, None)
                root_of(l, 0, rstd)
                ffn(l, 0, 0, (1, gx_high, gx_low, G_MIX))

                root_of(l, 1, rstd)
                scaled(kvc[:, 0, :], l, U_KV)
                scaled(kvc[:, 1, :], l, U_KV + 1)
                dve.drain()
                for i in range(2):
                    src = kvc[:, i, :]
                    src = bass.AP(tensor=src.tensor, offset=src.offset,
                                  ap=[src.ap[0], [1, CMP_LEN], [CMP_STRIDE, NCMP]])
                    pe_ = par[:, P_PE + i * CMP_LEN:P_PE + (i + 1) * CMP_LEN]
                    pe_ = bass.AP(tensor=pe_.tensor, offset=pe_.offset,
                                  ap=[pe_.ap[0], [1, CMP_LEN], [0, NCMP]])
                    last = TTt(blk[i], src, pe_, ALU.add)
                last.then_inc(blk_in, 1)

                def squares(src, n=T):
                    dve.drain()
                    TTt(sacc[:, 0:n], src, src, ALU.mult)
                    stat_given(None)

                def normed(l, s, x_, g, n=T):
                    root_of(l, s, rv, n)
                    return STT(x_, x_, g, rv[:, 0:n], ALU.mult, ALU.mult)

                scaled(kT[:, 0, :], l, U_KV + 2)
                squares(kT[:, 0, :])
                dve.wait_ge(ws_tr, risen(ws_tr, l, 1))
                TTt(wsT[:, :, :], pT[:, :].rearrange("p (g t) -> p g t", g=4),
                    bass.AP(tensor=tri[:, :].tensor, offset=tri[:, :].offset,
                            ap=[tri[:, :].ap[0], [0, 4], [1, P]]), ALU.mult).then_inc(t_free, 1)
                scaled(tb[:, 0, :], l, U_KV + 3)
                normed(l, 2, kT[:, 0, :], col(P_NK + 1))
                dve.wait_ge(v_tr, risen(v_tr, l, 1))
                dve.tensor_copy(vt[:, :, 0:2, 0:DH],
                                pT.rearrange("p (a g c) -> p a g c", a=4, g=2)).then_inc(t_free, 1)
                dve.memset(vt[:, :, :, DH:VW], 1.0)
                scaled(kT[:, 1, :], l, U_KV + 4)
                squares(kT[:, 1, :])
                dve.wait_ge(cmp2, risen(cmp2, l, 1))
                dve.tensor_copy(kcn[:, 0:NCMP], pS[:, 1, 0:NCMP])
                for g in range(KVG):
                    dve.tensor_copy(vcs[0:NCMP, g, 0:DH], pS[0:NCMP, 1 - g, P:P + DH])
                scaled(tb[:, 1, :], l, U_KV + 5)
                normed(l, 3, kT[:, 1, :], col(P_NK + 2))
                squares(kcn[:, 0:NCMP], NCMP)

                scaled(qT[:, 0, :], l, U_QP)
                normed(l, 4, kcn[:, 0:NCMP], col(P_NK), NCMP)
                squares(qT[:, 0, :])
                dve.wait_ge(v_tr, risen(v_tr, l, 2))
                dve.tensor_copy(vt[:, :, 2:4, 0:DH],
                                pT.rearrange("p (a g c) -> p a g c", a=4, g=2)).then_inc(t_free, 1)
                for j in range(1, PAIRS):
                    scaled(qT[:, j, :], l, U_QP + j)
                    normed(l, 4 + j, qT[:, j - 1, :], g8[:, 0:1])
                    squares(qT[:, j, :])
                NG = 3 * HEADS
                scaled(hb, l, U_NG)
                normed(l, 8, qT[:, PAIRS - 1, :], g8[:, 0:1])
                scaled(sr, l, U_NG + 1)
                dve.drain()
                TTt(sr, sr, hb, ALU.add).then_inc(ng_in, 1)

                taps = [0] * CT

                def conv(count, tiles=CT):
                    while count and min(taps[:tiles]) < CONV_W:
                        for j in range(tiles):
                            k, o = taps[j], cacc[:, j, :]
                            if k == CONV_W or not count:
                                continue
                            w = col(P_CW + j * CONV_W + k)
                            if k == 0:
                                TS(o, cin[:, j, 0:T], w, col(P_CB + j), ALU.mult, ALU.add)
                            else:
                                STT(o, cin[:, j, k:k + T], w, o, ALU.mult, ALU.add)
                            taps[j] += 1
                            count -= 1
                        dve.drain()

                dve.memset(cin[:, :, 0:CONV_W - 1], 0.0)
                for j in range(4):
                    scaled(tb[:, 0, :], l, U_CONV + 2 * j)
                    if j == 0:
                        dve.wait_ge(ng_tr, risen(ng_tr, l, 1))
                        dve.tensor_copy(gates[:, :, :], pT[:, :].rearrange("p (a c) -> p a c", a=4)
                                        [:, :, 0:NG])
                        dve.drain()
                        cmp0 = gates[:, 0, 0:NG:3]
                        TS(cmp0, cmp0, valid[:, 0:1], None, ALU.mult).then_inc(t_free, 1)
                    scaled(tb[:, 1, :], l, U_CONV + 2 * j + 1)
                    dve.wait_ge(conv_sig, risen(conv_sig, l, j + 1))
                    TTt(cin[:, j, CONV_W - 1:TP], tb[:, 0, :], sil, ALU.mult)
                    dve.drain()
                    if j < CT:
                        conv((6, 8, 8)[j], j + 1)
                    else:
                        dve.drain().then_inc(cin_in, 1)
                        conv(8)

                for j in range(8):
                    if j >= 2:
                        dve.wait_ge(gelu, risen(gelu, l, j - 1))
                    scaled(tb[:, j % 2, :], l, U_SGU + j)
                    if 2 <= j < 6:
                        TTt(sacc[:, :] if j == 2 else hb, vG[:, j - 2, :], vG[:, j - 2, :],
                            ALU.mult)
                        dve.drain()
                        if j > 2:
                            TTt(sacc[:, :], sacc[:, :], hb, ALU.add)
                        if j == 5:
                            stat_given(None)
                    if j < 6:
                        conv((6, 6, 3, 3, 3, 0)[j])
                    if j == 6:
                        root_of(l, 9, rv)
                        for k in range(4):
                            STT(vG[:, k, :], vG[:, k, :], col(P_SG + k), rv[:, :], ALU.mult,
                                ALU.mult)
                        dve.drain().then_inc(vn, 1)
                dve.wait_ge(gelu, risen(gelu, l, 8))
                for c in range(TT):
                    dve.wait_ge(sg_mm, risen(sg_mm, l, c + 1))
                    mixed = (hb, sr)[c % 2]
                    TTt(mixed, pS[:, c % 2, :], bbc[:, :, :].rearrange("p g t -> p (g t)"),
                        ALU.add)
                    dve.drain()
                    uc = uG[:, :, c * P:(c + 1) * P]
                    TTt(uc, uc, mixed.rearrange("p (g t) -> p g t", g=4), ALU.mult)\
                        .then_inc(sg_out, 1)
                dve.drain().then_inc(q_ok, 1)
                def unit_max(q):
                    j, c, e = scored[q]
                    bank = pA[:, 2 * (q % 2):2 * (q % 2) + 2, :]
                    dve.wait_ge(s_mm, risen(s_mm, l, q + 1))
                    if c is None:
                        for e in range(KVG):
                            src = bank[:, e, 0:P].rearrange("p (c n) -> p c n", c=4)
                            last = STT(cs[:, 4 * e:4 * e + 4, :], tabc[:, :, :], slope[j + 4 * e],
                                       src[:, :, 0:NCMP], ALU.mult, ALU.add)
                        last.then_inc(s_out, 1)
                        dve.drain()
                        for e in range(KVG):
                            dve.tensor_reduce(nmx[:, :, 3 * (j + 4 * e)],
                                              cs[:, 4 * e:4 * e + 4, :], AX_X, ALU.max,
                                              negate=True)
                        return
                    n, h = (c + 1) * P, j + 4 * e
                    t = tab[:, T - n:T]
                    t = bass.AP(tensor=t.tensor, offset=t.offset, ap=[t.ap[0], [0, 2], [1, n]])
                    a = att[:, q % 2, :, 0:n]
                    STT(a, t, slope[h], bank[:, :, 0:n], ALU.mult, ALU.add).then_inc(s_out, 1)
                    dve.drain()
                    dve.tensor_reduce(nmx[:, c, 3 * h + 1:3 * h + 3], a, AX_X, ALU.max,
                                      negate=True)

                def branch_unit(u, add):
                    if u % 2 == 0:
                        scaled(tb[:, 0, :], l, u)
                        return
                    m = (u - U_B) % 16 // 2
                    dve.wait_ge(mg_sig, risen(mg_sig, l, (u - U_B) // 2 + 1))
                    if add:
                        scaled(hb, l, u, by=sr)
                        dve.drain()
                        TTt(mrg[:, m, :], mrg[:, m, :], hb, ALU.add)
                    else:
                        scaled(mrg[:, m, :], l, u, by=sr)

                branch_unit(U_B, False)
                for q in range(NSC):
                    unit_max(q)
                    if q == 1:
                        for k in range(KB):
                            dve.wait_ge(br_h, risen(br_h, l, k + 1))
                            TTt(hL[:, BR["B"] + k, :], uG[:, k, :],
                                hH[:, BR["B"] + k, :].bitcast(F32), ALU.subtract).then_inc(br_l, 1)
                    if q % 2 and 1 <= q // 2 - B_LAG < 16:
                        branch_unit(U_B + q // 2 - B_LAG, False)
                    if q % 2 == 0:
                        conv(3)
                conv(CT * CONV_W)
                dve.drain()
                TTt(nmx[:, :, :], nmx[:, :, :],
                    qbias[:, :, :, :].rearrange("p c h b -> p c (h b)"), ALU.add).then_inc(nm_in, 1)

                dve.wait_ge(conv_in, risen(conv_in, l, 1))
                TTt(sacc[:, :], cacc[:, 0, :], cacc[:, 1, :], ALU.add)
                dve.drain()
                for k in (2, 3):
                    TTt(sacc[:, :], sacc[:, :], cacc[:, k, :], ALU.add)
                    dve.drain()
                stat_given(None)
                dve.wait_ge(st_out, risen(st_out, l, STEP["nm"] + 1))
                TTt(nmL[:, :], pA[0:3 * HEADS, STEP["nm"] % 2, :], nmH[:, :].bitcast(F32),
                    ALU.subtract).then_inc(nm_l, 1)
                dve.wait_ge(st_out, risen(st_out, l, STEP["mean"] + 1))
                for k in range(KB):
                    TTt(cacc[:, k, :], cacc[:, k, :], sil, ALU.add)
                dve.drain()
                for k in range(KB):
                    TTt(sacc[:, :] if k == 0 else hb, cacc[:, k, :], cacc[:, k, :], ALU.mult)
                    dve.drain()
                    if k:
                        TTt(sacc[:, :], sacc[:, :], hb, ALU.add)
                        dve.drain()
                stat_given(None)
                dve.wait_ge(st_out, risen(st_out, l, STEP["var"] + 1))
                dve.reciprocal(rv[:, :], rv[:, :])
                dve.drain()
                for k in range(KB):
                    TTt(cacc[:, k, :], cacc[:, k, :], rv[:, :], ALU.mult).then_inc(ln_sc, 1)

                def outputs(n):
                    j, e = n // 2, n % 2
                    h = j + 4 * e
                    dve.wait_ge(pv, risen(pv, l, 3 * n + 3))
                    banks = pA[:, 2:4, 0:6 * VW].rearrange("p a (m c) -> p a m c", m=6)
                    TS(ow[:, :, :], banks[:, :, :, DH], 1e-30, None, ALU.max)
                    dve.drain()
                    dve.reciprocal(ow[:, :, :], ow[:, :, :])
                    dve.drain()
                    w = ow[:, :, :].rearrange("p a m -> p (a m)")
                    w4 = w.rearrange("p (c b) -> p c b", c=TT)
                    TTt(w4, w4, gates[:, :, 3 * h:3 * h + 3], ALU.mult)
                    dve.drain()
                    prod = oprod.rearrange("p (a m c) -> p a m c", a=2, m=6)
                    w = bass.AP(tensor=w.tensor, offset=w.offset,
                                ap=[w.ap[0], [6, 2], [1, 6], [0, DH]])
                    TTt(prod, banks[:, :, :, 0:DH], w, ALU.mult).then_inc(o_out, 1)
                    dve.drain()
                    if e == 0 and j >= 1:
                        dve.wait_ge(st_mm, risen(st_mm, l, STEP["pair", j - 1] + 1))
                    dve.tensor_reduce(o8[:, :, e * DH:(e + 1) * DH],
                                      oprod.rearrange("p (c b d) -> p c d b", c=TT, b=3),
                                      AX_X, ALU.add).then_inc(o_in, 1)

                def pair_low(j):
                    dve.wait_ge(st_out, risen(st_out, l, STEP["pair", j] + 1))
                    TTt(hL[:, BR["C"] + j, :], qT[:, j, :],
                        hH[:, BR["C"] + j, :].bitcast(F32), ALU.subtract).then_inc(br_l, 1)

                for i in range(3, ITEMS + 1):
                    if 0 <= i - A_LAG < 16:
                        branch_unit(U_A + i - A_LAG, True)
                    if i % 3 == 0:
                        outputs(i // 3 - 1)
                    if i == 3:
                        for k in range(KB):
                            dve.wait_ge(br_h, risen(br_h, l, 4 + k + 1))
                            TTt(hL[:, BR["A"] + k, :], cacc[:, k, :],
                                hH[:, BR["A"] + k, :].bitcast(F32), ALU.subtract).then_inc(br_l, 1)
                    if i - 1 in PAIR_AT:
                        pair_low(PAIR_AT[i - 1])
                pair_low(PAIRS - 1)

                def merged_low(m):
                    dve.wait_ge(m_h, risen(m_h, l, m + 1))
                    TTt(merged_tile(hL, gxL, m), mrg[:, m, :],
                        merged_tile(hH, gxH, m).bitcast(F32), ALU.subtract).then_inc(m_l, 1)

                def memory_low(i):
                    bank = pA[:, i, :]
                    dve.wait_ge(mem_h, risen(mem_h, l, i + 1))
                    for k in range(2):
                        kk = 2 * i + k
                        last = STT(memL[:, kk, :], bank[:, k * M:(k + 1) * M], col(G_MEM + kk),
                                   memH[:, kk, :].bitcast(F32), ALU.mult, ALU.subtract)
                    last.then_inc(mem_l, 1)

                for m in range(8):
                    scaled(tb[:, 0, :], l, U_C + 2 * m)
                    dve.wait_ge(mg_sig, risen(mg_sig, l, 16 + m + 1))
                    scaled(hb, l, U_C + 2 * m + 1, by=sr)
                    dve.drain()
                    TTt(mrg[:, m, :], mrg[:, m, :], hb, ALU.add).then_inc(m_in, 1)
                    if m == 4:
                        for k in range(4):
                            merged_low(k)
                    if m == 6:
                        dve.wait_ge(mem_st, risen(mem_st, l, 1))
                        dve.reciprocal(mst[:, :], mst[:, :])
                        dve.drain()
                        for a in range(2):
                            last = TS(memn[:, a, :], memn[:, a, :], mst[:, a:a + 1], None, ALU.mult)
                        last.then_inc(mem_sc, 1)
                for m in range(4, 8):
                    merged_low(m)

                norm(l, 2, lambda k: xnorm_tile(hH, gxH, k), lambda k: xnorm_tile(hL, gxL, k), G_X,
                     residual(l, U_WO, 1.0))
                for i in range(4):
                    memory_low(i)
                root_of(l, 12, rstd)
                for j in range(4):
                    scaled(qT[:, j, :], l, U_XQ + j)
                    if j:
                        normed(l, 12 + j, qT[:, j - 1, :], g8[:, 1:2])
                    squares(qT[:, j, :])

                def x_max(h):
                    for half in range(2):
                        dve.wait_ge(xs_mm, risen(xs_mm, l, 2 * h + half + 1))
                        dve.tensor_reduce(nmx[:, 2 * half:2 * half + 2, h],
                                          pS[:, half, :].rearrange("p (c m) -> p c m", c=2),
                                          AX_X, ALU.max, negate=True).then_inc(xs_out, 1)

                for h in range(8):
                    bank = ready(l, U_XKV + h)
                    dst = kx[:, h, :] if h < 4 else tb[:, (h - 4) // 2,
                                                       ((h - 4) % 2) * M:((h - 4) % 2 + 1) * M]
                    dve.tensor_copy(dst, bank[:, 0:M]).then_inc(evac, 1)
                    if h == 1:
                        normed(l, 16, qT[:, 3, :], g8[:, 1:2])
                        squares(kT[:, 0, :])
                    if h in (3, 5):
                        normed(l, 17 + (h == 5), kT[:, (h == 5) * 1, :], col(P_XK))
                        dve.drain().then_inc(xk_ok, 1)
                    if h == 3:
                        squares(kT[:, 1, :])
                    if h == 4:
                        dve.memset(vx[:, :, :, XDH:XDH + 1], 1.0)
                    if h >= 6:
                        x_max(2 * (h - 6))
                        x_max(2 * (h - 6) + 1)
                        i = h - 6
                        dve.wait_ge(xv_tr, risen(xv_tr, l, i + 1))
                        dve.tensor_copy(vx[:, :, 2 * i:2 * i + 2, 0:XDH],
                                        pT.rearrange("p (a h c) -> p a h c", a=2, h=2))\
                                            .then_inc(xv_cp, 1)

                dve.wait_ge(xst_out, risen(xst_out, l, XSTEP["nm"] + 1))
                TTt(nmL[:, :], pA[0:3 * HEADS, XSTEP["nm"] % 2, :], nmH[:, :].bitcast(F32),
                    ALU.subtract).then_inc(xnm_l, 1)

                def x_low(h):
                    dve.wait_ge(xst_out, risen(xst_out, l, XSTEP["turn", h] + 1))
                    TTt(hL[:, h, :], qT[:, h, :], hH[:, h, :].bitcast(F32), ALU.subtract)\
                        .then_inc(xo_l, 1)

                for h in range(4):
                    dve.wait_ge(xpv, risen(xpv, l, h + 1))
                    banks = pA[:, 2:4, 0:2 * (XDH + 1)].rearrange("p a (m c) -> p a m c", m=2)
                    w = ow[:, :, 0:2]
                    dve.reciprocal(w, banks[:, :, :, XDH])
                    dve.drain()
                    w = bass.AP(tensor=w.tensor, offset=w.offset,
                                ap=[w.ap[0], [6, 2], [1, 2], [0, XDH]])
                    TTt(o8[:, :, :].rearrange("p (a m) c -> p a m c", a=2),
                        banks[:, :, :, 0:XDH], w, ALU.mult).then_inc(xo_out, 1)
                    if h >= 1:
                        x_low(h - 1)
                x_low(3)
                norm(l, 3, gx_high, gx_low, G_F2, residual(l, U_XO, 1.0))
                root_of(l, 19, rstd)
                ffn(l, U_F2, 1, None)
                dve.drain()

            for n in range(2 * TT):
                a, hf = divmod(n, 2)
                dve.wait_ge(fin_tr, n + 1)
                dve.tensor_copy(xnat[:, a, hf * T:(hf + 1) * T], pg[:, n % 4, :])\
                   .then_inc(fin_cp, 1)


_INS = ['x', 'mem', 'norm_ffn1', 'ffn1_wi', 'ffn1_wo', 'norm_mix', 'w_in', 'conv_w', 'conv_b',
        'conv_ln_g', 'conv_ln_b', 'conv_out', 'sgu_norm', 'sgu_ws', 'sgu_b', 'sgu_out',
        'nsa_q_norm', 'nsa_k_norm', 'cmp_pe', 'cmp_w1', 'cmp_w2', 'nsa_out', 'w_out', 'norm_xattn',
        'mem_norm', 'xq', 'xkv', 'xq_norm', 'xk_norm', 'xo', 'norm_ffn2', 'ffn2_wi', 'ffn2_wo']


def kernel(**inputs):
    import numpy as np
    import concourse.bacc as bacc
    from concourse.bass_utils import run_bass_kernel_spmd

    nc = bacc.Bacc("TRN2", target_bir_lowering=False, num_devices=1,
                   dynamic_dma_scratch_size=1024)
    arrays, args = {}, []
    for name in _INS:
        a = np.ascontiguousarray(inputs[name])
        arrays[f"in_{name}"] = a
        args.append(nc.dram_tensor(f"in_{name}", a.shape, mybir.dt.from_np(a.dtype),
                                   kind="ExternalInput").ap())
    shape = arrays["in_x"].shape
    args.append(nc.dram_tensor("out_y", shape, F32, kind="ExternalOutput").ap())
    trunk(nc, *args)
    r = run_bass_kernel_spmd(nc, [arrays], core_ids=[0])
    return r.results[0]["out_y"]
```
